# Optimizing a Trainium2 kernel written in Bass

```python
import jax
import jax.numpy as jnp
from jax import lax
import numpy as np

D_MODEL = 1024
BATCH = 1
SEQ = 512
DEPTH = 2

GRID_W = 64
CTX_LEN = 256
N_MIXERS = 2
N_CONV_LAYERS = (DEPTH + 1) // 2
N_NA_LAYERS = DEPTH // 2
CONV_WIDTH = 31
NA_HEADS = 16
NA_HEAD_DIM = D_MODEL // NA_HEADS
NA_KH = 8
NA_KW = 16
NA_KB_W = 2 * NA_KW
NA_NCB = GRID_W // NA_KW
D_FF = ((8 * D_MODEL // 3 + 127) // 128) * 128
FFN_CONV_WIDTH = 3
N_MOD = 6
RMS_EPS = 1e-6
LN_EPS = 1e-5
NEG_INF = -1e30

kernel_name = 'hybrid_conv_natten_dit_block'

def rms_norm(x, g):
    xf = x.astype(jnp.float32)
    y = xf * lax.rsqrt(jnp.mean(xf * xf, axis=-1, keepdims=True) + RMS_EPS)
    return (y * g.astype(jnp.float32)).astype(x.dtype)

def layer_norm(x, g, b):
    xf = x.astype(jnp.float32)
    xc = xf - jnp.mean(xf, axis=-1, keepdims=True)
    y = xc * lax.rsqrt(jnp.mean(xc * xc, axis=-1, keepdims=True) + LN_EPS)
    return (y * g.astype(jnp.float32) + b.astype(jnp.float32)).astype(x.dtype)

def depthwise_conv(x, w):
    width = w.shape[0]
    pad = width // 2
    return lax.conv_general_dilated(
        x, w[:, None, :].astype(x.dtype), window_strides=(1,),
        padding=[(pad, width - 1 - pad)], dimension_numbers=('NWC', 'WIO', 'NWC'),
        feature_group_count=x.shape[-1])

def ada_mod(cond, w, b):
    m = jax.nn.silu(cond) @ w + b
    return jnp.split(m[..., None, :], N_MOD, axis=-1)

def modulate(h, shift, scale):
    return h * (1 + scale) + shift

def conformer_conv(h, w_pw1, b_pw1, w_dw, b_dw, ln_g, ln_b, w_pw2, b_pw2):
    u = h @ w_pw1 + b_pw1
    a, g = jnp.split(u, 2, axis=-1)
    u = a * jax.nn.sigmoid(g)
    u = depthwise_conv(u, w_dw) + b_dw
    u = jax.nn.silu(layer_norm(u, ln_g, ln_b))
    return u @ w_pw2 + b_pw2

def conv_ffn(h, w_up, w_dw, b_dw, w_down):
    u = h @ w_up
    gate, val = jnp.split(u, 2, axis=-1)
    gate = depthwise_conv(gate, w_dw) + b_dw
    return (jax.nn.gelu(gate) * val) @ w_down

def na_column_tables():
    qcol = np.arange(GRID_W).reshape(NA_NCB, NA_KW)
    kstart = np.clip(np.arange(NA_NCB) * NA_KW - NA_KW // 2, 0, GRID_W - NA_KB_W)
    kcol = kstart[:, None] + np.arange(NA_KB_W)[None, :]
    c0 = np.clip(qcol - NA_KW // 2, 0, GRID_W - NA_KW)
    kc = kcol[:, None, :]
    in_win = (kc >= c0[:, :, None]) & (kc < c0[:, :, None] + NA_KW)
    rel_idx = np.clip(kc - qcol[:, :, None] + NA_KW - 1, 0, 2 * NA_KW - 2)
    return kcol, in_win, rel_idx

def na_mixer(a_lat, a_ctx, w_qkv, w_o, rpb, with_ctx_queries):
    b, n, d = a_lat.shape
    rows = n // GRID_W
    kh = min(NA_KH, rows)
    scale = NA_HEAD_DIM ** -0.5
    qkv = (a_lat @ w_qkv).reshape(b, rows, GRID_W, 3, NA_HEADS, NA_HEAD_DIM)
    q_grid, k_grid, v_grid = qkv[..., 0, :, :], qkv[..., 1, :, :], qkv[..., 2, :, :]
    kv_c = (a_ctx @ w_qkv[:, d:]).reshape(b, a_ctx.shape[1], 2, NA_HEADS, NA_HEAD_DIM)
    k_c, v_c = kv_c[..., 0, :, :], kv_c[..., 1, :, :]
    kcol, in_win, rel_idx = na_column_tables()
    rpb_cols = jnp.where(jnp.asarray(in_win)[None, None],
                         rpb.astype(jnp.float32)[:, :, rel_idx], NEG_INF)
    n_loc = kh * NA_KB_W

    def attend_row(r):
        r0 = jnp.clip(r - kh // 2, 0, rows - kh)
        k_slab = lax.dynamic_slice_in_dim(k_grid, r0, kh, axis=1)[:, :, kcol]
        v_slab = lax.dynamic_slice_in_dim(v_grid, r0, kh, axis=1)[:, :, kcol]
        q_row = lax.dynamic_index_in_dim(q_grid, r, axis=1, keepdims=False).reshape(
            b, NA_NCB, NA_KW, NA_HEADS, NA_HEAD_DIM)
        row_rel = r0 + jnp.arange(kh) - r + (NA_KH - 1)
        bias = jnp.transpose(jnp.take(rpb_cols, row_rel, axis=1), (0, 2, 3, 1, 4))
        s_loc = jnp.einsum('bnqhd,bknjhd->bhnqkj', q_row, k_slab,
                           preferred_element_type=jnp.float32) * scale + bias
        s_ctx = jnp.einsum('bnqhd,bchd->bhnqc', q_row, k_c,
                           preferred_element_type=jnp.float32) * scale
        s = jnp.concatenate([s_loc.reshape(b, NA_HEADS, NA_NCB, NA_KW, n_loc), s_ctx], axis=-1)
        p = jax.nn.softmax(s, axis=-1).astype(v_grid.dtype)
        p_loc = p[..., :n_loc].reshape(b, NA_HEADS, NA_NCB, NA_KW, kh, NA_KB_W)
        o = (jnp.einsum('bhnqkj,bknjhd->bnqhd', p_loc, v_slab)
             + jnp.einsum('bhnqc,bchd->bnqhd', p[..., n_loc:], v_c))
        return o.reshape(b, GRID_W, d)

    o_lat = lax.map(attend_row, jnp.arange(rows))
    y_lat = jnp.moveaxis(o_lat, 0, 1).reshape(b, n, d) @ w_o
    y_ctx = None
    if with_ctx_queries:
        q_c = (a_ctx @ w_qkv[:, :d]).reshape(b, a_ctx.shape[1], NA_HEADS, NA_HEAD_DIM)
        s = jnp.einsum('bqhd,bkhd->bhqk', q_c, k_c, preferred_element_type=jnp.float32) * scale
        p = jax.nn.softmax(s, axis=-1).astype(v_c.dtype)
        y_ctx = jnp.einsum('bhqk,bkhd->bqhd', p, v_c).reshape(b, a_ctx.shape[1], d) @ w_o
    return y_lat, y_ctx

def setup_inputs(seed: int = 0) -> dict:
    key = jax.random.key(seed)
    ks = iter(jax.random.split(key, 32))
    D, F = D_MODEL, D_FF

    def nrm(shape, s):
        return jax.random.normal(next(ks), shape, jnp.float32) * s

    def gain(shape):
        return 1.0 + nrm(shape, 0.05)

    return {
        'x': nrm((BATCH, SEQ, D), 1.0),
        'c': nrm((BATCH, D), 1.0),
        'ctx': nrm((BATCH, CTX_LEN, D), 1.0),
        'c_ctx': nrm((D,), 1.0),
        'mod_w': nrm((DEPTH, D, N_MOD * D), 0.5 * D ** -0.5),
        'mod_b': nrm((DEPTH, N_MOD * D), 0.02),
        'mix_pre_g': gain((DEPTH, D)),
        'mix_post_g': gain((DEPTH, D)),
        'ffn_pre_g': gain((DEPTH, D)),
        'ffn_post_g': gain((DEPTH, D)),
        'cv_w_pw1': nrm((N_CONV_LAYERS, D, 2 * D), D ** -0.5),
        'cv_b_pw1': nrm((N_CONV_LAYERS, 2 * D), 0.02),
        'cv_w_dw': nrm((N_CONV_LAYERS, CONV_WIDTH, D), CONV_WIDTH ** -0.5),
        'cv_b_dw': nrm((N_CONV_LAYERS, D), 0.02),
        'cv_ln_g': gain((N_CONV_LAYERS, D)),
        'cv_ln_b': nrm((N_CONV_LAYERS, D), 0.02),
        'cv_w_pw2': nrm((N_CONV_LAYERS, D, D), D ** -0.5),
        'cv_b_pw2': nrm((N_CONV_LAYERS, D), 0.02),
        'na_w_qkv': nrm((N_NA_LAYERS, D, 3 * D), D ** -0.5),
        'na_w_o': nrm((N_NA_LAYERS, D, D), D ** -0.5),
        'na_rpb': nrm((N_NA_LAYERS, NA_HEADS, 2 * NA_KH - 1, 2 * NA_KW - 1), 0.5),
        'ffn_w_up': nrm((DEPTH, D, 2 * F), D ** -0.5),
        'ffn_w_dw': nrm((DEPTH, FFN_CONV_WIDTH, F), FFN_CONV_WIDTH ** -0.5),
        'ffn_b_dw': nrm((DEPTH, F), 0.02),
        'ffn_w_down': nrm((DEPTH, F, D), F ** -0.5),
    }

def reference(x, c, ctx, c_ctx, mod_w, mod_b, mix_pre_g, mix_post_g, ffn_pre_g, ffn_post_g,
              cv_w_pw1, cv_b_pw1, cv_w_dw, cv_b_dw, cv_ln_g, cv_ln_b, cv_w_pw2, cv_b_pw2,
              na_w_qkv, na_w_o, na_rpb, ffn_w_up, ffn_w_dw, ffn_b_dw, ffn_w_down):
    h_ctx = ctx
    for i in range(DEPTH):
        last = i == DEPTH - 1
        j = i // N_MIXERS
        use_na = (i % N_MIXERS) == 1
        sh1, sc1, g1, sh2, sc2, g2 = ada_mod(c, mod_w[i], mod_b[i])
        csh1, csc1, cg1, csh2, csc2, cg2 = ada_mod(c_ctx, mod_w[i], mod_b[i])
        a_lat = modulate(rms_norm(x, mix_pre_g[i]), sh1, sc1)
        need_ctx = use_na or not last
        a_ctx = modulate(rms_norm(h_ctx, mix_pre_g[i]), csh1, csc1) if need_ctx else None
        if use_na:
            y_lat, y_ctx = na_mixer(a_lat, a_ctx, na_w_qkv[j], na_w_o[j], na_rpb[j], not last)
        else:
            cv = (cv_w_pw1[j], cv_b_pw1[j], cv_w_dw[j], cv_b_dw[j],
                  cv_ln_g[j], cv_ln_b[j], cv_w_pw2[j], cv_b_pw2[j])
            y_lat = conformer_conv(a_lat, *cv)
            y_ctx = None if last else conformer_conv(a_ctx, *cv)
        x = x + g1 * rms_norm(y_lat, mix_post_g[i])
        ffn = (ffn_w_up[i], ffn_w_dw[i], ffn_b_dw[i], ffn_w_down[i])
        f_lat = conv_ffn(modulate(rms_norm(x, ffn_pre_g[i]), sh2, sc2), *ffn)
        x = x + g2 * rms_norm(f_lat, ffn_post_g[i])
        if not last:
            h_ctx = h_ctx + cg1 * rms_norm(y_ctx, mix_post_g[i])
            f_ctx = conv_ffn(modulate(rms_norm(h_ctx, ffn_pre_g[i]), csh2, csc2), *ffn)
            h_ctx = h_ctx + cg2 * rms_norm(f_ctx, ffn_post_g[i])
    return x


_drawn_inputs = setup_inputs


def setup_inputs(seed=0):
    import zlib

    import numpy as np

    out = dict(_drawn_inputs(seed))
    spreads = {}
    factors = {'mix_pre_g': 2.71,
     'mix_post_g': 2.726,
     'ffn_post_g': 2.815,
     'cv_b_pw1': 8.0,
     'cv_b_dw': 3.941,
     'cv_ln_g': 2.868,
     'cv_ln_b': 7.479,
     'cv_b_pw2': 4.441,
     'ffn_b_dw': 7.896}
    for name, (base, spread) in spreads.items():
        noise = np.random.default_rng([zlib.crc32(name.encode()), seed]).standard_normal(out[name].shape)
        drawn = base * np.exp(spread * noise) if base else spread * noise
        out[name] = jnp.asarray(drawn.astype(out[name].dtype))
    for name, factor in factors.items():
        out[name] = (out[name] * factor).astype(out[name].dtype)
    return out
```

```python
from contextlib import ExitStack

import concourse.bass as bass
from concourse import mybir

F32 = mybir.dt.float32
F32R = mybir.dt.float32r
ALU = mybir.AluOpType
ACT = mybir.ActivationFunctionType
ds = bass.ds

P = 128
RING = 4
NEG_INF = -1e30
RMS_EPS = 1e-6
LN_EPS = 1e-5
GRID_W, NA_KH, NA_KW = 64, 8, 16
KB_W = 2 * NA_KW
LAT, CTX = "lat", "ctx"


def col_starts():
    return [min(max(n * NA_KW - NA_KW // 2, 0), GRID_W - KB_W) for n in range(GRID_W // NA_KW)]


class Phase:

    def __init__(self, name, kind, side, iters, kts, src, ring=RING, lo="pool", acc_evacs=0):
        self.name, self.kind, self.side, self.iters, self.kts, self.src = name, kind, side, iters, kts, src
        self.ring, self.lo, self.acc_evacs = ring, lo, acc_evacs
        self.per = len(kts)
        self.split = kind != "ada"

    def slot(self, j):
        return j % self.ring


def lay_out_counts(phases, evacs_before):
    blk = spl = 0
    evac = evacs_before
    landed = [0] * RING
    user = [None] * RING
    reader = [0] * RING
    for ph in phases:
        ph.blk0, ph.spl0, ph.evac0 = blk, spl, evac
        ph.landed0, ph.user0, ph.reader0 = list(landed), list(user), list(reader)
        for i in range(ph.iters * ph.per):
            s = ph.slot(i % ph.per)
            landed[s] += 16
            blk += 1
            if ph.split:
                spl += 1
                reader[s] = blk
                user[s] = ("lo", spl)
            else:
                user[s] = ("pe", blk)
        evac += ph.acc_evacs


def build(nc, x, ctx, mod_w, cv_w_pw1, cv_w_pw2, na_w_qkv, na_w_o, ffn_w_up, ffn_w_down, na_rpb,
          vectors, ident_in, mask_in, out):
    L, D = x.shape
    C = ctx.shape[0]
    N = {LAT: L, CTX: C}
    KD = D // P
    F = ffn_w_down.shape[1]
    KF = F // P
    MOD = 6 * KD
    TAPS = vectors["cv_w_dw"].shape[0] // KD
    PADC = TAPS // 2
    HEAD_D = 64
    NB = GRID_W // NA_KW
    SCALE = HEAD_D ** -0.5
    RPB_ROWS, RPB_COLS = na_rpb.shape[2], na_rpb.shape[3]
    RPB_HEAD = RPB_ROWS * RPB_COLS
    HEADS = na_rpb.shape[1]
    RUN = (NA_KH - 1) * RPB_COLS + NA_KW + KB_W
    STARTS = col_starts()
    WIN = NA_KH * KB_W
    OFFS = [STARTS[n] - NA_KW * n for n in range(NB)]

    at, rows = {}, 0
    for name, ap in vectors.items():
        at[name] = rows
        rows += ap.shape[0]
    VT = (rows + P - 1) // P

    def w_cols(w, r0, kt, c):
        return w[r0:r0 + kt * P, ds(c, P)].rearrange("(k p) n -> p k n", p=P)

    DOWN_K = [8, 7, 7]
    DOWN_R = [0, 8, 15]
    phases = {}

    def phase(name, kind, side, iters, kts, src, **kw):
        phases[name] = Phase(name, kind, side, iters, kts, src, **kw)

    def add_ada(name, layer, m0, iters):
        phase(name, "ada", None, iters, [KD] * 4,
              lambda it, j: w_cols(mod_w[layer], 0, KD, it * (4 * P) + (m0 + j) * P))

    def add_pw1(name, side):
        phase(name, "glu", side, KD // 2, [KD] * 4,
              lambda it, j: w_cols(cv_w_pw1[0], 0, KD, it * (2 * P) + (j % 2) * D + (j // 2) * P),
              acc_evacs=2 * KD)

    def add_square(name, side, w):
        phase(name, "y", side, KD // 4, [KD] * 4,
              lambda it, j: w_cols(w, 0, KD, it * (4 * P) + j * P), acc_evacs=KD)

    def add_up(name, side, layer):
        phase(name, "up", side, KF // 2, [KD] * 4,
              lambda it, j: w_cols(ffn_w_up[layer], 0, KD, it * (2 * P) + (j % 2) * F + (j // 2) * P),
              acc_evacs=KF)

    def add_down(name, side, layer, lo="pool"):
        phase(name, "down", side, KD // 4, DOWN_K * 4,
              lambda it, j: w_cols(ffn_w_down[layer], DOWN_R[j % 3] * P, DOWN_K[j % 3],
                                   it * (4 * P) + (j // 3) * P), acc_evacs=KD, lo=lo)

    add_ada("ada0a", 0, 0, 4)
    add_pw1("pw1c", CTX)
    add_pw1("pw1l", LAT)
    add_ada("ada0b", 0, 2 * KD, 8)
    add_ada("ada1", 1, 0, 12)
    add_square("pw2c", CTX, cv_w_pw2[0])
    add_square("pw2l", LAT, cv_w_pw2[0])
    add_up("up0c", CTX, 0)
    add_down("down0c", CTX, 0, lo="dve")
    add_up("up0l", LAT, 0)
    add_down("down0l", LAT, 0)
    phase("qkv", "qkv", LAT, KD // 2, [KD] * 6,
          lambda it, j: w_cols(na_w_qkv[0], 0, KD, it * (2 * P) + (j % 3) * D + (j // 3) * P), ring=2)
    add_square("o", LAT, na_w_o[0])
    add_up("up1", LAT, 1)
    add_down("down1", LAT, 1)

    INIT_EVACS = VT + 2 * KD
    order = list(phases.values())
    lay_out_counts(order, INIT_EVACS)
    following = {a.name: b for a, b in zip(order, order[1:])}

    stack = ExitStack()
    with stack:
        def sb(name, cols, dt=F32, on=stack):
            return on.enter_context(nc.sbuf_tensor(name, [P, cols], dt))

        def sem(name):
            return stack.enter_context(nc.semaphore(name))

        X = {LAT: sb("x_lat", KD * L), CTX: sb("x_ctx", KD * C)}
        raw = [sb(f"w_raw{i}", KD * P) for i in range(RING)]
        whi = [sb(f"w_hi{i}", KD * P, F32R) for i in range(RING)]
        wlo = [sb(f"w_lo{i}", KD * P, F32R) for i in range(RING)]
        vec = sb("vectors", VT * P)
        mod = sb("modulation", 2 * 2 * MOD)
        drv = sb("derived", 2 * 2 * 4 * KD)
        ident = sb("ident", P)
        ones = sb("ones", P)
        cond = sb("cond", 2 * KD)
        acc = {LAT: sb("feature_sum_lat", L), CTX: sb("feature_sum_ctx", C)}
        rowmax = [sb(f"row_max{i}", 1) for i in range(2)]
        negmax = [sb(f"neg_max{i}", 1) for i in range(2)]
        rowsum = [sb(f"row_sum{i}", 1) for i in range(2)]
        spacer, negmax_credit = sb("spacer", 1), sb("credit", 1)
        rowinv = [sb(f"row_inv{i}", 1) for i in range(2)]

        with ExitStack() as g:
            gate_in = [sb(f"gate_in{i}", L + 2, on=g) for i in range(1)]
            gate = [sb(f"gate{i}", L, on=g) for i in range(1)]
        with ExitStack() as g:
            sq = [sb(f"sq{i}", L, on=g) for i in range(2)]
        keep = sb("scratch_room", 2 * L + 8)

        Hhi, Hlo, Yh, SQ = {}, {}, {}, {}
        for side in (LAT, CTX):
            with ExitStack() as g:
                Hhi[side] = sb(f"h_hi_{side}", KD * N[side], F32R, on=g)
                Hlo[side] = sb(f"h_lo_{side}", KD * N[side], F32R, on=g)
            with ExitStack() as g:
                Yh[side] = sb(f"y_{side}", KD * N[side], on=g)
                SQ[side] = sb(f"squares_{side}", KD * N[side], on=g)
            sb(f"h_room_{side}", 2 * KD * N[side])

        with ExitStack() as g:
            tok = sb("x_by_token", (L + C) // P * D, on=g)
            vec_rows = sb("vector_rows", VT * P, on=g)
            rpb_rows = sb("rpb_rows", RPB_HEAD, on=g)
            rpb_back = sb("rpb_backwards", RPB_HEAD, on=g)
        UW = {s: N[s] + 2 * PADC for s in N}
        with ExitStack() as g:
            U, V, Yb = {}, {}, {}
            U[LAT] = sb("u_lat", KD * UW[LAT], on=g)
            sb("u_pad", KF * C - KD * UW[LAT], on=g)
            Yb[LAT] = sb("yb_lat", KD * L, on=g)
            V[LAT] = sb("v_lat", KD * L, on=g)
            U[CTX] = sb("u_ctx", KD * UW[CTX], on=g)
            V[CTX] = sb("v_ctx", KD * C, on=g)
            glu_a = [sb(f"glu_a{i}", L, on=g) for i in range(2)]
            glu_s = [sb(f"glu_s{i}", L, on=g) for i in range(2)]
            Yb[CTX] = sb("yb_ctx", KD * C, on=g)
        with ExitStack() as g:
            Ghi = sb("g_hi", KF * L, F32R, on=g)
            Glo = sb("g_lo", KF * L, F32R, on=g)
        with ExitStack() as g:
            Ohi = sb("o_hi", KD * L, F32R, on=g)
            Olo = sb("o_lo", KD * L, F32R, on=g)
            qT = [sb(f"q{i}", L, on=g) for i in range(2)]
            kT = [sb(f"k{i}", L + C, on=g) for i in range(2)]
            vT = [sb(f"v{i}", NB * NA_KH * KB_W + C, on=g) for i in range(2)]
            vtok = [sb(f"v_by_token{i}", (2 * NB + 2) * P, on=g) for i in range(2)]
            bias = [sb(f"bias{i}", NB * 512, on=g) for i in range(2)]
            table = [sb(f"bias_table{i}", 2 * RUN, on=g) for i in range(1)]
            mask = sb("mask", NB * KB_W, on=g)
            scores = [sb(f"scores{i}", 512, on=g) for i in range(2)]
            probs = [sb(f"probs{i}", 512, on=g) for i in range(1)]
            probsT = [sb(f"probs_t{i}", 512, on=g) for i in range(1)]
        with ExitStack() as g:
            final = sb("final_by_token", L // P * D, on=g)
        sb("large_room", 2 * KF * L + 160)

        bank = [stack.enter_context(nc.psum_tensor(f"bank{i}", [P, 512], F32)) for i in range(8)]
        STAT, RINV, ADA = bank[4], bank[6], bank[7]
        TMP = [bank[5], bank[7]]

        table_dram = nc.dram_tensor("padded_rpb", (NA_KW + na_rpb.shape[1] * RPB_HEAD + NA_KW,), F32,
                                    kind="Internal").ap()

        w_in = [sem(f"w_in{i}") for i in range(RING)]
        w_hi = sem("w_hi")
        w_lo = sem("w_lo")
        blk = sem("blk")
        evac = sem("evac")
        x_in, c_in, v_in, cst_in = sem("x_in"), sem("c_in"), sem("v_in"), sem("cst_in")
        rpb_in, pad_in, tab_in, mask_in_s = sem("rpb_in"), sem("pad_in"), sem("tab_in"), sem("mask_in")
        rpb_rev, rpb_out = sem("rpb_rev"), sem("rpb_out")
        zeros_s = sem("zeros")
        turned = sem("turned")
        ones_s = sem("ones_s")
        cond_s = sem("cond_s")
        mods = sem("mods")
        mod_raw = sem("mod_raw")
        stat = sem("stat")
        rms = sem("rms")
        rcp = sem("rcp")
        x_sq = sem("x_sq")
        x_up = sem("x_up")
        y_sc = sem("y_sc")
        t_rdy = sem("t_rdy")
        h_hi = sem("h_hi")
        h_val = sem("h_val")
        h_lo = sem("h_lo")
        glu = sem("glu")
        tap = sem("tap")
        conv = sem("conv")
        centred = sem("centred")
        summed = sem("summed")
        pads = sem("pads")
        gate_rdy = sem("gate_rdy")
        gate_t0 = sem("gate_t0")
        gate_cv = sem("gate_cv")
        gelu = sem("gelu")
        prod = sem("prod")
        g_hi = sem("g_hi")
        g_rdy = sem("g_rdy")
        kv_ev = sem("kv_ev")
        vt_tr, vt_ev = sem("vt_tr"), sem("vt_ev")
        bias_rdy = sem("bias_rdy")
        bias_z = sem("bias_z")
        s_rdy, s_max, s_neg = sem("s_rdy"), sem("s_max"), sem("s_neg")
        p_exp, p_inv, p_nrm = sem("p_exp"), sem("p_inv"), sem("p_nrm")
        pt_tr, pt_ev, pv = sem("pt_tr"), sem("pt_ev"), sem("pv")
        o_hi, o_lo = sem("o_hi"), sem("o_lo")
        out_tr, out_ev, stored = sem("out_tr"), sem("out_ev"), sem("stored")

        def vcol(name, i):
            return vec[:, ds(at[name] + i, 1)]

        def window(ap, n, r0, r1):
            return ap.rearrange("p (r c) -> p r c", c=GRID_W)[:, r0:r1, STARTS[n]:STARTS[n] + KB_W]

        def mod_cols(side, layer, part):
            c0 = ((0 if side == LAT else 1) * 2 + layer) * MOD + part * KD
            return c0

        def drv_col0(side, layer, kind):
            return ((layer * 2 + (0 if side == LAT else 1)) * 4 + kind) * KD

        class Chain:
            def __init__(self, side, Y=None, gain=None, pre=None):
                self.side, self.Y, self.gain, self.pre, self.n = side, Y, gain, pre, N[side]

        def pre_of(side, layer, ffn):
            return (drv_col0(side, layer, 2 if ffn else 0), mod_cols(side, layer, 3 if ffn else 0))

        chains = {
            "in_c": Chain(CTX, pre=pre_of(CTX, 0, False)),
            "in_l": Chain(LAT, pre=pre_of(LAT, 0, False)),
            "ln_c": Chain(CTX), "ln_l": Chain(LAT),
            "mix_c": Chain(CTX, Yb[CTX], drv_col0(CTX, 0, 1), pre_of(CTX, 0, True)),
            "mix_l": Chain(LAT, Yb[LAT], drv_col0(LAT, 0, 1), pre_of(LAT, 0, True)),
            "ffn_c": Chain(CTX, Yh[CTX], drv_col0(CTX, 0, 3), pre_of(CTX, 1, False)),
            "ffn_l": Chain(LAT, Yh[LAT], drv_col0(LAT, 0, 3), pre_of(LAT, 1, False)),
            "att_l": Chain(LAT, Yh[LAT], drv_col0(LAT, 1, 1), pre_of(LAT, 1, True)),
            "out_l": Chain(LAT, Yh[LAT], drv_col0(LAT, 1, 3)),
        }
        n_stat = n_rms = n_sq = n_up = n_h = 0
        for name, ch in chains.items():
            ln = name.startswith("ln")
            ch.stat0, ch.rms0, ch.sq0, ch.up0, ch.h0 = n_stat, n_rms, n_sq, n_up, n_h
            n_stat += (ch.Y is not None) + (ch.pre is not None) + 2 * ln
            n_rms += (ch.Y is not None) + (ch.pre is not None) + ln
            n_up += KD * (ch.Y is not None)
            n_sq += KD * (ch.pre is not None or ln)
            n_h += KD * (ch.pre is not None or ln)
        sums = ["conv_c", "conv_l", "pw2c", "pw2l", "down0c", "down0l", "o", "down1"]
        sum0 = {name: i * (KD + 1) for i, name in enumerate(sums)}
        sum_of = {"ln_c": "conv_c", "ln_l": "conv_l", "mix_c": "pw2c", "mix_l": "pw2l", "ffn_c": "down0c",
                  "ffn_l": "down0l", "att_l": "o", "out_l": "down1"}
        y_of = {"pw2c": Yb[CTX], "pw2l": Yb[LAT], "down0c": Yh[CTX], "down0l": Yh[LAT], "o": Yh[LAT],
                "down1": Yh[LAT]}
        ups = ["up0c", "up0l", "up1"]
        up_pairs0 = {name: i * KF for i, name in enumerate(ups)}

        def loop(eng, ph, body, cuts=(), hooks=None, inside=None):
            hooks, inside = hooks or {}, inside or {}
            edges = sorted({0, *cuts, ph.iters - 1, ph.iters})
            for a, b in zip(edges, edges[1:]):
                if a in hooks:
                    hooks[a]()
                if b - a == 1:
                    body(a, b == ph.iters)
                    if a in inside:
                        inside[a](a)
                else:
                    with eng.Fori(a, b) as it:
                        body(it, False)
                        if a in inside:
                            inside[a](it)
            if ph.iters in hooks:
                hooks[ph.iters]()

        FFN_CUTS = (1, 5, 9)

        block = stack.enter_context(nc.Block())

        @block.sync
        def _(sp):
            def load(ph, it, j, first):
                s = ph.slot(j)
                if first and j < ph.ring:
                    if ph.user0[s]:
                        who, n = ph.user0[s]
                        sp.wait_ge(w_lo if who == "lo" else blk, n)
                elif ph.split:
                    sp.wait_ge(w_lo, it * ph.per + (ph.spl0 + j - ph.ring + 1))
                else:
                    sp.wait_ge(blk, it * ph.per + (ph.blk0 + j - ph.ring + 1))
                kt = ph.kts[j]
                sp.dma_start(raw[s][:, 0:kt * P].rearrange("p (k n) -> p k n", n=P),
                             ph.src(it, j)).then_inc(w_in[s], 16)

            def tables(it, j, first):
                if not (first and j == 0):
                    sp.wait_ge(bias_rdy, it * 4 + 2 * j)
                for hp in range(2):
                    src = bass.AP(tensor=table_dram.tensor, offset=it * (4 * RPB_HEAD) + (2 * j + hp) * RPB_HEAD,
                                  ap=[[RPB_COLS, P // NA_KW], [1, NA_KW], [1, RUN]])
                    sp.dma_start(table[0][:, hp * RUN:(hp + 1) * RUN], src).then_inc(tab_in, 16)

            for ph in order:
                if ph.kind == "qkv":
                    sp.wait_ge(rpb_out, 16)
                    sp.wait_ge(pad_in, 32)
                    sp.wait_ge(g_rdy, 1 + 2 * KF)
                    sp.wait_ge(blk, ph.blk0)

                def body(it, first):
                    for j in range(ph.per):
                        load(ph, it, j, first)
                        if ph.kind == "qkv" and j % 3 == 2:
                            tables(it, j // 3, first)

                body(0, True)
                if ph.iters > 2:
                    with sp.Fori(1, ph.iters) as it:
                        body(it, False)
                elif ph.iters == 2:
                    body(1, False)

            for j in range(L // P):
                for h in range(2):
                    sp.wait_ge(out_ev, h * 4 + j + 1)
                    sp.dma_start(out[j * P:(j + 1) * P, h * 512:(h + 1) * 512],
                                 final[:, j * D + h * 512:j * D + (h + 1) * 512]).then_inc(stored, 16)
            sp.wait_ge(stored, 16 * 2 * (L // P))

        @block.gpsimd
        def _(pool):
            pool.memset(ones[:, :], 1.0).then_inc(ones_s, 1)
            pool.memset(acc[CTX][:, 0:NA_KW], 0.0).then_inc(zeros_s, 1)

            def lo_of(ph, it, j):
                s, kt = ph.slot(j), ph.kts[j]
                pool.wait_ge(w_hi, it * ph.per + (ph.spl0 + j + 1))
                pool.tensor_tensor(wlo[s][:, 0:kt * P], raw[s][:, 0:kt * P],
                                   whi[s][:, 0:kt * P].bitcast(F32), ALU.subtract).then_inc(w_lo, 1)

            def lo_ahead(ph, it, j, last):
                nj, nit, nph = j + ph.ring, it, ph
                if nj >= ph.per:
                    nj -= ph.per
                    if last:
                        nph, nit = following.get(ph.name), 0
                        if nph is None or not nph.split or nph.lo != "pool" or nj >= nph.ring:
                            return
                    else:
                        nit = it + 1
                lo_of(nph, nit, nj)

            def lo_first(ph, prev):
                n = min(prev.ring, ph.ring) if prev.split and prev.lo == ph.lo else 0
                for j in range(n, ph.ring):
                    lo_of(ph, 0, j)

            def add_up(side, base, tile, src, waits):
                waits()
                pool.wait_ge(summed, tile + (base + 1))
                pool.tensor_tensor(acc[side][:, :], acc[side][:, :], src, ALU.add).then_inc(summed, 1)

            pool.wait_ge(evac, INIT_EVACS)
            pool.wait_ge(rpb_out, 16)
            for s in (LAT, CTX):
                pool.memset(U[s][:, :], 0.0).then_inc(glu, 1)
            pool.wait_ge(glu, 2)

            for name, prev in (("pw1c", "ada0a"), ("pw1l", "pw1c")):
                ph = phases[name]
                n, w = N[ph.side], UW[ph.side]
                g0 = 2 + (KD if name == "pw1l" else 0)
                lo_first(ph, phases[prev])

                def body(it, last):
                    for j in range(4):
                        if j % 2 == 1:
                            p = j // 2
                            pool.wait_ge(evac, it * 4 + (ph.evac0 + j + 1))
                            pool.tensor_tensor(U[ph.side][:, ds(it * (2 * w) + p * w + PADC, n)],
                                               glu_a[p][:, 0:n], glu_s[p][:, 0:n], ALU.mult).then_inc(glu, 1)
                        lo_ahead(ph, it, j, last)

                loop(pool, ph, body)

            for side, name, c0 in ((CTX, "conv_c", 0), (LAT, "conv_l", KD)):
                base = sum0[name]
                if side == CTX:
                    pool.wait_ge(pad_in, 32)
                pool.memset(acc[side][:, :], 0.0).then_inc(summed, 1)
                with pool.Fori(0, KD) as m:
                    add_up(side, base, m, V[side][:, ds(m * N[side], N[side])],
                           lambda: pool.wait_ge(conv, m + (c0 + 1)))

            def y_phase(name, prev, stat_read):
                ph = phases[name]
                side, n, base = ph.side, N[ph.side], sum0[name]
                pool.wait_ge(stat, stat_read)
                pool.memset(acc[side][:, :], 0.0).then_inc(summed, 1)
                if ph.lo == "pool":
                    lo_first(ph, phases[prev])

                def body(it, last):
                    tiles = 0
                    for j in range(ph.per):
                        if ph.kind == "y" or j % 3 == 2:
                            t = tiles
                            add_up(side, base, it * 4 + t, sq[t % 2][:, 0:n],
                                   lambda: pool.wait_ge(evac, it * 4 + (ph.evac0 + t + 1)))
                            tiles += 1
                        if ph.lo == "pool":
                            lo_ahead(ph, it, j, last)

                loop(pool, ph, body)

            def up_phase(name, prev):
                ph = phases[name]
                lo_first(ph, phases[prev])

                def body(it, last):
                    for j in range(ph.per):
                        lo_ahead(ph, it, j, last)

                loop(pool, ph, body)

            y_phase("pw2c", "ada1", chains["ln_c"].stat0 + 1)
            y_phase("pw2l", "pw2c", chains["ln_l"].stat0 + 1)
            up_phase("up0c", "pw2l")
            y_phase("down0c", "up0c", chains["mix_c"].stat0 + 1)
            up_phase("up0l", "down0c")
            y_phase("down0l", "up0l", chains["mix_l"].stat0 + 1)

            ph = phases["qkv"]

            def head_bias(m, hp):
                if hp == 0:
                    pool.wait_ge(tab_in, m * 32 + 32)
                for n in range(NB):
                    run = table[0][:, hp * RUN:(hp + 1) * RUN]
                    rel = bass.AP(tensor=run.tensor, offset=run.offset + RUN - 1 - NA_KW - OFFS[n],
                                  ap=[list(run.ap[0]), [-RPB_COLS, NA_KH], [-1, KB_W]])
                    mk = mask[:, n * KB_W:(n + 1) * KB_W]
                    mk = bass.AP(tensor=mk.tensor, offset=mk.offset, ap=[list(mk.ap[0]), [0, NA_KH], [1, KB_W]])
                    ins = pool.tensor_tensor(
                        bias[hp][:, n * 512:n * 512 + 256].rearrange("p (k j) -> p k j", j=KB_W),
                        rel, mk, ALU.add)
                ins.then_inc(bias_rdy, 1)

            pool.wait_ge(blk, ph.blk0)
            for hp in range(2):
                pool.memset(bias[hp][:, :], 0.0).then_inc(bias_z, 1)
            pool.wait_ge(bias_z, 2)
            pool.wait_ge(mask_in_s, 16)
            lo_first(ph, phases["down0l"])
            head_bias(0, 0)
            head_bias(0, 1)

            def qkv_body(it, last):
                for j in range(ph.per):
                    lo_ahead(ph, it, j, last)
                    mj = j // 3
                    if j % 3 == 2 and not (isinstance(it, int) and it == 0 and mj == 0):
                        for hp in range(2):
                            pool.wait_ge(s_max, it * 16 + (8 * mj - 8 + 4 * (hp + 1) + 2))
                            head_bias(it * 2 + mj, hp)

            loop(pool, ph, qkv_body, cuts=(1,))

            y_phase("o", "qkv", chains["ffn_l"].stat0 + 1)
            up_phase("up1", "o")
            y_phase("down1", "up1", chains["att_l"].stat0 + 1)

        @block.scalar
        def _(act):
            act.dma_start(ident[:, :], ident_in).then_inc(cst_in, 16)
            loads = 0
            for name, ap in vectors.items():
                r, n = at[name], ap.shape[0]
                done = 0
                while done < n:
                    p = (r + done) % P
                    k = min(n - done, P - p)
                    t = (r + done) // P
                    act.dma_start(vec_rows[p:p + k, t * P:(t + 1) * P], ap[done:done + k, :]).then_inc(v_in, 16)
                    done += k
                    loads += 1
            act.dma_start(tok[:, L // P * D:].rearrange("p (t d) -> p t d", d=D),
                          ctx.rearrange("(t p) d -> p t d", p=P)).then_inc(c_in, 16)
            act.dma_start(tok[:, 0:L // P * D].rearrange("p (t d) -> p t d", d=D),
                          x.rearrange("(t p) d -> p t d", p=P)).then_inc(x_in, 16)

            rpb_size = na_rpb.shape[1] * RPB_HEAD
            act.wait_ge(zeros_s, 1)
            for start in (0, NA_KW + rpb_size):
                act.dma_start(table_dram[start:start + NA_KW].rearrange("(a n) -> a n", a=1),
                              acc[CTX][0:1, 0:NA_KW]).then_inc(pad_in, 16)
            act.dma_start(rpb_rows[0:HEADS, :], na_rpb[0].rearrange("h a b -> h (a b)")).then_inc(rpb_in, 16)
            act.wait_ge(rpb_rev, 1)
            act.dma_start(table_dram[NA_KW:NA_KW + rpb_size].rearrange("(h n) -> h n", n=RPB_HEAD),
                          rpb_back[0:HEADS, :]).then_inc(rpb_out, 16)

            def hi_of(ph, it, j, first):
                s, kt = ph.slot(j), ph.kts[j]
                act.wait_ge(w_in[s], it * (16 * ph.per // ph.ring) + (ph.landed0[s] + 16 * (j // ph.ring + 1)))
                if first and j < ph.ring:
                    if ph.reader0[s]:
                        act.wait_ge(blk, ph.reader0[s])
                else:
                    act.wait_ge(blk, it * ph.per + (ph.blk0 + j - ph.ring + 1))
                act.activation(whi[s][:, 0:kt * P], raw[s][:, 0:kt * P], ACT.Copy).then_inc(w_hi, 1)

            def hi_ahead(ph, it, j, last):
                nj, nit, nph = j + ph.ring, it, ph
                if nj >= ph.per:
                    nj -= ph.per
                    if last:
                        nph, nit = following.get(ph.name), 0
                        if nph is None or not nph.split or nj >= nph.ring:
                            return
                        hi_of(nph, 0, nj, True)
                        return
                    nit = it + 1
                hi_of(nph, nit, nj, False)

            def hi_first(ph, prev):
                n = min(prev.ring, ph.ring) if prev.split else 0
                for j in range(n, ph.ring):
                    hi_of(ph, 0, j, True)

            def root(ch, stage, eps):
                act.wait_ge(stat, ch.stat0 + stage)
                act.activation(RINV[:, 0:ch.n], STAT[:, 0:ch.n], ACT.Sqrt, bias=eps,
                               scale=1.0 / D).then_inc(rms, 1)

            def squares(ch, k):
                act.activation(SQ[ch.side][:, ds(k * ch.n, ch.n)], X[ch.side][:, ds(k * ch.n, ch.n)],
                               ACT.Square).then_inc(x_sq, 1)

            def square_updated(ch, k):
                act.wait_ge(x_up, k + (ch.up0 + 1))
                squares(ch, k)

            def hi_h(ch, t, j):
                act.wait_ge(t_rdy, t * 2 + (ch.h0 + j + 1))
                act.activation(Hhi[ch.side][:, ds(t * (2 * ch.n) + j * ch.n, ch.n)], TMP[j][:, 0:ch.n],
                               ACT.Identity, bias=mod[:, ds(t * 2 + (ch.pre[1] + j), 1)]).then_inc(h_hi, 1)

            evs = 0
            for t in range(VT):
                act.wait_ge(turned, evs + 1)
                act.activation(vec[:, t * P:(t + 1) * P], bank[evs % 4][:, 0:P], ACT.Copy).then_inc(evac, 1)
                evs += 1
            act.wait_ge(evac, VT)
            act.activation(cond[:, :], vec[:, at["c"]:at["c"] + 2 * KD], ACT.Silu).then_inc(cond_s, 1)
            for side in (CTX, LAT):
                for k in range(KD):
                    act.wait_ge(turned, evs + 1)
                    act.activation(X[side][:, k * N[side]:(k + 1) * N[side]], bank[evs % 4][:, 0:N[side]],
                                   ACT.Copy).then_inc(evac, 1)
                    evs += 1
            act.wait_ge(evac, INIT_EVACS)
            for name in ("in_c", "in_l"):
                ch = chains[name]
                with act.Fori(0, KD) as k:
                    squares(ch, k)
            for name in ("in_c", "in_l"):
                ch = chains[name]
                root(ch, 1, RMS_EPS)
                with act.Fori(0, KD // 2) as t:
                    for j in range(2):
                        hi_h(ch, t, j)

            def glu_phase(name, prev):
                ph = phases[name]
                n = N[ph.side]
                g0 = 2 + (KD if name == "pw1l" else 0)
                hi_first(ph, phases[prev])

                def body(it, last):
                    for j in range(4):
                        p = j // 2
                        act.wait_ge(blk, it * 4 + (ph.blk0 + j + 1))
                        if j % 2 == 0:
                            act.wait_ge(glu, it * 2 + (g0 + p - 1))
                            act.activation(glu_a[p][:, 0:n], bank[j][:, 0:n], ACT.Identity,
                                           bias=vcol("cv_b_pw1", it * 2 + p)).then_inc(evac, 1)
                        else:
                            act.activation(glu_s[p][:, 0:n], bank[j][:, 0:n], ACT.Sigmoid,
                                           bias=vcol("cv_b_pw1", it * 2 + (KD + p))).then_inc(evac, 1)
                        hi_ahead(ph, it, j, last)

                loop(act, ph, body)

            glu_phase("pw1c", "ada0a")
            glu_phase("pw1l", "pw1c")

            def ln_silu(ch, t, j):
                act.wait_ge(t_rdy, t * 2 + (ch.h0 + j + 1))
                bcol = vcol("cv_ln_b", t * 2 + j)
                tile = ds(t * (2 * ch.n) + j * ch.n, ch.n)
                act.activation(Hhi[ch.side][:, tile], TMP[j][:, 0:ch.n], ACT.Silu, bias=bcol).then_inc(h_hi, 1)
                act.activation(V[ch.side][:, tile], TMP[j][:, 0:ch.n], ACT.Silu, bias=bcol).then_inc(h_val, 1)

            for i, name in enumerate(("ln_c", "ln_l")):
                ch = chains[name]
                with act.Fori(0, KD) as k:
                    act.wait_ge(centred, k + (i * KD + 1))
                    act.activation(SQ[ch.side][:, ds(k * ch.n, ch.n)], V[ch.side][:, ds(k * ch.n, ch.n)],
                                   ACT.Square).then_inc(x_sq, 1)
                root(ch, 2, LN_EPS)
                with act.Fori(0, KD // 2) as t:
                    for j in range(2):
                        ln_silu(ch, t, j)

            def y_phase(name, prev, hooks=None):
                ph = phases[name]
                n, Y, q0 = N[ph.side], y_of[name], sum0[name]
                hi_first(ph, phases[prev])

                def body(it, last):
                    tiles = 0
                    for j in range(ph.per):
                        if ph.kind == "y" or j % 3 == 2:
                            t = tiles
                            tiles += 1
                            act.wait_ge(blk, it * ph.per + (ph.blk0 + j + 1))
                            act.wait_ge(summed, it * 4 + (q0 + t))
                            kw = {"bias": vcol("cv_b_pw2", it * 4 + t)} if name.startswith("pw2") else {}
                            f = ACT.Identity if kw else ACT.Copy
                            act.activation(Y[:, ds(it * (4 * n) + t * n, n)], bank[t][:, 0:n], f, **kw)
                            act.activation(sq[t % 2][:, 0:n], bank[t][:, 0:n], ACT.Square, **kw).then_inc(evac, 1)
                        hi_ahead(ph, it, j, last)

                loop(act, ph, body, hooks=hooks)

            def up_phase(name, prev, layer, cuts=(), hooks=None, inside=None):
                ph = phases[name]
                n, p0 = N[ph.side], up_pairs0[name]
                hi_first(ph, phases[prev])
                act.wait_ge(pads, 2 * (ups.index(name) + 1))

                def body(it, last):
                    for j in range(4):
                        p = j // 2
                        act.wait_ge(blk, it * 4 + (ph.blk0 + j + 1))
                        if j % 2 == 0:
                            act.wait_ge(gate_cv, it * 2 + (p0 + p + 1))
                            act.activation(gate_in[0][:, 1:n + 1], bank[j][:, 0:n], ACT.Copy).then_inc(gate_t0, 1)
                            act.wait_ge(g_rdy, it * 2 + (p0 + p + 1))
                            act.activation(gate[0][:, 0:n], bank[j][:, 0:n], ACT.Identity,
                                           bias=vcol("ffn_b_dw", it * 2 + (layer * KF + p)),
                                           scale=vcol("ffn_w_dw", it * 2 + ((layer * 3 + 1) * KF + p))
                                           ).then_inc(evac, 1)
                        else:
                            act.wait_ge(gate_cv, it * 2 + (p0 + p + 2))
                            act.activation(gate[0][:, 0:n], gate[0][:, 0:n],
                                           ACT.Gelu_apprx_tanh).then_inc(gelu, 1)
                        hi_ahead(ph, it, j, last)

                loop(act, ph, body, cuts, hooks, inside)

            def two(f, ch, a):
                def step(it):
                    for j in range(2):
                        f(ch, it * 2 + (j - 2 * a))
                return step

            def two_hi(ch, a):
                def step(it):
                    for j in range(2):
                        hi_h(ch, it - a, j)
                return step

            def post_now(ch):
                root(ch, 1, RMS_EPS)
                if ch.pre:
                    with act.Fori(0, KD) as k:
                        square_updated(ch, k)

            def pre_now(ch):
                root(ch, 2, RMS_EPS)
                with act.Fori(0, KD // 2) as t:
                    for j in range(2):
                        hi_h(ch, t, j)

            mc, ml, fc, fl, al = (chains[k] for k in ("mix_c", "mix_l", "ffn_c", "ffn_l", "att_l"))
            y_phase("pw2c", "ada1")
            y_phase("pw2l", "pw2c", hooks={1: lambda: post_now(mc)})
            pre_now(mc)
            up_phase("up0c", "pw2l", 0, FFN_CUTS,
                     {1: lambda: root(ml, 1, RMS_EPS), 5: lambda: root(ml, 2, RMS_EPS)},
                     {1: two(square_updated, ml, 1), 5: two_hi(ml, 5)})
            y_phase("down0c", "up0c")
            up_phase("up0l", "down0c", 0, FFN_CUTS,
                     {1: lambda: root(fc, 1, RMS_EPS), 5: lambda: root(fc, 2, RMS_EPS)},
                     {1: two(square_updated, fc, 1), 5: two_hi(fc, 5)})
            y_phase("down0l", "up0l")
            act.wait_ge(blk, phases["qkv"].blk0)
            act.dma_start(mask[:, :], mask_in).then_inc(mask_in_s, 16)
            post_now(fl)
            pre_now(fl)

            ph = phases["qkv"]
            hi_first(ph, phases["down0l"])

            def qkv_evac(m, q, b):
                act.wait_ge(blk, b(1))
                act.activation(qT[q][:, :].rearrange("p (n r c) -> p r n c", n=NB, c=NA_KW),
                               bank[0][:, 0:L].rearrange("p (r n c) -> p r n c", n=NB, c=NA_KW),
                               ACT.Copy, scale=SCALE).then_inc(kv_ev, 1)
                yield 0
                act.wait_ge(blk, b(2))
                act.activation(kT[q][:, L:L + C], bank[2][:, 0:C], ACT.Copy).then_inc(kv_ev, 1)
                act.activation(kT[q][:, 0:L], bank[1][:, 0:L], ACT.Copy).then_inc(kv_ev, 1)
                yield 1
                act.wait_ge(blk, b(3))
                for n in range(NB):
                    act.activation(vT[q][:, n * WIN:(n + 1) * WIN].rearrange("p (r c) -> p r c", c=KB_W),
                                   window(bank[3][:, 0:L], n, 0, NA_KH), ACT.Copy)
                act.activation(vT[q][:, NB * WIN:NB * WIN + C], bank[2][:, C:2 * C], ACT.Copy).then_inc(kv_ev, 2)
                yield 2

            def take_pair(it, mj, last):
                def b(k):
                    return it * 6 + (ph.blk0 + 3 * mj + k)
                for j in qkv_evac(None, mj, b):
                    hi_ahead(ph, it, 3 * mj + j, last)

            def exp_tile(i, par):
                act.wait_ge(s_neg, i + 1)
                act.wait_ge(pt_tr, i + 1)
                act.activation(probs[0][:, :], scores[par][:, :], ACT.Exp, bias=negmax[par][:, :],
                               accum_out=rowsum[par][:, :]).then_inc(p_exp, 1)

            def pt_copy(i):
                act.wait_ge(pt_tr, i + 2)
                act.wait_ge(pv, i + 1)
                act.activation(probsT[0][:, :], bank[7][:, :], ACT.Copy).then_inc(pt_ev, 1)

            def by_rows(ap):
                return ap.rearrange("p (n r c) -> p r n c", n=NB, c=NA_KW)

            def o_tile(t, m):
                return t[:, ds(m * L, L)].rearrange("p (r n c) -> p r n c", n=NB, c=NA_KW)

            def attend(m, q):
                base = m * 8
                exp_tile(base, 0)
                for t in range(8):
                    pt_copy(base + t) if t == 7 else None
                    if t < 7:
                        pt_copy(base + t)
                        act.wait_ge(s_neg, base + (t + 2))
                        act.wait_ge(pt_tr, base + (t + 2))
                        act.activation(probs[0][:, :], scores[(t + 1) % 2][:, :], ACT.Exp,
                                       bias=negmax[(t + 1) % 2][:, :],
                                       accum_out=rowsum[(t + 1) % 2][:, :]).then_inc(p_exp, 1)
                act.wait_ge(pv, base + 9)
                act.activation(o_tile(Ohi, m), by_rows(bank[4][:, :]), ACT.Copy).then_inc(o_hi, 1)

            act.activation(negmax_credit[:, :], ident[:, 0:1], ACT.Copy).then_inc(pt_ev, 1)
            take_pair(0, 0, False)

            def qkv_body(it, last):
                take_pair(it, 1, last)
                attend(it * 2, 0)
                if not last:
                    take_pair(it + 1, 0, False)
                attend(it * 2 + 1, 1)

            with act.Fori(0, ph.iters - 2) as it:
                qkv_body(it, False)
            act_it = ph.iters - 2
            take_pair(act_it, 1, False)
            attend(2 * act_it, 0)
            take_pair(act_it + 1, 0, True)
            attend(2 * act_it + 1, 1)
            qkv_body(ph.iters - 1, True)

            y_phase("o", "qkv")
            post_now(al)
            pre_now(al)
            up_phase("up1", "o", 1)
            y_phase("down1", "up1")
            root(chains["out_l"], 1, RMS_EPS)
            for i in range(8):
                h, j = i // 4, i % 4
                act.wait_ge(out_tr, i + 1)
                act.activation(final[:, j * D + h * 512:j * D + (h + 1) * 512], bank[i % 4][:, :],
                               ACT.Copy).then_inc(out_ev, 1)

        @block.vector
        def _(dve):
            def lo_of(ph, it, j):
                s, kt = ph.slot(j), ph.kts[j]
                dve.wait_ge(w_hi, it * ph.per + (ph.spl0 + j + 1))
                dve.tensor_tensor(wlo[s][:, 0:kt * P], raw[s][:, 0:kt * P],
                                  whi[s][:, 0:kt * P].bitcast(F32), ALU.subtract).then_inc(w_lo, 1)

            dve.memset(negmax[0][:, :], 0.0).then_inc(gate_cv, 1)
            dve.memset(negmax[1][:, :], 0.0).then_inc(g_rdy, 1)
            dve.memset(rowmax[0][:, :], 0.0).then_inc(prod, 1)
            dve.memset(rowmax[1][:, :], 0.0).then_inc(prod, 1)
            dve.memset(rowinv[0][:, :], 0.0).then_inc(s_max, 1)
            dve.memset(spacer[:, :], 0.0).then_inc(s_max, 1)
            dve.memset(rowsum[0][:, :], 0.0).then_inc(h_lo, 1)
            dve.memset(rowsum[1][:, :], 0.0).then_inc(h_lo, 1)
            dve.memset(rowinv[1][:, :], 0.0).then_inc(o_lo, 1)

            def modulation(layer, part0, parts, blocks):
                dve.wait_ge(blk, blocks)
                n = parts * KD
                for q in range(2):
                    c0 = layer * MOD + part0 * KD
                    dve.tensor_tensor(mod[:, q * 2 * MOD + c0:q * 2 * MOD + c0 + n],
                                      ADA[:, 2 * c0 + q:2 * (c0 + n):2],
                                      vec[:, at["mod_b"] + c0:at["mod_b"] + c0 + n], ALU.add).then_inc(mod_raw, 1)

            raws = 0

            def gains(side, layer, kinds):
                for kind in kinds:
                    part = {0: 1, 1: 2, 2: 4, 3: 5}[kind]
                    g = {0: "mix_pre_g", 1: "mix_post_g", 2: "ffn_pre_g", 3: "ffn_post_g"}[kind]
                    c0 = mod_cols(side, layer, part)
                    d0 = drv_col0(side, layer, kind)
                    v0 = at[g] + layer * KD
                    dve.scalar_tensor_tensor(drv[:, d0:d0 + KD], mod[:, c0:c0 + KD],
                                             1.0 if kind in (0, 2) else 0.0, vec[:, v0:v0 + KD],
                                             ALU.add, ALU.mult).then_inc(mods, 1)

            dve.wait_ge(rpb_in, 16)
            dve.tensor_copy(rpb_back[0:HEADS, :], rpb_rows[0:HEADS, ::-1]).then_inc(rpb_rev, 1)
            dve.wait_ge(evac, VT)
            modulation(0, 0, 2, phases["pw1c"].blk0)
            dve.wait_ge(mod_raw, 2)
            gains(CTX, 0, (0,))
            gains(LAT, 0, (0,))
            dve.wait_ge(mods, 2)

            def recip(ch, stage):
                dve.wait_ge(rms, ch.rms0 + stage)
                dve.reciprocal(RINV[:, 0:ch.n], RINV[:, 0:ch.n]).then_inc(rcp, 1)
                dve.wait_ge(rcp, ch.rms0 + stage)

            def update_pair(ch, t):
                n, s = ch.n, ch.side
                for j in range(2):
                    y = ch.Y[:, ds(t * (2 * n) + j * n, n)]
                    dve.scalar_tensor_tensor(y, y, drv[:, ds(t * 2 + (ch.gain + j), 1)], RINV[:, 0:n],
                                             ALU.mult, ALU.mult).then_inc(y_sc, 1)
                for j in range(2):
                    xk = X[s][:, ds(t * (2 * n) + j * n, n)]
                    dve.wait_ge(y_sc, t * 2 + (ch.up0 + j + 1))
                    dve.tensor_tensor(xk, xk, ch.Y[:, ds(t * (2 * n) + j * n, n)], ALU.add).then_inc(x_up, 1)

            def modulate_pair(ch, t):
                n, s = ch.n, ch.side
                for j in range(2):
                    dve.wait_ge(h_lo, t * 2 + (ch.h0 + j + 1))
                    dve.scalar_tensor_tensor(TMP[j][:, 0:n], X[s][:, ds(t * (2 * n) + j * n, n)],
                                             drv[:, ds(t * 2 + (ch.pre[0] + j), 1)], RINV[:, 0:n],
                                             ALU.mult, ALU.mult).then_inc(t_rdy, 1)
                for j in range(2):
                    tile = ds(t * (2 * n) + j * n, n)
                    dve.wait_ge(h_hi, t * 2 + (ch.h0 + j + 1))
                    dve.scalar_tensor_tensor(Hlo[s][:, tile], TMP[j][:, 0:n],
                                             mod[:, ds(t * 2 + (ch.pre[1] + j), 1)],
                                             Hhi[s][:, tile].bitcast(F32),
                                             ALU.add, ALU.subtract).then_inc(h_lo, 1)

            def post_now(ch):
                recip(ch, 1)
                with dve.Fori(0, KD // 2) as t:
                    update_pair(ch, t)

            def pre_now(ch, stage=2):
                recip(ch, stage)
                with dve.Fori(0, KD // 2) as t:
                    modulate_pair(ch, t)

            pre_now(chains["in_c"], 1)
            pre_now(chains["in_l"], 1)

            for side, g0, t0 in ((CTX, 2, 0), (LAT, 2 + KD, KD * TAPS)):
                n, w = N[side], UW[side]
                with dve.Fori(0, KD) as m:
                    dve.wait_ge(glu, m + (g0 + 1))
                    v = V[side][:, ds(m * n, n)]
                    for s in range(TAPS):
                        u = U[side][:, ds(m * w + s, n)]
                        if s == 0:
                            ins = dve.tensor_scalar(v, u, vcol("cv_w_dw", m), vcol("cv_b_dw", m), ALU.mult, ALU.add)
                        else:
                            dve.wait_ge(tap, m * (TAPS - 1) + (t0 // TAPS * (TAPS - 1) + s))
                            ins = dve.scalar_tensor_tensor(v, u, vcol("cv_w_dw", m + s * KD), v, ALU.mult, ALU.add)
                        ins.then_inc(conv if s == TAPS - 1 else tap, 1)

            modulation(0, 2, 4, phases["pw2c"].blk0)
            modulation(1, 0, 6, phases["pw2c"].blk0)
            dve.wait_ge(mod_raw, 6)
            for side in (CTX, LAT):
                gains(side, 0, (2,))
                gains(side, 1, (0, 2))
            for side, layer, kind in ((CTX, 0, 1), (CTX, 0, 3), (LAT, 0, 1), (LAT, 0, 3), (LAT, 1, 1), (LAT, 1, 3)):
                gains(side, layer, (kind,))
            dve.wait_ge(mods, 14)

            for i, name in enumerate(("ln_c", "ln_l")):
                ch = chains[name]
                n, s = ch.n, ch.side
                dve.wait_ge(stat, ch.stat0 + 1)
                dve.wait_ge(conv, (i + 1) * KD)
                with dve.Fori(0, KD) as k:
                    v = V[s][:, ds(k * n, n)]
                    dve.scalar_tensor_tensor(v, STAT[:, 0:n], -1.0 / D, v, ALU.mult, ALU.add).then_inc(centred, 1)
                recip(ch, 1)
                with dve.Fori(0, KD // 2) as t:
                    for j in range(2):
                        dve.wait_ge(h_lo, t * 2 + (ch.h0 + j + 1))
                        dve.scalar_tensor_tensor(TMP[j][:, 0:n], V[s][:, ds(t * (2 * n) + j * n, n)],
                                                 vcol("cv_ln_g", t * 2 + j), RINV[:, 0:n],
                                                 ALU.mult, ALU.mult).then_inc(t_rdy, 1)
                    for j in range(2):
                        tile = ds(t * (2 * n) + j * n, n)
                        dve.wait_ge(h_val, t * 2 + (i * KD + j + 1))
                        dve.tensor_tensor(Hlo[s][:, tile], V[s][:, tile], Hhi[s][:, tile].bitcast(F32),
                                          ALU.subtract).then_inc(h_lo, 1)

            def up_phase(name, layer, summed_before, cuts=(), hooks=None, inside=None):
                ph = phases[name]
                n, p0 = N[ph.side], up_pairs0[name]
                dve.wait_ge(summed, summed_before)
                dve.memset(gate_in[0][:, 0:1], 0.0).then_inc(pads, 1)
                dve.memset(gate_in[0][:, n + 1:n + 2], 0.0).then_inc(pads, 1)
                dve.wait_ge(pads, 2 * (ups.index(name) + 1))

                def body(it, last):
                    for p in range(2):
                        gt = gate[0][:, 0:n]
                        m = it * 2 + p
                        dve.wait_ge(evac, it * 2 + (ph.evac0 + p + 1))
                        dve.scalar_tensor_tensor(gt, gate_in[0][:, 0:n], vcol("ffn_w_dw", m + layer * 3 * KF),
                                                 gt, ALU.mult, ALU.add).then_inc(tap, 1)
                        dve.wait_ge(tap, it * 2 + (2 * KD * (TAPS - 1) + p0 + p + 1))
                        dve.scalar_tensor_tensor(gt, gate_in[0][:, 2:n + 2],
                                                 vcol("ffn_w_dw", m + (layer * 3 + 2) * KF),
                                                 gt, ALU.mult, ALU.add).then_inc(gate_cv, 1)
                        dve.wait_ge(gelu, it * 2 + (p0 + p + 1))
                        dve.wait_ge(blk, it * 4 + (ph.blk0 + 2 * p + 2))
                        dve.tensor_tensor(gt, gt, bank[2 * p + 1][:, 0:n], ALU.mult).then_inc(prod, 1)
                        dve.wait_ge(prod, it * 2 + (2 + p0 + p + 1))
                        hi = Ghi[:, ds(it * (2 * n) + p * n, n)]
                        dve.tensor_copy(hi, gt).then_inc(g_hi, 1)
                        dve.wait_ge(g_hi, it * 2 + (p0 + p + 1))
                        dve.tensor_tensor(Glo[:, ds(it * (2 * n) + p * n, n)], gt, hi.bitcast(F32),
                                          ALU.subtract).then_inc(g_rdy, 1)

                loop(dve, ph, body, cuts, hooks, inside)

            mc, ml, fc, fl, al = (chains[k] for k in ("mix_c", "mix_l", "ffn_c", "ffn_l", "att_l"))
            post_now(mc)
            pre_now(mc)
            up_phase("up0c", 0, sum0["down0c"], FFN_CUTS,
                     {1: lambda: recip(ml, 1), 5: lambda: recip(ml, 2)},
                     {1: lambda it: update_pair(ml, it - 1), 5: lambda it: modulate_pair(ml, it - 5)})
            ph = phases["down0c"]
            for j in range(ph.ring):
                lo_of(ph, 0, j)
            for j in range(ph.per):
                if j + ph.ring < ph.per:
                    lo_of(ph, 0, j + ph.ring)
            for j in range(ph.per):
                lo_of(ph, 1, j)
            up_phase("up0l", 0, sum0["down0l"], FFN_CUTS,
                     {1: lambda: recip(fc, 1), 5: lambda: recip(fc, 2)},
                     {1: lambda it: update_pair(fc, it - 1), 5: lambda it: modulate_pair(fc, it - 5)})
            post_now(fl)
            pre_now(fl)

            def v_by_token(m, q):
                for b in range(3):
                    w = 512 if b < 2 else 256
                    dve.wait_ge(vt_tr, m * 3 + (b + 1))
                    dve.tensor_copy(vtok[q][:, b * 512:b * 512 + w], bank[7][:, 0:w]).then_inc(vt_ev, 1)

            def take_max(i, t):
                par, hp, n = t % 2, t // 4, t % 4
                if t % 4 == 0:
                    dve.wait_ge(bias_rdy, i[0] * 2 + (hp + 1))
                dve.wait_ge(s_rdy, i[0] * 8 + (t + 1))
                dve.memset(spacer[:, :], 0.0)
                dve.tensor_tensor_reduce(out=scores[par][:, :], in0=bank[5 + par][:, :],
                                         in1=bias[hp][:, n * 512:(n + 1) * 512], scale=1.0, scalar=-3e38,
                                         op0=ALU.add, op1=ALU.max,
                                         accum_out=rowmax[par][:, :]).then_inc(s_max, 1)
                dve.wait_ge(s_max, i[0] * 8 + (t + 3))
                dve.tensor_scalar(negmax[par][:, :], rowmax[par][:, :], -1.0, None, ALU.mult).then_inc(s_neg, 1)

            def normalise(i, t):
                par = t % 2
                dve.wait_ge(p_exp, i[0] * 8 + (t + 1))
                dve.reciprocal(rowinv[par][:, :], rowsum[par][:, :]).then_inc(p_inv, 1)
                dve.wait_ge(p_inv, i[0] * 8 + (t + 1))
                dve.tensor_scalar(probs[0][:, :], probs[0][:, :], rowinv[par][:, :], None,
                                  ALU.mult).then_inc(p_nrm, 1)

            def attend(m, q):
                v_by_token(m, q)
                i = (m,)
                take_max(i, 0)
                for t in range(8):
                    if t < 7:
                        take_max(i, t + 1)
                    normalise(i, t)
                dve.wait_ge(o_hi, m + 1)
                o = [t[:, ds(m * L, L)].rearrange("p (r n c) -> p r n c", n=NB, c=NA_KW) for t in (Olo, Ohi)]
                b4 = bank[4][:, :].rearrange("p (n r c) -> p r n c", n=NB, c=NA_KW)
                dve.tensor_tensor(o[0], b4, o[1].bitcast(F32), ALU.subtract).then_inc(o_lo, 1)

            with dve.Fori(0, KD // 2) as it:
                attend(it * 2, 0)
                attend(it * 2 + 1, 1)

            post_now(al)
            pre_now(al)
            up_phase("up1", 1, sum0["down1"])
            post_now(chains["out_l"])

        @block.tensor
        def _(pe):
            pe.wait_ge(cst_in, 16)
            n_loads = sum(-(-((at[name] % P) + ap.shape[0]) // P) for name, ap in vectors.items())
            pe.wait_ge(v_in, 16 * n_loads)
            evs = 0

            def own_bank():
                if evs >= 4:
                    pe.wait_ge(evac, evs - 3)
                return bank[evs % 4]

            for t in range(VT):
                b = own_bank()
                r = min(P, rows - t * P)
                pe.transpose(b[:, 0:r], vec_rows[0:r, t * P:(t + 1) * P], ident[0:r, 0:r]).then_inc(turned, 1)
                evs += 1
            for side, s, t0 in ((CTX, c_in, L // P), (LAT, x_in, 0)):
                pe.wait_ge(s, 16)
                for k in range(KD):
                    b = own_bank()
                    for t in range(N[side] // P):
                        ins = pe.transpose(b[:, t * P:(t + 1) * P],
                                           tok[:, (t0 + t) * D + k * P:(t0 + t) * D + (k + 1) * P], ident[:, :])
                    ins.then_inc(turned, 1)
                    evs += 1

            def ada_phase(name, layer, m0):
                ph = phases[name]
                c0 = 2 * (layer * MOD + m0)

                def body(it, last):
                    for j in range(4):
                        s = ph.slot(j)
                        pe.wait_ge(w_in[s], it * 16 + (ph.landed0[s] + 16))
                        for k in range(KD):
                            ins = pe.matmul(ADA[:, ds(it * 8 + (c0 + 2 * j), 2)], raw[s][:, k * P:(k + 1) * P],
                                            cond[:, k:2 * KD:KD], start=(k == 0), stop=(k == KD - 1))
                        ins.then_inc(blk, 1)

                loop(pe, ph, body)

            def products(b, n, s, kts, hi, lo, k0, first, last):
                for k in range(kts):
                    w = slice(k * P, (k + 1) * P)
                    a = slice((k0 + k) * n, (k0 + k + 1) * n)
                    pe.matmul(b, whi[s][:, w], hi[:, a], start=(first and k == 0), stop=False)
                    pe.matmul(b, whi[s][:, w], lo[:, a], start=False, stop=False)
                    ins = pe.matmul(b, wlo[s][:, w], hi[:, a], start=False, stop=(last and k == kts - 1))
                return ins

            def split_wait(ph, it, j):
                pe.wait_ge(w_lo, it * ph.per + (ph.spl0 + j + 1))

            def linear(name, free=None, cuts=(), hooks=None, inside=None):
                ph = phases[name]
                n = N[ph.side]
                hi, lo = (Ohi, Olo) if name == "o" else (Hhi[ph.side], Hlo[ph.side])

                def body(it, last):
                    for j in range(4):
                        split_wait(ph, it, j)
                        if ph.kind == "up" and j % 2 == 0:
                            pe.wait_ge(evac, it * 2 + (ph.evac0 + j // 2 - 1))
                        elif ph.kind == "up":
                            pe.wait_ge(prod, it * 2 + (2 + up_pairs0[name] + j // 2 - 1))
                        else:
                            pe.wait_ge(evac, it * 4 + (ph.evac0 + j - 3))
                        products(bank[j][:, 0:n], n, ph.slot(j), KD, hi, lo, 0, True, True).then_inc(blk, 1)

                loop(pe, ph, body, cuts, hooks, inside)

            def down(name, layer_pairs):
                ph = phases[name]
                n = N[ph.side]
                pe.wait_ge(evac, ph.evac0)
                pe.wait_ge(g_rdy, 1 + layer_pairs)

                def body(it, last):
                    for j in range(ph.per):
                        t, part = j // 3, j % 3
                        split_wait(ph, it, j)
                        if part == 0:
                            pe.wait_ge(evac, it * 4 + (ph.evac0 + t - 3))
                        products(bank[t][:, 0:n], n, ph.slot(j), DOWN_K[part], Ghi, Glo, DOWN_R[part],
                                 part == 0, part == 2).then_inc(blk, 1)

                loop(pe, ph, body)

            def stat_sum(ch, name):
                pe.wait_ge(summed, sum0[name] + KD + 1)
                pe.matmul(STAT[:, 0:ch.n], ones[:, :], acc[ch.side][:, :], start=True, stop=True).then_inc(stat, 1)

            def stat_squares(ch):
                pe.wait_ge(x_sq, ch.sq0 + KD)
                for k in range(KD):
                    ins = pe.matmul(STAT[:, 0:ch.n], ones[:, :], SQ[ch.side][:, k * ch.n:(k + 1) * ch.n],
                                    start=(k == 0), stop=(k == KD - 1))
                ins.then_inc(stat, 1)

            pe.wait_ge(cond_s, 1)
            ada_phase("ada0a", 0, 0)
            pe.wait_ge(ones_s, 1)
            stat_squares(chains["in_c"])
            pe.wait_ge(rms, 1)
            stat_squares(chains["in_l"])
            pe.wait_ge(evac, INIT_EVACS)
            pe.wait_ge(h_lo, 2 + KD)
            linear("pw1c")
            pe.wait_ge(h_lo, 2 + 2 * KD)
            linear("pw1l")
            ada_phase("ada0b", 0, 2 * KD)
            ada_phase("ada1", 1, 0)
            for name in ("ln_c", "ln_l"):
                stat_sum(chains[name], sum_of[name])
                pe.wait_ge(centred, KD * (1 if name == "ln_c" else 2))
                stat_squares(chains[name])
                pe.wait_ge(rms, chains[name].rms0 + 1)
            pe.wait_ge(h_lo, 2 + chains["ln_c"].h0 + KD)
            linear("pw2c")
            mc, ml, fc, fl, al = (chains[k] for k in ("mix_c", "mix_l", "ffn_c", "ffn_l", "att_l"))
            pe.wait_ge(h_lo, 2 + chains["ln_l"].h0 + KD)
            linear("pw2l", hooks={1: lambda: stat_sum(mc, "pw2c")})
            stat_squares(mc)
            pe.wait_ge(h_lo, 2 + mc.h0 + KD)
            linear("up0c", cuts=FFN_CUTS, hooks={1: lambda: stat_sum(ml, "pw2l"), 5: lambda: stat_squares(ml)})
            down("down0c", KF)
            pe.wait_ge(h_lo, 2 + ml.h0 + KD)
            linear("up0l", cuts=FFN_CUTS, hooks={1: lambda: stat_sum(fc, "down0c"), 5: lambda: stat_squares(fc)})
            down("down0l", 2 * KF)
            stat_sum(fl, "down0l")
            stat_squares(fl)
            pe.wait_ge(h_lo, 2 + fl.h0 + KD)

            ph = phases["qkv"]
            pe.wait_ge(evac, ph.evac0)

            def qkv_products(it, mj, first=False):
                def ev(k):
                    if not first:
                        pe.wait_ge(kv_ev, it * 10 + (5 * mj - 5 + k))
                b0, n1, n2 = bank, L, C
                s = [ph.slot(3 * mj + j) for j in range(3)]
                split_wait(ph, it, 3 * mj)
                ev(1)
                products(b0[0][:, 0:n1], n1, s[0], KD, Hhi[LAT], Hlo[LAT], 0, True, True).then_inc(blk, 1)
                split_wait(ph, it, 3 * mj + 1)
                ev(5)
                products(b0[1][:, 0:n1], n1, s[1], KD, Hhi[LAT], Hlo[LAT], 0, True, True)
                products(b0[2][:, 0:n2], n2, s[1], KD, Hhi[CTX], Hlo[CTX], 0, True, True).then_inc(blk, 1)
                split_wait(ph, it, 3 * mj + 2)
                products(b0[3][:, 0:n1], n1, s[2], KD, Hhi[LAT], Hlo[LAT], 0, True, True)
                pe.wait_ge(kv_ev, it * 10 + (5 * mj + 2))
                products(b0[2][:, n2:2 * n2], n2, s[2], KD, Hhi[CTX], Hlo[CTX], 0, True, True).then_inc(blk, 1)

            def turn_v(m, q):
                pe.wait_ge(kv_ev, m * 5 + 5)
                for b in range(3):
                    if b == 0:
                        pe.wait_ge(pt_ev, m * 8 + 1)
                    else:
                        pe.wait_ge(vt_ev, m * 3 + b)
                    for i in range(4 if b < 2 else 2):
                        ins = pe.transpose(bank[7][:, i * P:(i + 1) * P],
                                           vT[q][:, (4 * b + i) * P:(4 * b + i + 1) * P], ident[:, :])
                    ins.then_inc(vt_tr, 1)

            def score(m, q, t):
                hp, n = t // 4, t % 4
                rows_ = slice(hp * HEAD_D, (hp + 1) * HEAD_D)
                lhs = qT[q][rows_, n * P:(n + 1) * P]
                b = bank[5 + t % 2]
                pe.wait_ge(s_max, m * 8 + (t + 1))
                pe.matmul(b[:, 0:256], lhs, window(kT[q][rows_, 0:L], n, 0, NA_KH), start=True, stop=True)
                pe.matmul(b[:, 256:512], lhs, kT[q][rows_, L:L + C], start=True, stop=True).then_inc(s_rdy, 1)

            def turn_p(m, t):
                pe.wait_ge(p_nrm, m * 8 + (t + 1))
                pe.wait_ge(pt_ev, m * 8 + (t + 1))
                for i in range(4):
                    ins = pe.transpose(bank[7][:, i * P:(i + 1) * P], probs[0][:, i * P:(i + 1) * P], ident[:, :])
                ins.then_inc(pt_tr, 1)

            def weighted(m, q, t):
                hp, n = t // 4, t % 4
                if t == 0:
                    pe.wait_ge(o_lo, m + 1)
                pe.wait_ge(pt_ev, m * 8 + (t + 2))
                for i in range(4):
                    c = 2 * n + i if i < 2 else 2 * NB + i - 2
                    ins = pe.matmul(bank[4][hp * HEAD_D:(hp + 1) * HEAD_D, n * P:(n + 1) * P],
                                    vtok[q][:, c * P + hp * HEAD_D:c * P + (hp + 1) * HEAD_D],
                                    probsT[0][:, i * P:(i + 1) * P], start=(i == 0), stop=(i == 3))
                ins.then_inc(pv, 1)

            def attend(m, q, ahead):
                turn_v(m, q)
                score(m, q, 0)
                score(m, q, 1)
                ahead()
                pe.wait_ge(vt_ev, m * 3 + 3)
                for t in range(8):
                    turn_p(m, t)
                    if t < 6:
                        score(m, q, t + 2)
                    weighted(m, q, t)

            qkv_products(0, 0, first=True)
            pe.transpose(bank[7][:, 0:P], ident[:, :], ident[:, :]).then_inc(pt_tr, 1)
            pe.matmul(bank[4][0:HEAD_D, 0:2], ident[:, 0:HEAD_D], ident[:, 0:2], start=True, stop=True).then_inc(pv, 1)
            with pe.Fori(0, ph.iters - 1) as it:
                attend(it * 2, 0, lambda: qkv_products(it, 1))
                attend(it * 2 + 1, 1, lambda: qkv_products(it + 1, 0))
            last = ph.iters - 1
            attend(2 * last, 0, lambda: qkv_products(last, 1))
            attend(2 * last + 1, 1, lambda: None)

            pe.wait_ge(o_lo, 1 + KD)
            linear("o")
            stat_sum(al, "o")
            stat_squares(al)
            pe.wait_ge(h_lo, 2 + al.h0 + KD)
            linear("up1")
            down("down1", 3 * KF)
            fin = chains["out_l"]
            stat_sum(fin, "down1")
            for i in range(8):
                h, j = i // 4, i % 4
                pe.wait_ge(x_up, fin.up0 + 4 * (h + 1))
                pe.wait_ge(evac, phases["down1"].evac0 + KD)
                if i >= 4:
                    pe.wait_ge(out_ev, i - 3)
                for k in range(4):
                    kk = 4 * h + k
                    ins = pe.transpose(bank[i % 4][:, k * P:(k + 1) * P],
                                       X[LAT][:, kk * L + j * P:kk * L + (j + 1) * P], ident[:, :])
                ins.then_inc(out_tr, 1)


VECTORS = ["mod_b", "mix_pre_g", "mix_post_g", "ffn_pre_g", "ffn_post_g", "cv_b_pw1", "cv_b_dw", "cv_ln_g",
           "cv_ln_b", "cv_b_pw2", "cv_w_dw", "ffn_b_dw", "ffn_w_dw", "c", "c_ctx"]
MATRICES = ["mod_w", "cv_w_pw1", "cv_w_pw2", "na_w_qkv", "na_w_o", "ffn_w_up", "ffn_w_down", "na_rpb"]


def kernel(**inputs):
    import numpy as np
    import concourse.bacc as bacc
    from concourse.bass_utils import run_bass_kernel_spmd

    nc = bacc.Bacc("TRN2", target_bir_lowering=False, num_devices=1, dynamic_dma_scratch_size=1024)
    arrays = {}

    def give(name, a):
        arrays[f"in_{name}"] = a
        return nc.dram_tensor(f"in_{name}", a.shape, F32, kind="ExternalInput").ap()

    x = give("x", np.ascontiguousarray(inputs["x"])[0])
    ctx = give("ctx", np.ascontiguousarray(inputs["ctx"])[0])
    mats = {n: give(n, np.ascontiguousarray(inputs[n])) for n in MATRICES}
    vecs = {n: give(n, np.ascontiguousarray(inputs[n]).reshape(-1, P)) for n in VECTORS}

    ident = np.eye(P, dtype=np.float32)
    starts = col_starts()
    mask = np.zeros((P, len(starts), KB_W), np.float32)
    for p in range(P):
        for n, k0 in enumerate(starts):
            q = n * NA_KW + p % NA_KW
            c0 = min(max(q - NA_KW // 2, 0), GRID_W - NA_KW)
            for j in range(KB_W):
                if not c0 <= k0 + j < c0 + NA_KW:
                    mask[p, n, j] = NEG_INF
    ident_in = give("ident", ident)
    mask_in = give("mask", mask.reshape(P, -1))
    out = nc.dram_tensor("out", tuple(x.shape), F32, kind="ExternalOutput").ap()
    build(nc, x, ctx, **mats, vectors=vecs, ident_in=ident_in, mask_in=mask_in, out=out)
    r = run_bass_kernel_spmd(nc, [arrays], core_ids=[0])
    return r.results[0]["out"][None]
```

```python
from contextlib import ExitStack

import concourse.bass as bass
from concourse import mybir

F32 = mybir.dt.float32
F32R = mybir.dt.float32r
ALU = mybir.AluOpType
ACT = mybir.ActivationFunctionType
ds = bass.ds

P = 128
POOL_CONV = 2
RING = 4
NEG_INF = -1e30
RMS_EPS = 1e-6
LN_EPS = 1e-5
GRID_W, NA_KH, NA_KW = 64, 8, 16
KB_W = 2 * NA_KW
LAT, CTX = "lat", "ctx"


def col_starts():
    return [min(max(n * NA_KW - NA_KW // 2, 0), GRID_W - KB_W) for n in range(GRID_W // NA_KW)]


class Phase:

    def __init__(self, name, kind, side, iters, kts, src, ring=RING, lo="pool", acc_evacs=0, width=P):
        self.name, self.kind, self.side, self.iters, self.kts, self.src = name, kind, side, iters, kts, src
        self.ring, self.lo, self.acc_evacs = ring, lo, acc_evacs
        self.per, self.width = len(kts), width
        self.split = kind != "ada"

    def slot(self, j):
        return j % self.ring


def lay_out_counts(phases, evacs_before):
    blk = spl = 0
    evac = evacs_before
    landed = [0] * RING
    user = [None] * RING
    reader = [0] * RING
    for ph in phases:
        ph.blk0, ph.spl0, ph.evac0 = blk, spl, evac
        ph.landed0, ph.user0, ph.reader0 = list(landed), list(user), list(reader)
        for i in range(ph.iters * ph.per):
            s = ph.slot(i % ph.per)
            landed[s] += 16
            blk += 1
            if ph.split:
                spl += 1
                reader[s] = blk
                user[s] = ("lo", spl)
            else:
                user[s] = ("pe", blk)
        evac += ph.acc_evacs


def build(nc, x, ctx, mod_w, cv_w_pw1, cv_w_pw2, na_w_qkv, na_w_o, ffn_w_up, ffn_w_down, na_rpb,
          vectors, ident_in, mask_in, out):
    L, D = x.shape
    C = ctx.shape[0]
    N = {LAT: L, CTX: C}
    KD = D // P
    F = ffn_w_down.shape[1]
    KF = F // P
    MOD = 6 * KD
    TAPS = vectors["cv_w_dw"].shape[0] // KD
    PADC = TAPS // 2
    HEAD_D = 64
    NB = GRID_W // NA_KW
    SCALE = HEAD_D ** -0.5
    RPB_ROWS, RPB_COLS = na_rpb.shape[2], na_rpb.shape[3]
    RPB_HEAD = RPB_ROWS * RPB_COLS
    HEADS = na_rpb.shape[1]
    RUN = (NA_KH - 1) * RPB_COLS + NA_KW + KB_W
    STARTS = col_starts()
    WIN = NA_KH * KB_W
    OFFS = [STARTS[n] - NA_KW * n for n in range(NB)]

    at, rows = {}, 0
    for name, ap in vectors.items():
        at[name] = rows
        rows += ap.shape[0]
    VT = (rows + P - 1) // P

    def w_cols(w, r0, kt, c, width=P):
        return w[r0:r0 + kt * P, ds(c, width)].rearrange("(k p) n -> p k n", p=P)

    CHUNK = 4 * P
    DOWN_K = [8, 7, 7]
    DOWN_R = [0, 8, 15]
    phases = {}

    def phase(name, kind, side, iters, kts, src, **kw):
        phases[name] = Phase(name, kind, side, iters, kts, src, **kw)

    def add_ada(name, layer, m0, tiles):
        phase(name, "ada", None, tiles // 8, [KD // 4] * 8,
              lambda it, j: w_cols(mod_w[layer], (j % 4) * (KD // 4) * P, KD // 4,
                                   it * (8 * P) + (m0 + j // 4 * 4) * P, CHUNK), width=CHUNK)

    def add_pw1(name, side):
        phase(name, "glu", side, KD // 2, [KD] * 4,
              lambda it, j: w_cols(cv_w_pw1[0], 0, KD, it * (2 * P) + (j % 2) * D + (j // 2) * P),
              acc_evacs=2 * KD)

    def add_square(name, side, w):
        phase(name, "y", side, KD // 4, [KD] * 4,
              lambda it, j: w_cols(w, 0, KD, it * (4 * P) + j * P), acc_evacs=KD)

    def add_up(name, side, layer):
        phase(name, "up", side, KF // 2, [KD] * 4,
              lambda it, j: w_cols(ffn_w_up[layer], 0, KD, it * (2 * P) + (j % 2) * F + (j // 2) * P),
              acc_evacs=KF)

    def add_down(name, side, layer, lo="pool"):
        phase(name, "down", side, KD // 4, DOWN_K * 4,
              lambda it, j: w_cols(ffn_w_down[layer], DOWN_R[j % 3] * P, DOWN_K[j % 3],
                                   it * (4 * P) + (j // 3) * P), acc_evacs=KD, lo=lo)

    add_ada("ada0a", 0, 0, 2 * KD)
    add_pw1("pw1c", CTX)
    add_pw1("pw1l", LAT)
    add_ada("ada0b", 0, 2 * KD, 4 * KD)
    add_square("pw2c", CTX, cv_w_pw2[0])
    add_ada("ada1", 1, 0, 6 * KD)
    add_up("up0c", CTX, 0)
    add_square("pw2l", LAT, cv_w_pw2[0])
    add_down("down0c", CTX, 0)
    add_up("up0l", LAT, 0)
    add_down("down0l", LAT, 0)
    phase("qkv", "qkv", LAT, KD // 2, [KD] * 6,
          lambda it, j: w_cols(na_w_qkv[0], 0, KD, it * (2 * P) + (j % 3) * D + (j // 3) * P), ring=3)
    add_square("o", LAT, na_w_o[0])
    add_up("up1", LAT, 1)
    add_down("down1", LAT, 1)

    INIT_EVACS = VT + 2 * KD
    order = list(phases.values())
    lay_out_counts(order, INIT_EVACS)
    following = {a.name: b for a, b in zip(order, order[1:])}

    stack = ExitStack()
    with stack:
        def sb(name, cols, dt=F32, on=stack):
            return on.enter_context(nc.sbuf_tensor(name, [P, cols], dt))

        def sem(name):
            return stack.enter_context(nc.semaphore(name))

        X = {LAT: sb("x_lat", KD * L), CTX: sb("x_ctx", KD * C)}
        raw = [sb(f"w_raw{i}", KD * P) for i in range(RING)]
        whi = [sb(f"w_hi{i}", KD * P, F32R) for i in range(RING)]
        wlo = [sb(f"w_lo{i}", KD * P, F32R) for i in range(RING)]
        vec = sb("vectors", VT * P)
        mod = sb("modulation", 2 * 2 * MOD)
        drv = sb("derived", 2 * 2 * 4 * KD)
        ident = sb("ident", P)
        ones = sb("ones", P)
        cond = sb("cond", 2 * KD)
        acc = {LAT: sb("feature_sum_lat", L), CTX: sb("feature_sum_ctx", C)}
        rowmax = [sb(f"row_max{i}", 1) for i in range(2)]
        negmax = [sb(f"neg_max{i}", 1) for i in range(2)]
        rowsum = [sb(f"row_sum{i}", 1) for i in range(2)]
        spacer, negmax_credit = sb("spacer", 1), sb("credit", 1)
        pool_spacer = sb("pool_spacer", 1)
        rowinv = [sb(f"row_inv{i}", 1) for i in range(2)]

        with ExitStack() as g:
            gate_in = [sb(f"gate_in{i}", L + 2, on=g) for i in range(1)]
            gate = [sb(f"gate{i}", L, on=g) for i in range(1)]
        with ExitStack() as g:
            sq = [sb(f"sq{i}", L, on=g) for i in range(2)]
        with ExitStack() as g:
            probs1, probsT1 = sb("probs1", 512, on=g), sb("probs_t1", 512, on=g)
        ada_row = [sb(f"ada_row{i}", P) for i in range(2)]
        keep = sb("scratch_room", 2 * L + 8)

        Hhi, Hlo, Yh, SQ = {}, {}, {}, {}
        for side in (LAT, CTX):
            with ExitStack() as g:
                Hhi[side] = sb(f"h_hi_{side}", KD * N[side], F32R, on=g)
                Hlo[side] = sb(f"h_lo_{side}", KD * N[side], F32R, on=g)
            with ExitStack() as g:
                Yh[side] = sb(f"y_{side}", KD * N[side], on=g)
                SQ[side] = sb(f"squares_{side}", KD * N[side], on=g)
            sb(f"h_room_{side}", 2 * KD * N[side])

        with ExitStack() as g:
            tok = sb("x_by_token", (L + C) // P * D, on=g)
            vec_rows = sb("vector_rows", VT * P, on=g)
            rpb_rows = sb("rpb_rows", RPB_HEAD, on=g)
            rpb_back = sb("rpb_backwards", RPB_HEAD, on=g)
        UW = {s: N[s] + 2 * PADC for s in N}
        with ExitStack() as g:
            U, V, Yb, Ghi, Glo = {}, {}, {}, {}, {}
            with ExitStack() as h:
                U[LAT] = sb("u_lat", KD * UW[LAT], on=h)
            with ExitStack() as h:
                Yb[LAT] = sb("yb_lat", KD * L, on=h)
            sb("u_room", KD * UW[LAT], on=g)
            V[LAT] = sb("v_lat", KD * L, on=g)
            with ExitStack() as h:
                U[CTX] = sb("u_ctx", KD * UW[CTX], on=h)
                V[CTX] = sb("v_ctx", KD * C, on=h)
                glu_a = [sb(f"glu_a{i}", L, on=h) for i in range(2)]
                glu_s = [sb(f"glu_s{i}", L, on=h) for i in range(2)]
                Yb[CTX] = sb("yb_ctx", KD * C, on=h)
            Ghi[CTX] = sb("g_hi_ctx", KF * C, F32R, on=g)
            Glo[CTX] = sb("g_lo_ctx", KF * C, F32R, on=g)
        with ExitStack() as g:
            Ghi[LAT] = sb("g_hi", KF * L, F32R, on=g)
            Glo[LAT] = sb("g_lo", KF * L, F32R, on=g)
        with ExitStack() as g:
            Ohi = sb("o_hi", KD * L, F32R, on=g)
            Olo = sb("o_lo", KD * L, F32R, on=g)
            qT = [sb(f"q{i}", L, on=g) for i in range(2)]
            kT = [sb(f"k{i}", L + C, on=g) for i in range(2)]
            vT = [sb(f"v{i}", NB * NA_KH * KB_W + C, on=g) for i in range(2)]
            vtok = [sb(f"v_by_token{i}", (2 * NB + 2) * P, on=g) for i in range(2)]
            bias = [sb(f"bias{i}", NB * 512, on=g) for i in range(2)]
            table = [sb(f"bias_table{i}", 2 * RUN, on=g) for i in range(1)]
            mask = sb("mask", NB * KB_W, on=g)
            scores = [sb(f"scores{i}", 512, on=g) for i in range(2)]
            probs = [sb("probs0", 512, on=g)]
            probsT = [sb("probs_t0", 512, on=g)]
        probs.append(probs1)
        probsT.append(probsT1)
        with ExitStack() as g:
            final = sb("final_by_token", L // P * D, on=g)
        sb("large_room", 2 * KF * L + 160)

        bank = [stack.enter_context(nc.psum_tensor(f"bank{i}", [P, 512], F32)) for i in range(8)]
        STAT, RINV = bank[4], bank[6]
        SCORES = [[bank[5], bank[6]], [bank[0], bank[1]]]
        TURNED = [bank[7], bank[2]]
        ADA_T = [bank[5], bank[7]]

        table_dram = nc.dram_tensor("padded_rpb", (NA_KW + na_rpb.shape[1] * RPB_HEAD + NA_KW,), F32,
                                    kind="Internal").ap()

        w_in = [sem(f"w_in{i}") for i in range(RING)]
        w_hi = sem("w_hi")
        w_lo = sem("w_lo")
        blk = sem("blk")
        evac = sem("evac")
        x_in, c_in, v_in, cst_in = sem("x_in"), sem("c_in"), sem("v_in"), sem("cst_in")
        rpb_in, pad_in, tab_in, mask_in_s = sem("rpb_in"), sem("pad_in"), sem("tab_in"), sem("mask_in")
        rpb_rev, rpb_out = sem("rpb_rev"), sem("rpb_out")
        zeros_s = sem("zeros")
        turned = sem("turned")
        ones_s = sem("ones_s")
        cond_s = sem("cond_s")
        row_out = sem("row_out")
        row_z = sem("row_z")
        ada_tr = sem("ada_tr")
        ada_ev = sem("ada_ev")
        mods = sem("mods")
        stat = sem("stat")
        rms = sem("rms")
        rcp = sem("rcp")
        x_sq = sem("x_sq")
        x_up = sem("x_up")
        y_sc = sem("y_sc")
        t_rdy = sem("t_rdy")
        h_hi = sem("h_hi")
        h_val = sem("h_val")
        h_lo = sem("h_lo")
        glu = sem("glu")
        tap = sem("tap")
        conv = sem("conv")
        pool_conv = sem("pool_conv")
        pool_tap = sem("pool_tap")
        centred = sem("centred")
        summed = sem("summed")
        pads = sem("pads")
        gate_rdy = sem("gate_rdy")
        gate_t0 = sem("gate_t0")
        gate_cv = sem("gate_cv")
        gelu = sem("gelu")
        prod = sem("prod")
        g_hi = sem("g_hi")
        g_rdy = sem("g_rdy")
        kv_ev = sem("kv_ev")
        vt_tr, vt_ev = sem("vt_tr"), sem("vt_ev")
        bias_rdy = sem("bias_rdy")
        bias_z = sem("bias_z")
        s_rdy, s_max, s_neg = sem("s_rdy"), sem("s_max"), sem("s_neg")
        p_exp, p_inv, p_nrm = sem("p_exp"), sem("p_inv"), sem("p_nrm")
        pt_tr, pt_ev, pv = sem("pt_tr"), sem("pt_ev"), sem("pv")
        o_hi, o_lo = sem("o_hi"), sem("o_lo")
        out_tr, out_ev, stored = sem("out_tr"), sem("out_ev"), sem("stored")

        def vcol(name, i):
            return vec[:, ds(at[name] + i, 1)]

        def window(ap, n, r0, r1):
            return ap.rearrange("p (r c) -> p r c", c=GRID_W)[:, r0:r1, STARTS[n]:STARTS[n] + KB_W]

        def mod_cols(side, layer, part):
            c0 = ((0 if side == LAT else 1) * 2 + layer) * MOD + part * KD
            return c0

        def drv_col0(side, layer, kind):
            return ((layer * 2 + (0 if side == LAT else 1)) * 4 + kind) * KD

        class Chain:
            def __init__(self, side, Y=None, gain=None, pre=None):
                self.side, self.Y, self.gain, self.pre, self.n = side, Y, gain, pre, N[side]

        def pre_of(side, layer, ffn):
            return (drv_col0(side, layer, 2 if ffn else 0), mod_cols(side, layer, 3 if ffn else 0))

        chains = {
            "in_c": Chain(CTX, pre=pre_of(CTX, 0, False)),
            "in_l": Chain(LAT, pre=pre_of(LAT, 0, False)),
            "ln_c": Chain(CTX),
            "mix_c": Chain(CTX, Yb[CTX], drv_col0(CTX, 0, 1), pre_of(CTX, 0, True)),
            "ln_l": Chain(LAT),
            "mix_l": Chain(LAT, Yb[LAT], drv_col0(LAT, 0, 1), pre_of(LAT, 0, True)),
            "ffn_c": Chain(CTX, Yh[CTX], drv_col0(CTX, 0, 3), pre_of(CTX, 1, False)),
            "ffn_l": Chain(LAT, Yh[LAT], drv_col0(LAT, 0, 3), pre_of(LAT, 1, False)),
            "att_l": Chain(LAT, Yh[LAT], drv_col0(LAT, 1, 1), pre_of(LAT, 1, True)),
            "out_l": Chain(LAT, Yh[LAT], drv_col0(LAT, 1, 3)),
        }
        n_stat = n_rms = n_sq = n_up = n_h = 0
        for name, ch in chains.items():
            ln = name.startswith("ln")
            ch.stat0, ch.rms0, ch.sq0, ch.up0, ch.h0 = n_stat, n_rms, n_sq, n_up, n_h
            n_stat += (ch.Y is not None) + (ch.pre is not None) + 2 * ln
            n_rms += (ch.Y is not None) + (ch.pre is not None) + ln
            n_up += KD * (ch.Y is not None)
            n_sq += KD * (ch.pre is not None or ln)
            n_h += KD * (ch.pre is not None or ln)
        sums = ["conv_c", "pw2c", "conv_l", "pw2l", "down0c", "down0l", "o", "down1"]
        sum0 = {name: i * (KD + 1) for i, name in enumerate(sums)}
        sum_of = {"ln_c": "conv_c", "ln_l": "conv_l", "mix_c": "pw2c", "mix_l": "pw2l", "ffn_c": "down0c",
                  "ffn_l": "down0l", "att_l": "o", "out_l": "down1"}
        y_of = {"pw2c": Yb[CTX], "pw2l": Yb[LAT], "down0c": Yh[CTX], "down0l": Yh[LAT], "o": Yh[LAT],
                "down1": Yh[LAT]}
        ups = ["up0c", "up0l", "up1"]
        up_pairs0 = {name: i * KF for i, name in enumerate(ups)}

        def loop(eng, ph, body, cuts=(), hooks=None, inside=None):
            hooks, inside = hooks or {}, inside or {}
            edges = sorted({0, *cuts, ph.iters - 1, ph.iters})
            for a, b in zip(edges, edges[1:]):
                if a in hooks:
                    hooks[a]()
                if b - a == 1:
                    body(a, b == ph.iters)
                    if a in inside:
                        inside[a](a)
                else:
                    with eng.Fori(a, b) as it:
                        body(it, False)
                        if a in inside:
                            inside[a](it)
            if ph.iters in hooks:
                hooks[ph.iters]()

        FFN_CUTS = (1, 5, 9)

        block = stack.enter_context(nc.Block())

        @block.sync
        def _(sp):
            def load(ph, it, j, first):
                s = ph.slot(j)
                if first and j < ph.ring:
                    if ph.user0[s]:
                        who, n = ph.user0[s]
                        sp.wait_ge(w_lo if who == "lo" else blk, n)
                elif ph.split:
                    sp.wait_ge(w_lo, it * ph.per + (ph.spl0 + j - ph.ring + 1))
                else:
                    sp.wait_ge(blk, it * ph.per + (ph.blk0 + j - ph.ring + 1))
                kt = ph.kts[j]
                sp.dma_start(raw[s][:, 0:kt * ph.width].rearrange("p (k n) -> p k n", n=ph.width),
                             ph.src(it, j)).then_inc(w_in[s], 16)

            def tables(it, j, first):
                if not (first and j == 0):
                    sp.wait_ge(bias_rdy, it * 4 + 2 * j)
                else:
                    sp.wait_ge(rpb_out, 16)
                    sp.wait_ge(pad_in, 32)
                    sp.wait_ge(g_rdy, 1 + 2 * KF)
                    sp.wait_ge(blk, phases["qkv"].blk0)
                for hp in range(2):
                    src = bass.AP(tensor=table_dram.tensor, offset=it * (4 * RPB_HEAD) + (2 * j + hp) * RPB_HEAD,
                                  ap=[[RPB_COLS, P // NA_KW], [1, NA_KW], [1, RUN]])
                    sp.dma_start(table[0][:, hp * RUN:(hp + 1) * RUN], src).then_inc(tab_in, 16)

            for ph in order:
                def body(it, first):
                    for j in range(ph.per):
                        load(ph, it, j, first)
                        if ph.kind == "qkv" and j % 3 == 2:
                            tables(it, j // 3, first)

                body(0, True)
                if ph.iters > 2:
                    with sp.Fori(1, ph.iters) as it:
                        body(it, False)
                elif ph.iters == 2:
                    body(1, False)

            for j in range(L // P):
                for h in range(2):
                    sp.wait_ge(out_ev, h * 4 + j + 1)
                    sp.dma_start(out[j * P:(j + 1) * P, h * 512:(h + 1) * 512],
                                 final[:, j * D + h * 512:j * D + (h + 1) * 512]).then_inc(stored, 16)
            sp.wait_ge(stored, 16 * 2 * (L // P))

        @block.gpsimd
        def _(pool):
            pool.memset(ones[:, :], 1.0).then_inc(ones_s, 1)
            for t in ada_row:
                pool.memset(t[:, :], 0.0).then_inc(row_z, 1)
            pool.memset(acc[CTX][:, 0:NA_KW], 0.0).then_inc(zeros_s, 1)

            def lo_of(ph, it, j):
                s, kt = ph.slot(j), ph.kts[j]
                pool.wait_ge(w_hi, it * ph.per + (ph.spl0 + j + 1))
                pool.tensor_tensor(wlo[s][:, 0:kt * P], raw[s][:, 0:kt * P],
                                   whi[s][:, 0:kt * P].bitcast(F32), ALU.subtract).then_inc(w_lo, 1)

            def lo_ahead(ph, it, j, last):
                nj, nit, nph = j + ph.ring, it, ph
                if nj >= ph.per:
                    nj -= ph.per
                    if last:
                        nph, nit = following.get(ph.name), 0
                        if nph is None or not nph.split or nph.lo != "pool" or nj >= nph.ring:
                            return
                    else:
                        nit = it + 1
                lo_of(nph, nit, nj)

            def lo_first(ph, prev):
                n = min(prev.ring, ph.ring) if prev.split and prev.lo == ph.lo else 0
                for j in range(n, ph.ring):
                    lo_of(ph, 0, j)

            def add_up(side, base, tile, src, waits):
                waits()
                pool.wait_ge(summed, tile + (base + 1))
                pool.tensor_tensor(acc[side][:, :], acc[side][:, :], src, ALU.add).then_inc(summed, 1)

            pool.wait_ge(evac, INIT_EVACS)
            pool.wait_ge(rpb_out, 16)
            for s in (LAT, CTX):
                pool.memset(U[s][:, :], 0.0).then_inc(glu, 1)
            pool.wait_ge(glu, 2)

            for name, prev in (("pw1c", "ada0a"), ("pw1l", "pw1c")):
                ph = phases[name]
                n, w = N[ph.side], UW[ph.side]
                g0 = 2 + (KD if name == "pw1l" else 0)
                lo_first(ph, phases[prev])

                def body(it, last):
                    for j in range(4):
                        if j % 2 == 1:
                            p = j // 2
                            pool.wait_ge(evac, it * 4 + (ph.evac0 + j + 1))
                            pool.tensor_tensor(U[ph.side][:, ds(it * (2 * w) + p * w + PADC, n)],
                                               glu_a[p][:, 0:n], glu_s[p][:, 0:n], ALU.mult).then_inc(glu, 1)
                        lo_ahead(ph, it, j, last)

                loop(pool, ph, body)

            taps_done = 0

            def convolve(m):
                nonlocal taps_done
                w = UW[LAT]
                v = V[LAT][:, m * L:(m + 1) * L]
                for s in range(TAPS):
                    u = U[LAT][:, m * w + s:m * w + s + L]
                    if s == 0:
                        pool.tensor_scalar(v, u, vcol("cv_w_dw", m), vcol("cv_b_dw", m), ALU.mult,
                                           ALU.add).then_inc(pool_tap, 1)
                        taps_done += 1
                        continue
                    scaled = glu_a[s % 2][:, 0:L]
                    pool.tensor_scalar(scaled, u, vcol("cv_w_dw", s * KD + m), 1.0, ALU.mult,
                                       ALU.mult).then_inc(pool_tap, 1)
                    pool.wait_ge(pool_tap, taps_done + 1)
                    ins = pool.tensor_tensor(v, v, scaled, ALU.add)
                    ins.then_inc(pool_tap, 1)
                    taps_done += 2
                pool.wait_ge(pool_tap, taps_done)
                pool.memset(pool_spacer[:, :], 0.0).then_inc(pool_conv, 1)

            def conv_sums(side, name, c0):
                base = sum0[name]
                pool.memset(acc[side][:, :], 0.0).then_inc(summed, 1)
                by_dve = KD if side == CTX else KD - POOL_CONV
                with pool.Fori(0, by_dve) as m:
                    add_up(side, base, m, V[side][:, ds(m * N[side], N[side])],
                           lambda: pool.wait_ge(conv, m + (c0 + 1)))
                for m in range(by_dve, KD):
                    add_up(side, base, m, V[side][:, m * N[side]:(m + 1) * N[side]],
                           lambda: pool.wait_ge(pool_conv, m - by_dve + 1))

            def y_phase(name, prev, stat_read):
                ph = phases[name]
                side, n, base = ph.side, N[ph.side], sum0[name]
                pool.wait_ge(stat, stat_read)
                pool.memset(acc[side][:, :], 0.0).then_inc(summed, 1)
                if ph.lo == "pool":
                    lo_first(ph, phases[prev])

                def body(it, last):
                    tiles = 0
                    for j in range(ph.per):
                        if ph.kind == "y" or j % 3 == 2:
                            t = tiles
                            add_up(side, base, it * 4 + t, sq[t % 2][:, 0:n],
                                   lambda: pool.wait_ge(evac, it * 4 + (ph.evac0 + t + 1)))
                            tiles += 1
                        if ph.lo == "pool":
                            lo_ahead(ph, it, j, last)

                loop(pool, ph, body)

            def up_phase(name, prev):
                ph = phases[name]
                lo_first(ph, phases[prev])

                def body(it, last):
                    for j in range(ph.per):
                        lo_ahead(ph, it, j, last)

                loop(pool, ph, body)

            pool.wait_ge(pad_in, 32)
            conv_sums(CTX, "conv_c", 0)
            convolve(KD - 2)
            y_phase("pw2c", "ada0b", chains["ln_c"].stat0 + 1)
            convolve(KD - 1)
            conv_sums(LAT, "conv_l", KD)
            up_phase("up0c", "ada1")
            y_phase("pw2l", "up0c", chains["ln_l"].stat0 + 1)
            y_phase("down0c", "pw2l", chains["mix_c"].stat0 + 1)
            up_phase("up0l", "down0c")
            y_phase("down0l", "up0l", chains["mix_l"].stat0 + 1)

            ph = phases["qkv"]

            def head_bias(m, hp):
                if hp == 0:
                    pool.wait_ge(tab_in, m * 32 + 32)
                for n in range(NB):
                    run = table[0][:, hp * RUN:(hp + 1) * RUN]
                    rel = bass.AP(tensor=run.tensor, offset=run.offset + RUN - 1 - NA_KW - OFFS[n],
                                  ap=[list(run.ap[0]), [-RPB_COLS, NA_KH], [-1, KB_W]])
                    mk = mask[:, n * KB_W:(n + 1) * KB_W]
                    mk = bass.AP(tensor=mk.tensor, offset=mk.offset, ap=[list(mk.ap[0]), [0, NA_KH], [1, KB_W]])
                    ins = pool.tensor_tensor(
                        bias[hp][:, n * 512:n * 512 + 256].rearrange("p (k j) -> p k j", j=KB_W),
                        rel, mk, ALU.add)
                ins.then_inc(bias_rdy, 1)

            pool.wait_ge(blk, ph.blk0)
            for hp in range(2):
                pool.memset(bias[hp][:, :], 0.0).then_inc(bias_z, 1)
            pool.wait_ge(bias_z, 2)
            pool.wait_ge(mask_in_s, 16)
            lo_first(ph, phases["down0l"])
            head_bias(0, 0)
            head_bias(0, 1)

            def qkv_body(it, last):
                for j in range(ph.per):
                    lo_ahead(ph, it, j, last)
                    mj = j // 3
                    if j % 3 == 2 and not (isinstance(it, int) and it == 0 and mj == 0):
                        for hp in range(2):
                            pool.wait_ge(s_max, it * 16 + (8 * mj - 8 + 7 + hp + 2))
                            head_bias(it * 2 + mj, hp)

            loop(pool, ph, qkv_body, cuts=(1,))

            y_phase("o", "qkv", chains["ffn_l"].stat0 + 1)
            up_phase("up1", "o")
            y_phase("down1", "up1", chains["att_l"].stat0 + 1)

        @block.scalar
        def _(act):
            act.dma_start(ident[:, :], ident_in).then_inc(cst_in, 16)
            loads = 0
            for name, ap in vectors.items():
                r, n = at[name], ap.shape[0]
                done = 0
                while done < n:
                    p = (r + done) % P
                    k = min(n - done, P - p)
                    t = (r + done) // P
                    act.dma_start(vec_rows[p:p + k, t * P:(t + 1) * P], ap[done:done + k, :]).then_inc(v_in, 16)
                    done += k
                    loads += 1
            act.dma_start(tok[:, L // P * D:].rearrange("p (t d) -> p t d", d=D),
                          ctx.rearrange("(t p) d -> p t d", p=P)).then_inc(c_in, 16)
            act.dma_start(tok[:, 0:L // P * D].rearrange("p (t d) -> p t d", d=D),
                          x.rearrange("(t p) d -> p t d", p=P)).then_inc(x_in, 16)

            rpb_size = na_rpb.shape[1] * RPB_HEAD
            act.wait_ge(zeros_s, 1)
            for start in (0, NA_KW + rpb_size):
                act.dma_start(table_dram[start:start + NA_KW].rearrange("(a n) -> a n", a=1),
                              acc[CTX][0:1, 0:NA_KW]).then_inc(pad_in, 16)
            act.dma_start(rpb_rows[0:HEADS, :], na_rpb[0].rearrange("h a b -> h (a b)")).then_inc(rpb_in, 16)

            def hi_of(ph, it, j, first):
                s, kt = ph.slot(j), ph.kts[j]
                act.wait_ge(w_in[s], it * (16 * ph.per // ph.ring) + (ph.landed0[s] + 16 * (j // ph.ring + 1)))
                if first and j < ph.ring:
                    if ph.reader0[s]:
                        act.wait_ge(blk, ph.reader0[s])
                else:
                    act.wait_ge(blk, it * ph.per + (ph.blk0 + j - ph.ring + 1))
                act.activation(whi[s][:, 0:kt * P], raw[s][:, 0:kt * P], ACT.Copy).then_inc(w_hi, 1)

            def hi_ahead(ph, it, j, last):
                nj, nit, nph = j + ph.ring, it, ph
                if nj >= ph.per:
                    nj -= ph.per
                    if last:
                        nph, nit = following.get(ph.name), 0
                        if nph is None or not nph.split or nj >= nph.ring:
                            return
                        hi_of(nph, 0, nj, True)
                        return
                    nit = it + 1
                hi_of(nph, nit, nj, False)

            def hi_first(ph, prev):
                n = min(prev.ring, ph.ring) if prev.split else 0
                for j in range(n, ph.ring):
                    hi_of(ph, 0, j, True)

            def root(ch, stage, eps):
                act.wait_ge(stat, ch.stat0 + stage)
                act.activation(RINV[:, 0:ch.n], STAT[:, 0:ch.n], ACT.Sqrt, bias=eps,
                               scale=1.0 / D).then_inc(rms, 1)

            def square_of(ch, t, j):
                tile = ds(t * (2 * ch.n) + j * ch.n, ch.n)
                act.activation(SQ[ch.side][:, tile], X[ch.side][:, tile], ACT.Square).then_inc(x_sq, 1)

            def square_updated(ch, t, j):
                act.wait_ge(x_up, t * 2 + (ch.up0 + j + 1))
                square_of(ch, t, j)

            def hi_h(ch, t, j):
                act.wait_ge(t_rdy, t * 2 + (ch.h0 + j + 1))
                tile = ds(t * (2 * ch.n) + j * ch.n, ch.n)
                act.activation(Hhi[ch.side][:, tile], SQ[ch.side][:, tile],
                               ACT.Identity, bias=mod[:, ds(t * 2 + (ch.pre[1] + j), 1)]).then_inc(h_hi, 1)

            evs = 0
            for t in range(VT):
                act.wait_ge(turned, evs + 1)
                act.activation(vec[:, t * P:(t + 1) * P], bank[evs % 4][:, 0:P], ACT.Copy).then_inc(evac, 1)
                evs += 1
            act.wait_ge(evac, VT)
            act.activation(cond[:, :], vec[:, at["c"]:at["c"] + 2 * KD], ACT.Silu).then_inc(cond_s, 1)
            for side in (CTX, LAT):
                for k in range(KD):
                    act.wait_ge(turned, evs + 1)
                    act.activation(X[side][:, k * N[side]:(k + 1) * N[side]], bank[evs % 4][:, 0:N[side]],
                                   ACT.Copy).then_inc(evac, 1)
                    evs += 1

            act.wait_ge(rpb_rev, 1)
            act.dma_start(table_dram[NA_KW:NA_KW + rpb_size].rearrange("(h n) -> h n", n=RPB_HEAD),
                          rpb_back[0:HEADS, :]).then_inc(rpb_out, 16)

            def input_squares():
                act.wait_ge(evac, INIT_EVACS)
                for name in ("in_c", "in_l"):
                    in_fori(square_of, chains[name])

            def glu_phase(name, prev):
                ph = phases[name]
                n = N[ph.side]
                g0 = 2 + (KD if name == "pw1l" else 0)
                if prev:
                    hi_first(ph, phases[prev])

                def body(it, last):
                    for j in range(4):
                        p = j // 2
                        act.wait_ge(blk, it * 4 + (ph.blk0 + j + 1))
                        if j % 2 == 0:
                            act.wait_ge(glu, it * 2 + (g0 + p - 1))
                            act.activation(glu_a[p][:, 0:n], bank[j][:, 0:n], ACT.Identity,
                                           bias=vcol("cv_b_pw1", it * 2 + p)).then_inc(evac, 1)
                        else:
                            act.activation(glu_s[p][:, 0:n], bank[j][:, 0:n], ACT.Sigmoid,
                                           bias=vcol("cv_b_pw1", it * 2 + (KD + p))).then_inc(evac, 1)
                        hi_ahead(ph, it, j, last)

                loop(act, ph, body)

            def ada_phase(name, layer, m0, cuts=(), hooks=None):
                ph = phases[name]
                c0 = (layer * MOD + m0) // 4
                act.wait_ge(row_z, 2)

                def body(it, last):
                    for u in range(2):
                        act.wait_ge(blk, it * 8 + (ph.blk0 + 4 * u + 4))
                        for g in range(4):
                            r = slice(32 * g, 32 * g + 2)
                            ins = act.activation(ada_row[u][r, :], bank[u][r, 0:P], ACT.Copy)
                        ins.then_inc(row_out, 1)
                        act.wait_ge(ada_tr, it * 2 + (c0 + u + 1))
                        for i in range(4):
                            m = layer * MOD + m0 + 4 * u + i
                            cols = mod[:, ds(it * 8 + m, 2, step=2 * MOD)]
                            ins = act.activation(cols, ADA_T[u][:, 32 * i:32 * i + 2], ACT.Identity,
                                                 bias=vcol("mod_b", it * 8 + m))
                        ins.then_inc(ada_ev, 1)

                loop(act, ph, body, cuts, hooks)

            def ln_square(ch, t, j):
                i = 0 if ch.side == CTX else 1
                act.wait_ge(centred, t * 2 + (i * KD + j + 1))
                tile = ds(t * (2 * ch.n) + j * ch.n, ch.n)
                act.activation(SQ[ch.side][:, tile], V[ch.side][:, tile], ACT.Square).then_inc(x_sq, 1)

            def ln_silu(ch, t, j):
                act.wait_ge(t_rdy, t * 2 + (ch.h0 + j + 1))
                bcol = vcol("cv_ln_b", t * 2 + j)
                tile = ds(t * (2 * ch.n) + j * ch.n, ch.n)
                act.activation(V[ch.side][:, tile], V[ch.side][:, tile], ACT.Silu, bias=bcol).then_inc(h_val, 1)

            def pairs_of(f, ch, a=0):
                def step(it):
                    for j in range(2):
                        f(ch, it - a, j)
                return step

            def in_fori(f, ch):
                with act.Fori(0, KD // 2) as t:
                    pairs_of(f, ch)(t)

            def y_phase(name, prev, steps=None):
                ph = phases[name]
                n, Y, q0 = N[ph.side], y_of[name], sum0[name]
                hi_first(ph, phases[prev])
                if ph.kind == "y" and prev.startswith("up"):
                    act.wait_ge(g_rdy, 1 + up_pairs0[prev] + KF)

                def body(it, last):
                    tiles = 0
                    for j in range(ph.per):
                        if ph.kind == "y" or j % 3 == 2:
                            t = tiles
                            tiles += 1
                            act.wait_ge(blk, it * ph.per + (ph.blk0 + j + 1))
                            act.wait_ge(summed, it * 4 + (q0 + t))
                            kw = {"bias": vcol("cv_b_pw2", it * 4 + t)} if name.startswith("pw2") else {}
                            f = ACT.Identity if kw else ACT.Copy
                            act.activation(Y[:, ds(it * (4 * n) + t * n, n)], bank[t][:, 0:n], f, **kw)
                            act.activation(sq[t % 2][:, 0:n], bank[t][:, 0:n], ACT.Square, **kw).then_inc(evac, 1)
                        hi_ahead(ph, it, j, last)
                        for step in (steps or {}).get((it, j), ()):
                            step()

                loop(act, ph, body)

            def up_phase(name, prev, layer, cuts=(), hooks=None, inside=None):
                ph = phases[name]
                n, p0 = N[ph.side], up_pairs0[name]
                hi_first(ph, phases[prev])
                act.wait_ge(pads, 2 * (ups.index(name) + 1))

                def body(it, last):
                    for j in range(4):
                        p = j // 2
                        act.wait_ge(blk, it * 4 + (ph.blk0 + j + 1))
                        if j % 2 == 0:
                            act.wait_ge(gate_cv, it * 2 + (p0 + p + 1))
                            act.activation(gate_in[0][:, 1:n + 1], bank[j][:, 0:n], ACT.Copy).then_inc(gate_t0, 1)
                            act.wait_ge(g_rdy, it * 2 + (p0 + p + 1))
                            act.activation(gate[0][:, 0:n], bank[j][:, 0:n], ACT.Identity,
                                           bias=vcol("ffn_b_dw", it * 2 + (layer * KF + p)),
                                           scale=vcol("ffn_w_dw", it * 2 + ((layer * 3 + 1) * KF + p))
                                           ).then_inc(evac, 1)
                        else:
                            act.wait_ge(gate_cv, it * 2 + (p0 + p + 2))
                            act.activation(gate[0][:, 0:n], gate[0][:, 0:n],
                                           ACT.Gelu_apprx_tanh).then_inc(gelu, 1)
                        hi_ahead(ph, it, j, last)

                loop(act, ph, body, cuts, hooks, inside)

            def post_now(ch):
                root(ch, 1, RMS_EPS)
                if ch.pre:
                    in_fori(square_updated, ch)

            def pre_now(ch):
                root(ch, 2, RMS_EPS)
                in_fori(hi_h, ch)

            mc, ll, ml, fc, fl, al = (chains[k] for k in ("mix_c", "ln_l", "mix_l", "ffn_c", "ffn_l", "att_l"))
            ada_phase("ada0a", 0, 0, hooks={1: input_squares})
            root(chains["in_c"], 1, RMS_EPS)
            in_fori(hi_h, chains["in_c"])
            hi_first(phases["pw1c"], phases["ada0a"])
            root(chains["in_l"], 1, RMS_EPS)
            in_fori(hi_h, chains["in_l"])
            glu_phase("pw1c", None)
            glu_phase("pw1l", "pw1c")
            lc = chains["ln_c"]
            ada_phase("ada0b", 0, 2 * KD, (2,), {2: lambda: (in_fori(ln_square, lc), root(lc, 2, LN_EPS),
                                                             in_fori(ln_silu, lc))})
            y_phase("pw2c", "ada0b")
            ada_phase("ada1", 1, 0, (1, 3, 4), {0: lambda: root(mc, 1, RMS_EPS),
                                             1: lambda: in_fori(square_updated, mc),
                                             3: lambda: root(mc, 2, RMS_EPS),
                                             4: lambda: in_fori(hi_h, mc)})
            up_phase("up0c", "ada1", 0, FFN_CUTS, {5: lambda: root(ll, 2, LN_EPS)},
                     {1: pairs_of(ln_square, ll, 1), 5: pairs_of(ln_silu, ll, 5)})
            y_phase("pw2l", "up0c")

            ml_steps = {(0, 2): [lambda: root(ml, 1, RMS_EPS)], (0, 11): [lambda: root(ml, 2, RMS_EPS)]}
            for k in range(KD // 2):
                ml_steps[0, 5 + k] = [lambda k=k: pairs_of(square_updated, ml)(k)]
                ml_steps[1, 3 + k] = [lambda k=k: pairs_of(hi_h, ml)(k)]
            y_phase("down0c", "pw2l", steps=ml_steps)
            up_phase("up0l", "down0c", 0, FFN_CUTS,
                     {1: lambda: root(fc, 1, RMS_EPS), 5: lambda: root(fc, 2, RMS_EPS)},
                     {1: pairs_of(square_updated, fc, 1), 5: pairs_of(hi_h, fc, 5)})
            y_phase("down0l", "up0l")
            act.wait_ge(blk, phases["qkv"].blk0)
            act.dma_start(mask[:, :], mask_in).then_inc(mask_in_s, 16)
            post_now(fl)
            pre_now(fl)

            ph = phases["qkv"]
            hi_first(ph, phases["down0l"])

            def qkv_evac(m, q, b):
                act.wait_ge(blk, b(1))
                act.activation(qT[q][:, :].rearrange("p (n r c) -> p r n c", n=NB, c=NA_KW),
                               bank[0][:, 0:L].rearrange("p (r n c) -> p r n c", n=NB, c=NA_KW),
                               ACT.Copy, scale=SCALE).then_inc(kv_ev, 1)
                yield 0
                act.wait_ge(blk, b(2))
                act.activation(kT[q][:, L:L + C], bank[2][:, 0:C], ACT.Copy).then_inc(kv_ev, 1)
                act.activation(kT[q][:, 0:L], bank[1][:, 0:L], ACT.Copy).then_inc(kv_ev, 1)
                yield 1
                act.wait_ge(blk, b(3))
                for n in range(NB):
                    act.activation(vT[q][:, n * WIN:(n + 1) * WIN].rearrange("p (r c) -> p r c", c=KB_W),
                                   window(bank[3][:, 0:L], n, 0, NA_KH), ACT.Copy)
                act.activation(vT[q][:, NB * WIN:NB * WIN + C], bank[2][:, C:2 * C], ACT.Copy).then_inc(kv_ev, 2)
                yield 2

            def take_pair(it, mj, last):
                def b(k):
                    return it * 6 + (ph.blk0 + 3 * mj + k)
                for j in qkv_evac(None, mj, b):
                    hi_ahead(ph, it, 3 * mj + j, last)

            def exp_tile(m, t):
                h = t % 2
                act.wait_ge(s_neg, m * 8 + (t + 1))
                act.activation(probs[h][:, :], scores[h][:, :], ACT.Exp, bias=negmax[h][:, :],
                               accum_out=rowsum[h][:, :]).then_inc(p_exp, 1)

            def pt_copy(m, t):
                act.wait_ge(pt_tr, m * 8 + (t + 2))
                if t >= 2:
                    act.wait_ge(pv, m * 8 + t)
                act.activation(probsT[t % 2][:, :], TURNED[t % 2][:, :], ACT.Copy).then_inc(pt_ev, 1)

            def by_rows(ap):
                return ap.rearrange("p (n r c) -> p r n c", n=NB, c=NA_KW)

            def o_tile(t, m):
                return t[:, ds(m * L, L)].rearrange("p (r n c) -> p r n c", n=NB, c=NA_KW)

            def attend(m, ahead):
                exp_tile(m, 0)
                exp_tile(m, 1)
                ahead()
                for t in range(8):
                    pt_copy(m, t)
                    if t + 2 < 8:
                        exp_tile(m, t + 2)
                act.wait_ge(pv, m * 8 + 9)
                act.activation(o_tile(Ohi, m), by_rows(bank[4][:, :]), ACT.Copy).then_inc(o_hi, 1)

            act.activation(negmax_credit[:, :], ident[:, 0:1], ACT.Copy).then_inc(pt_ev, 1)
            take_pair(0, 0, False)
            with act.Fori(0, ph.iters - 2) as it:
                attend(it * 2, lambda: take_pair(it, 1, False))
                attend(it * 2 + 1, lambda: take_pair(it + 1, 0, False))
            for it in (ph.iters - 2, ph.iters - 1):
                last = it == ph.iters - 1
                attend(it * 2, lambda: take_pair(it, 1, last))
                attend(it * 2 + 1, lambda: None if last else take_pair(it + 1, 0, True))

            y_phase("o", "qkv")
            post_now(al)
            pre_now(al)
            up_phase("up1", "o", 1)
            y_phase("down1", "up1")
            root(chains["out_l"], 1, RMS_EPS)
            for i in range(8):
                h, j = i // 4, i % 4
                act.wait_ge(out_tr, i + 1)
                act.activation(final[:, j * D + h * 512:j * D + (h + 1) * 512], bank[i % 4][:, :],
                               ACT.Copy).then_inc(out_ev, 1)

        @block.vector
        def _(dve):
            def lo_of(ph, it, j):
                s, kt = ph.slot(j), ph.kts[j]
                dve.wait_ge(w_hi, it * ph.per + (ph.spl0 + j + 1))
                dve.tensor_tensor(wlo[s][:, 0:kt * P], raw[s][:, 0:kt * P],
                                  whi[s][:, 0:kt * P].bitcast(F32), ALU.subtract).then_inc(w_lo, 1)

            dve.memset(negmax[0][:, :], 0.0).then_inc(gate_cv, 1)
            dve.memset(negmax[1][:, :], 0.0).then_inc(g_rdy, 1)
            dve.memset(rowmax[0][:, :], 0.0).then_inc(prod, 1)
            dve.memset(rowmax[1][:, :], 0.0).then_inc(prod, 1)
            dve.memset(rowinv[0][:, :], 0.0).then_inc(s_max, 1)
            dve.memset(spacer[:, :], 0.0).then_inc(s_max, 1)
            dve.memset(rowinv[1][:, :], 0.0).then_inc(o_lo, 1)

            def gains(side, layer, kinds):
                for kind in kinds:
                    part = {0: 1, 1: 2, 2: 4, 3: 5}[kind]
                    g = {0: "mix_pre_g", 1: "mix_post_g", 2: "ffn_pre_g", 3: "ffn_post_g"}[kind]
                    c0 = mod_cols(side, layer, part)
                    d0 = drv_col0(side, layer, kind)
                    v0 = at[g] + layer * KD
                    dve.scalar_tensor_tensor(drv[:, d0:d0 + KD], mod[:, c0:c0 + KD],
                                             1.0 if kind in (0, 2) else 0.0, vec[:, v0:v0 + KD],
                                             ALU.add, ALU.mult).then_inc(mods, 1)

            dve.wait_ge(rpb_in, 16)
            dve.tensor_copy(rpb_back[0:HEADS, :], rpb_rows[0:HEADS, ::-1]).then_inc(rpb_rev, 1)
            dve.wait_ge(evac, VT)
            dve.wait_ge(ada_ev, 2 * KD // 4)
            gains(CTX, 0, (0,))
            gains(LAT, 0, (0,))
            dve.wait_ge(mods, 2)

            def recip(ch, stage):
                dve.wait_ge(rms, ch.rms0 + stage)
                dve.reciprocal(RINV[:, 0:ch.n], RINV[:, 0:ch.n]).then_inc(rcp, 1)
                dve.wait_ge(rcp, ch.rms0 + stage)

            def update_pair(ch, t):
                n, s = ch.n, ch.side
                for j in range(2):
                    y = ch.Y[:, ds(t * (2 * n) + j * n, n)]
                    dve.scalar_tensor_tensor(y, y, drv[:, ds(t * 2 + (ch.gain + j), 1)], RINV[:, 0:n],
                                             ALU.mult, ALU.mult).then_inc(y_sc, 1)
                for j in range(2):
                    xk = X[s][:, ds(t * (2 * n) + j * n, n)]
                    dve.wait_ge(y_sc, t * 2 + (ch.up0 + j + 1))
                    dve.tensor_tensor(xk, xk, ch.Y[:, ds(t * (2 * n) + j * n, n)], ALU.add).then_inc(x_up, 1)

            def scale_pair(ch, t):
                n, s = ch.n, ch.side
                for j in range(2):
                    tile = ds(t * (2 * n) + j * n, n)
                    dve.scalar_tensor_tensor(SQ[s][:, tile], X[s][:, tile],
                                             drv[:, ds(t * 2 + (ch.pre[0] + j), 1)], RINV[:, 0:n],
                                             ALU.mult, ALU.mult).then_inc(t_rdy, 1)

            def lo_pair(ch, t):
                n, s = ch.n, ch.side
                for j in range(2):
                    tile = ds(t * (2 * n) + j * n, n)
                    dve.wait_ge(h_hi, t * 2 + (ch.h0 + j + 1))
                    dve.scalar_tensor_tensor(Hlo[s][:, tile], SQ[s][:, tile],
                                             mod[:, ds(t * 2 + (ch.pre[1] + j), 1)],
                                             Hhi[s][:, tile].bitcast(F32),
                                             ALU.add, ALU.subtract).then_inc(h_lo, 1)

            def modulate_pair(ch, t):
                scale_pair(ch, t)
                lo_pair(ch, t)

            def ln_centre_pair(ch, t):
                n, s = ch.n, ch.side
                for j in range(2):
                    v = V[s][:, ds(t * (2 * n) + j * n, n)]
                    dve.scalar_tensor_tensor(v, STAT[:, 0:n], -1.0 / D, v, ALU.mult, ALU.add).then_inc(centred, 1)

            def ln_scale_pair(ch, t):
                n, s = ch.n, ch.side
                for j in range(2):
                    v = V[s][:, ds(t * (2 * n) + j * n, n)]
                    dve.scalar_tensor_tensor(v, v, vcol("cv_ln_g", t * 2 + j), RINV[:, 0:n],
                                             ALU.mult, ALU.mult).then_inc(t_rdy, 1)

            def ln_lo_pair(ch, t):
                n, s = ch.n, ch.side
                i = 0 if s == CTX else 1
                for j in range(2):
                    tile = ds(t * (2 * n) + j * n, n)
                    dve.wait_ge(h_val, t * 2 + (i * KD + j + 1))
                    dve.tensor_copy(Hhi[s][:, tile], V[s][:, tile]).then_inc(h_hi, 1)
                for j in range(2):
                    tile = ds(t * (2 * n) + j * n, n)
                    dve.wait_ge(h_hi, t * 2 + (ch.h0 + j + 1))
                    dve.tensor_tensor(Hlo[s][:, tile], V[s][:, tile], Hhi[s][:, tile].bitcast(F32),
                                      ALU.subtract).then_inc(h_lo, 1)

            def in_fori(*steps):
                for f, ch in steps:
                    with dve.Fori(0, KD // 2) as t:
                        f(ch, t)

            def post_now(ch):
                recip(ch, 1)
                with dve.Fori(0, KD // 2) as t:
                    update_pair(ch, t)

            def pre_now(ch, stage=2):
                recip(ch, stage)
                in_fori((scale_pair, ch), (lo_pair, ch))

            pre_now(chains["in_c"], 1)
            pre_now(chains["in_l"], 1)

            def convolve(side, a, b):
                n, w = N[side], UW[side]
                g0, t0 = (2, 0) if side == CTX else (2 + KD, KD * (TAPS - 1))
                with dve.Fori(a, b) as t:
                    dve.wait_ge(glu, t * 2 + (g0 + 2))
                    for s in range(TAPS):
                        for j in range(2):
                            v = V[side][:, ds(t * (2 * n) + j * n, n)]
                            u = U[side][:, ds(t * (2 * w) + j * w + s, n)]
                            w_col = vcol("cv_w_dw", t * 2 + (s * KD + j))
                            if s == 0:
                                ins = dve.tensor_scalar(v, u, w_col, vcol("cv_b_dw", t * 2 + j), ALU.mult, ALU.add)
                            else:
                                dve.wait_ge(tap, t * (2 * (TAPS - 1)) + (t0 + 2 * s - 1 + j))
                                ins = dve.scalar_tensor_tensor(v, u, w_col, v, ALU.mult, ALU.add)
                            ins.then_inc(conv if s == TAPS - 1 else tap, 1)

            def ln_first(ch, i):
                dve.wait_ge(stat, ch.stat0 + 1)
                dve.wait_ge(conv, KD + 2 if i == 0 else 2 * KD - POOL_CONV)

            convolve(CTX, 0, KD // 2)
            lc, ll = chains["ln_c"], chains["ln_l"]
            convolve(LAT, 0, 1)
            ln_first(lc, 0)
            in_fori((ln_centre_pair, lc))
            recip(lc, 1)
            in_fori((ln_scale_pair, lc), (ln_lo_pair, lc))
            convolve(LAT, 1, 2)
            dve.wait_ge(ada_ev, MOD // 4)
            for side in (CTX, LAT):
                for kind in (1, 2, 3):
                    gains(side, 0, (kind,))
            dve.wait_ge(mods, 8)
            mc, ml, fc, fl, al = (chains[k] for k in ("mix_c", "mix_l", "ffn_c", "ffn_l", "att_l"))
            post_now(mc)
            convolve(LAT, 2, 3)
            pre_now(mc)
            dve.wait_ge(pool_conv, POOL_CONV)
            dve.wait_ge(ada_ev, 2 * MOD // 4)
            for side in (CTX, LAT):
                for kind in (0, 1, 2, 3):
                    gains(side, 1, (kind,))
            dve.wait_ge(mods, 16)

            def up_phase(name, layer, summed_before, cuts=(), hooks=None, inside=None):
                ph = phases[name]
                side, n, p0 = ph.side, N[ph.side], up_pairs0[name]
                dve.wait_ge(summed, summed_before)
                dve.memset(gate_in[0][:, 0:1], 0.0).then_inc(pads, 1)
                dve.memset(gate_in[0][:, n + 1:n + 2], 0.0).then_inc(pads, 1)
                dve.wait_ge(pads, 2 * (ups.index(name) + 1))

                def body(it, last):
                    for p in range(2):
                        gt = gate[0][:, 0:n]
                        m = it * 2 + p
                        dve.wait_ge(evac, it * 2 + (ph.evac0 + p + 1))
                        dve.scalar_tensor_tensor(gt, gate_in[0][:, 0:n], vcol("ffn_w_dw", m + layer * 3 * KF),
                                                 gt, ALU.mult, ALU.add).then_inc(tap, 1)
                        dve.wait_ge(tap, it * 2 + ((2 * KD - POOL_CONV) * (TAPS - 1) + p0 + p + 1))
                        dve.scalar_tensor_tensor(gt, gate_in[0][:, 2:n + 2],
                                                 vcol("ffn_w_dw", m + (layer * 3 + 2) * KF),
                                                 gt, ALU.mult, ALU.add).then_inc(gate_cv, 1)
                        dve.wait_ge(gelu, it * 2 + (p0 + p + 1))
                        dve.wait_ge(blk, it * 4 + (ph.blk0 + 2 * p + 2))
                        dve.tensor_tensor(gt, gt, bank[2 * p + 1][:, 0:n], ALU.mult).then_inc(prod, 1)
                        dve.wait_ge(prod, it * 2 + (2 + p0 + p + 1))
                        hi = Ghi[side][:, ds(it * (2 * n) + p * n, n)]
                        dve.tensor_copy(hi, gt).then_inc(g_hi, 1)
                        dve.wait_ge(g_hi, it * 2 + (p0 + p + 1))
                        dve.tensor_tensor(Glo[side][:, ds(it * (2 * n) + p * n, n)], gt, hi.bitcast(F32),
                                          ALU.subtract).then_inc(g_rdy, 1)

                loop(dve, ph, body, cuts, hooks, inside)

            up_phase("up0c", 0, sum0["conv_l"], FFN_CUTS,
                     {1: lambda: ln_first(ll, 1), 5: lambda: recip(ll, 1)},
                     {1: lambda it: ln_centre_pair(ll, it - 1),
                      5: lambda it: (ln_scale_pair(ll, it - 5), ln_lo_pair(ll, it - 5))})
            post_now(ml)
            pre_now(ml)
            up_phase("up0l", 0, sum0["down0l"], FFN_CUTS,
                     {1: lambda: recip(fc, 1), 5: lambda: recip(fc, 2)},
                     {1: lambda it: update_pair(fc, it - 1), 5: lambda it: modulate_pair(fc, it - 5)})
            post_now(fl)
            pre_now(fl)

            def v_by_token(m, q):
                for b in range(3):
                    w = 512 if b < 2 else 256
                    dve.wait_ge(vt_tr, m * 3 + (b + 1))
                    dve.tensor_copy(vtok[q][:, b * 512:b * 512 + w], bank[7][:, 0:w]).then_inc(vt_ev, 1)

            def take_max(i, t):
                par, hp, n = t % 2, t % 2, t // 2
                if t < 2:
                    dve.wait_ge(bias_rdy, i[0] * 2 + (hp + 1))
                dve.wait_ge(s_rdy, i[0] * 8 + (t + 1))
                dve.memset(spacer[:, :], 0.0)
                dve.tensor_tensor_reduce(out=scores[par][:, :], in0=SCORES[n % 2][hp][:, :],
                                         in1=bias[hp][:, n * 512:(n + 1) * 512], scale=1.0, scalar=-3e38,
                                         op0=ALU.add, op1=ALU.max,
                                         accum_out=rowmax[par][:, :]).then_inc(s_max, 1)
                dve.wait_ge(s_max, i[0] * 8 + (t + 3))
                dve.tensor_scalar(negmax[par][:, :], rowmax[par][:, :], -1.0, None, ALU.mult).then_inc(s_neg, 1)

            def normalise(i, t):
                par = t % 2
                dve.wait_ge(p_exp, i[0] * 8 + (t + 1))
                dve.reciprocal(rowinv[par][:, :], rowsum[par][:, :]).then_inc(p_inv, 1)
                dve.wait_ge(p_inv, i[0] * 8 + (t + 1))
                dve.tensor_scalar(probs[par][:, :], probs[par][:, :], rowinv[par][:, :], None,
                                  ALU.mult).then_inc(p_nrm, 1)

            def attend(m, q):
                v_by_token(m, q)
                i = (m,)
                take_max(i, 0)
                take_max(i, 1)
                for t in range(8):
                    normalise(i, t)
                    if t + 2 < 8:
                        take_max(i, t + 2)
                dve.wait_ge(o_hi, m + 1)
                o = [t[:, ds(m * L, L)].rearrange("p (r n c) -> p r n c", n=NB, c=NA_KW) for t in (Olo, Ohi)]
                b4 = bank[4][:, :].rearrange("p (n r c) -> p r n c", n=NB, c=NA_KW)
                dve.tensor_tensor(o[0], b4, o[1].bitcast(F32), ALU.subtract).then_inc(o_lo, 1)

            with dve.Fori(0, KD // 2) as it:
                attend(it * 2, 0)
                attend(it * 2 + 1, 1)

            post_now(al)
            pre_now(al)
            up_phase("up1", 1, sum0["down1"])
            post_now(chains["out_l"])

        @block.tensor
        def _(pe):
            pe.wait_ge(cst_in, 16)
            n_loads = sum(-(-((at[name] % P) + ap.shape[0]) // P) for name, ap in vectors.items())
            pe.wait_ge(v_in, 16 * n_loads)
            evs = 0

            def own_bank():
                if evs >= 4:
                    pe.wait_ge(evac, evs - 3)
                return bank[evs % 4]

            for t in range(VT):
                b = own_bank()
                r = min(P, rows - t * P)
                pe.transpose(b[:, 0:r], vec_rows[0:r, t * P:(t + 1) * P], ident[0:r, 0:r]).then_inc(turned, 1)
                evs += 1
            for side, s, t0 in ((CTX, c_in, L // P), (LAT, x_in, 0)):
                pe.wait_ge(s, 16)
                for k in range(KD):
                    b = own_bank()
                    for t in range(N[side] // P):
                        ins = pe.transpose(b[:, t * P:(t + 1) * P],
                                           tok[:, (t0 + t) * D + k * P:(t0 + t) * D + (k + 1) * P], ident[:, :])
                    ins.then_inc(turned, 1)
                    evs += 1

            def ada_phase(name, layer, m0, cuts=(), hooks=None):
                ph = phases[name]
                c0 = (layer * MOD + m0) // 4
                pe.wait_ge(evac, ph.evac0)

                def body(it, last):
                    for u in range(2):
                        for b in range(4):
                            j = 4 * u + b
                            s = ph.slot(j)
                            pe.wait_ge(w_in[s], it * 32 + (ph.landed0[s] + 16 * (j // ph.ring + 1)))
                            for i in range(2):
                                k = 2 * b + i
                                for g in range(4):
                                    c = i * CHUNK + g * P
                                    ins = pe.matmul(bank[u][32 * g:32 * g + 2, 0:P], cond[:, k:2 * KD:KD],
                                                    raw[s][:, c:c + P], start=(k == 0), stop=(k == KD - 1))
                            ins.then_inc(blk, 1)
                        pe.wait_ge(row_out, it * 2 + (c0 + u + 1))
                        pe.transpose(ADA_T[u][:, 0:P], ada_row[u][:, :], ident[:, :]).then_inc(ada_tr, 1)

                loop(pe, ph, body, cuts, hooks)

            def products(b, n, s, kts, hi, lo, k0, first, last, ready=None):
                for k in range(kts):
                    if ready:
                        pe.wait_ge(ready[0], ready[1] + k0 + k + 1)
                    w = slice(k * P, (k + 1) * P)
                    a = slice((k0 + k) * n, (k0 + k + 1) * n)
                    pe.matmul(b, whi[s][:, w], hi[:, a], start=(first and k == 0), stop=False)
                    pe.matmul(b, whi[s][:, w], lo[:, a], start=False, stop=False)
                    ins = pe.matmul(b, wlo[s][:, w], hi[:, a], start=False, stop=(last and k == kts - 1))
                return ins

            def split_wait(ph, it, j):
                pe.wait_ge(w_lo, it * ph.per + (ph.spl0 + j + 1))

            def linear(name, ready, cuts=(), hooks=None):
                ph = phases[name]
                n = N[ph.side]
                hi, lo = (Ohi, Olo) if name == "o" else (Hhi[ph.side], Hlo[ph.side])

                def body(it, last):
                    for j in range(4):
                        split_wait(ph, it, j)
                        if ph.kind == "up" and j % 2 == 0:
                            pe.wait_ge(evac, it * 2 + (ph.evac0 + j // 2 - 1))
                        elif ph.kind == "up":
                            pe.wait_ge(prod, it * 2 + (2 + up_pairs0[name] + j // 2 - 1))
                        else:
                            pe.wait_ge(evac, it * 4 + (ph.evac0 + j - 3))
                            if name == "pw2l" and j % 2 == 1:
                                pe.wait_ge(prod, 2 + KF - 1 + j // 2)
                        at_first = isinstance(it, int) and (it, j) == (0, 0)
                        products(bank[j][:, 0:n], n, ph.slot(j), KD, hi, lo, 0, True, True,
                                 ready if at_first else None).then_inc(blk, 1)

                loop(pe, ph, body, (1, *cuts), hooks)

            def down(name, pairs0, steps=None):
                ph = phases[name]
                n = N[ph.side]
                pe.wait_ge(evac, ph.evac0)

                def body(it, last):
                    for j in range(ph.per):
                        t, part = j // 3, j % 3
                        split_wait(ph, it, j)
                        if part == 0:
                            pe.wait_ge(evac, it * 4 + (ph.evac0 + t - 3))
                        products(bank[t][:, 0:n], n, ph.slot(j), DOWN_K[part], Ghi[ph.side], Glo[ph.side],
                                 DOWN_R[part], part == 0, part == 2,
                                 (g_rdy, 1 + pairs0) if (it, t) == (0, 0) else None).then_inc(blk, 1)
                        for step in (steps or {}).get((it, j), ()):
                            step()

                loop(pe, ph, body)

            def stat_sum(ch, name):
                pe.wait_ge(summed, sum0[name] + KD + 1)
                pe.matmul(STAT[:, 0:ch.n], ones[:, :], acc[ch.side][:, :], start=True, stop=True).then_inc(stat, 1)

            def stat_squares(ch):
                for k in range(KD):
                    pe.wait_ge(x_sq, ch.sq0 + k + 1)
                    ins = pe.matmul(STAT[:, 0:ch.n], ones[:, :], SQ[ch.side][:, k * ch.n:(k + 1) * ch.n],
                                    start=(k == 0), stop=(k == KD - 1))
                ins.then_inc(stat, 1)

            pe.wait_ge(cond_s, 1)
            def normed(name):
                return h_lo, chains[name].h0

            mc, ll, ml, fc, fl, al = (chains[k] for k in ("mix_c", "ln_l", "mix_l", "ffn_c", "ffn_l", "att_l"))
            pe.wait_ge(ones_s, 1)
            ada_phase("ada0a", 0, 0, hooks={1: lambda: stat_squares(chains["in_c"])})
            pe.wait_ge(rms, 1)
            stat_squares(chains["in_l"])
            linear("pw1c", normed("in_c"))
            linear("pw1l", normed("in_l"))
            lc = chains["ln_c"]

            def ln_c_stats():
                stat_sum(lc, "conv_c")
                pe.wait_ge(centred, KD)
                stat_squares(lc)

            ada_phase("ada0b", 0, 2 * KD, (2,), {2: ln_c_stats})
            linear("pw2c", normed("ln_c"))
            stat_sum(mc, "pw2c")
            ada_phase("ada1", 1, 0, (2,), {2: lambda: stat_squares(mc)})

            def ln_l_squares():
                pe.wait_ge(centred, 2 * KD)
                stat_squares(ll)

            linear("up0c", normed("mix_c"), FFN_CUTS, {1: lambda: stat_sum(ll, "conv_l"), 5: ln_l_squares})
            linear("pw2l", normed("ln_l"))
            down("down0c", 0, {(0, 1): [lambda: stat_sum(ml, "pw2l")], (0, 10): [lambda: stat_squares(ml)]})
            linear("up0l", normed("mix_l"), FFN_CUTS,
                   {1: lambda: stat_sum(fc, "down0c"), 5: lambda: stat_squares(fc)})
            down("down0l", KF)
            stat_sum(fl, "down0l")
            stat_squares(fl)

            ph = phases["qkv"]
            pe.wait_ge(evac, ph.evac0)

            def qkv_products(it, mj, first=False):
                ready = normed("ffn_l") if first else None
                """q, k and v of pair 2 it + mj."""
                def ev(k):
                    if not first:
                        pe.wait_ge(kv_ev, it * 10 + (5 * mj - 5 + k))
                b0, n1, n2 = bank, L, C
                s = [ph.slot(3 * mj + j) for j in range(3)]
                split_wait(ph, it, 3 * mj)
                ev(1)
                products(b0[0][:, 0:n1], n1, s[0], KD, Hhi[LAT], Hlo[LAT], 0, True, True,
                         ready).then_inc(blk, 1)
                split_wait(ph, it, 3 * mj + 1)
                ev(5)
                products(b0[1][:, 0:n1], n1, s[1], KD, Hhi[LAT], Hlo[LAT], 0, True, True)
                products(b0[2][:, 0:n2], n2, s[1], KD, Hhi[CTX], Hlo[CTX], 0, True, True).then_inc(blk, 1)
                split_wait(ph, it, 3 * mj + 2)
                products(b0[3][:, 0:n1], n1, s[2], KD, Hhi[LAT], Hlo[LAT], 0, True, True)
                pe.wait_ge(kv_ev, it * 10 + (5 * mj + 2))
                products(b0[2][:, n2:2 * n2], n2, s[2], KD, Hhi[CTX], Hlo[CTX], 0, True, True).then_inc(blk, 1)

            def turn_v(m, q, b):
                if b == 0:
                    pe.wait_ge(kv_ev, m * 5 + 5)
                    pe.wait_ge(pt_ev, m * 8 + 1)
                else:
                    pe.wait_ge(vt_ev, m * 3 + b)
                for i in range(4 if b < 2 else 2):
                    ins = pe.transpose(bank[7][:, i * P:(i + 1) * P],
                                       vT[q][:, (4 * b + i) * P:(4 * b + i + 1) * P], ident[:, :])
                ins.then_inc(vt_tr, 1)

            def score(m, q, n, products_ahead=True):
                if n < 2:
                    pe.wait_ge(s_max, m * 8 + 2)
                if n == 1 and products_ahead:
                    pe.wait_ge(kv_ev, m * 5 + 8)
                for part in range(2):
                    for h in range(2):
                        rows_ = slice(h * HEAD_D, (h + 1) * HEAD_D)
                        keys = kT[q][rows_, L:L + C] if part else window(kT[q][rows_, 0:L], n, 0, NA_KH)
                        if n >= 2 and part == 0:
                            pe.wait_ge(s_max, m * 8 + (2 * n + h - 1))
                        ins = pe.matmul(SCORES[n % 2][h][:, part * C:(part + 1) * C],
                                        qT[q][rows_, n * P:(n + 1) * P], keys, start=True, stop=True)
                        if part:
                            ins.then_inc(s_rdy, 1)

            def turn_p(m, t, products_ahead):
                if t >= 2:
                    pe.wait_ge(pt_ev, m * 8 + t)
                elif t == 1 and products_ahead:
                    pe.wait_ge(kv_ev, m * 5 + 10)
                pe.wait_ge(p_nrm, m * 8 + (t + 1))
                for i in range(4):
                    ins = pe.transpose(TURNED[t % 2][:, i * P:(i + 1) * P], probs[t % 2][:, i * P:(i + 1) * P],
                                       ident[:, :])
                ins.then_inc(pt_tr, 1)

            def weighted(m, q, n):
                if n == 0:
                    pe.wait_ge(o_lo, m + 1)
                pe.wait_ge(pt_ev, m * 8 + (2 * n + 3))
                for i in range(4):
                    c = 2 * n + i if i < 2 else 2 * NB + i - 2
                    for h in range(2):
                        ins = pe.matmul(bank[4][h * HEAD_D:(h + 1) * HEAD_D, n * P:(n + 1) * P],
                                        vtok[q][:, c * P + h * HEAD_D:c * P + (h + 1) * HEAD_D],
                                        probsT[h][:, i * P:(i + 1) * P], start=(i == 0), stop=(i == 3))
                        if i == 3:
                            ins.then_inc(pv, 1)

            def attend(m, q, ahead=None):
                turn_v(m, q, 0)
                score(m, q, 0)
                turn_v(m, q, 1)
                turn_v(m, q, 2)
                if ahead:
                    ahead()
                score(m, q, 1, bool(ahead))
                pe.wait_ge(vt_ev, m * 3 + 3)
                for n in range(NB):
                    turn_p(m, 2 * n, bool(ahead))
                    turn_p(m, 2 * n + 1, bool(ahead))
                    if n + 2 < NB:
                        score(m, q, n + 2)
                    weighted(m, q, n)

            qkv_products(0, 0, first=True)
            pe.transpose(bank[7][:, 0:P], ident[:, :], ident[:, :]).then_inc(pt_tr, 1)
            pe.matmul(bank[4][0:HEAD_D, 0:2], ident[:, 0:HEAD_D], ident[:, 0:2], start=True, stop=True).then_inc(pv, 1)
            with pe.Fori(0, ph.iters - 1) as it:
                attend(it * 2, 0, lambda: qkv_products(it, 1))
                attend(it * 2 + 1, 1, lambda: qkv_products(it + 1, 0))
            last = ph.iters - 1
            attend(2 * last, 0, lambda: qkv_products(last, 1))
            attend(2 * last + 1, 1)

            linear("o", (o_lo, 1))
            stat_sum(al, "o")
            stat_squares(al)
            linear("up1", normed("att_l"))
            down("down1", 2 * KF)
            fin = chains["out_l"]
            stat_sum(fin, "down1")
            for i in range(8):
                h, j = i // 4, i % 4
                pe.wait_ge(x_up, fin.up0 + 4 * (h + 1))
                pe.wait_ge(evac, phases["down1"].evac0 + KD)
                if i >= 4:
                    pe.wait_ge(out_ev, i - 3)
                for k in range(4):
                    kk = 4 * h + k
                    ins = pe.transpose(bank[i % 4][:, k * P:(k + 1) * P],
                                       X[LAT][:, kk * L + j * P:kk * L + (j + 1) * P], ident[:, :])
                ins.then_inc(out_tr, 1)


VECTORS = ["mod_b", "mix_pre_g", "mix_post_g", "ffn_pre_g", "ffn_post_g", "cv_b_pw1", "cv_b_dw", "cv_ln_g",
           "cv_ln_b", "cv_b_pw2", "cv_w_dw", "ffn_b_dw", "ffn_w_dw", "c", "c_ctx"]
MATRICES = ["mod_w", "cv_w_pw1", "cv_w_pw2", "na_w_qkv", "na_w_o", "ffn_w_up", "ffn_w_down", "na_rpb"]


def kernel(**inputs):
    import numpy as np
    import concourse.bacc as bacc
    from concourse.bass_utils import run_bass_kernel_spmd

    nc = bacc.Bacc("TRN2", target_bir_lowering=False, num_devices=1, dynamic_dma_scratch_size=1024)
    arrays = {}

    def give(name, a):
        arrays[f"in_{name}"] = a
        return nc.dram_tensor(f"in_{name}", a.shape, F32, kind="ExternalInput").ap()

    x = give("x", np.ascontiguousarray(inputs["x"])[0])
    ctx = give("ctx", np.ascontiguousarray(inputs["ctx"])[0])
    mats = {n: give(n, np.ascontiguousarray(inputs[n])) for n in MATRICES}
    vecs = {n: give(n, np.ascontiguousarray(inputs[n]).reshape(-1, P)) for n in VECTORS}

    ident = np.eye(P, dtype=np.float32)
    starts = col_starts()
    mask = np.zeros((P, len(starts), KB_W), np.float32)
    for p in range(P):
        for n, k0 in enumerate(starts):
            q = n * NA_KW + p % NA_KW
            c0 = min(max(q - NA_KW // 2, 0), GRID_W - NA_KW)
            for j in range(KB_W):
                if not c0 <= k0 + j < c0 + NA_KW:
                    mask[p, n, j] = NEG_INF
    ident_in = give("ident", ident)
    mask_in = give("mask", mask.reshape(P, -1))
    out = nc.dram_tensor("out", tuple(x.shape), F32, kind="ExternalOutput").ap()
    build(nc, x, ctx, **mats, vectors=vecs, ident_in=ident_in, mask_in=mask_in, out=out)
    r = run_bass_kernel_spmd(nc, [arrays], core_ids=[0])
    return r.results[0]["out"][None]
```

```python
from contextlib import ExitStack

import concourse.bass as bass
from concourse import mybir

F32 = mybir.dt.float32
F32R = mybir.dt.float32r
ALU = mybir.AluOpType
ACT = mybir.ActivationFunctionType
ds = bass.ds

P = 128
COMPACT = ("ffn_l", "att_l", "out_l")
SOME_TAPS = 14
POOL_CONV = 2
DVE_LO = 2
RING = 4
NEG_INF = -1e30
RMS_EPS = 1e-6
LN_EPS = 1e-5
GRID_W, NA_KH, NA_KW = 64, 8, 16
KB_W = 2 * NA_KW
LAT, CTX = "lat", "ctx"


def col_starts():
    return [min(max(n * NA_KW - NA_KW // 2, 0), GRID_W - KB_W) for n in range(GRID_W // NA_KW)]


class Phase:

    def __init__(self, name, kind, side, iters, kts, src, ring=RING, acc_evacs=0, width=P):
        self.name, self.kind, self.side, self.iters, self.kts, self.src = name, kind, side, iters, kts, src
        self.ring, self.acc_evacs = ring, acc_evacs
        self.per, self.width = len(kts), width
        self.split = kind != "ada"

    def slot(self, j):
        return j % self.ring


def lay_out_counts(phases, evacs_before):
    blk = spl = 0
    evac = evacs_before
    landed = [0] * RING
    user = [None] * RING
    reader = [0] * RING
    for ph in phases:
        ph.blk0, ph.spl0, ph.evac0 = blk, spl, evac
        ph.landed0, ph.user0, ph.reader0 = list(landed), list(user), list(reader)
        for i in range(ph.iters * ph.per):
            s = ph.slot(i % ph.per)
            landed[s] += 16
            blk += 1
            if ph.split:
                spl += 1
                reader[s] = blk
                user[s] = ("lo", spl)
            else:
                user[s] = ("pe", blk)
        evac += ph.acc_evacs


def build(nc, x, ctx, mod_w, cv_w_pw1, cv_w_pw2, na_w_qkv, na_w_o, ffn_w_up, ffn_w_down, na_rpb,
          vectors, ident_in, mask_in, out):
    L, D = x.shape
    C = ctx.shape[0]
    N = {LAT: L, CTX: C}
    KD = D // P
    F = ffn_w_down.shape[1]
    KF = F // P
    MOD = 6 * KD
    TAPS = vectors["cv_w_dw"].shape[0] // KD
    PADC = TAPS // 2
    HEAD_D = 64
    NB = GRID_W // NA_KW
    SCALE = HEAD_D ** -0.5
    RPB_ROWS, RPB_COLS = na_rpb.shape[2], na_rpb.shape[3]
    RPB_HEAD = RPB_ROWS * RPB_COLS
    HEADS = na_rpb.shape[1]
    RUN = (NA_KH - 1) * RPB_COLS + NA_KW + KB_W
    STARTS = col_starts()
    WIN = NA_KH * KB_W
    OFFS = [STARTS[n] - NA_KW * n for n in range(NB)]

    at, rows = {}, 0
    for name, ap in vectors.items():
        at[name] = rows
        rows += ap.shape[0]
    VT = (rows + P - 1) // P

    def w_cols(w, r0, kt, c, width=P):
        return w[r0:r0 + kt * P, ds(c, width)].rearrange("(k p) n -> p k n", p=P)

    CHUNK = 4 * P
    DOWN_K = [8, 7, 7]
    DOWN_R = [0, 8, 15]
    phases = {}

    def phase(name, kind, side, iters, kts, src, **kw):
        phases[name] = Phase(name, kind, side, iters, kts, src, **kw)

    def add_ada(name, layer, m0, tiles):
        phase(name, "ada", None, tiles // 8, [KD // 4] * 8,
              lambda it, j: w_cols(mod_w[layer], (j % 4) * (KD // 4) * P, KD // 4,
                                   it * (8 * P) + (m0 + j // 4 * 4) * P, CHUNK), width=CHUNK)

    def add_pw1(name, side):
        phase(name, "glu", side, KD // 2, [KD] * 4,
              lambda it, j: w_cols(cv_w_pw1[0], 0, KD, it * (2 * P) + (j % 2) * D + (j // 2) * P),
              acc_evacs=2 * KD)

    def add_square(name, side, w):
        phase(name, "y", side, KD // 4, [KD] * 4,
              lambda it, j: w_cols(w, 0, KD, it * (4 * P) + j * P), acc_evacs=KD)

    def add_up(name, side, layer):
        phase(name, "up", side, KF // 2, [KD] * 4,
              lambda it, j: w_cols(ffn_w_up[layer], 0, KD, it * (2 * P) + (j % 2) * F + (j // 2) * P),
              acc_evacs=KF)

    def add_down(name, side, layer):
        phase(name, "down", side, KD // 4, DOWN_K * 4,
              lambda it, j: w_cols(ffn_w_down[layer], DOWN_R[j % 3] * P, DOWN_K[j % 3],
                                   it * (4 * P) + (j // 3) * P), acc_evacs=KD)

    add_ada("ada0a", 0, 0, 2 * KD)
    add_pw1("pw1c", CTX)
    add_pw1("pw1l", LAT)
    add_ada("ada0b", 0, 2 * KD, 4 * KD)
    add_ada("ada1a", 1, 0, 3 * KD)
    add_square("pw2c", CTX, cv_w_pw2[0])
    add_ada("ada1b", 1, 3 * KD, 3 * KD)
    add_up("up0c", CTX, 0)
    add_square("pw2l", LAT, cv_w_pw2[0])
    add_down("down0c", CTX, 0)
    add_up("up0l", LAT, 0)
    add_down("down0l", LAT, 0)
    phase("qkv", "qkv", LAT, KD // 2, [KD] * 6,
          lambda it, j: w_cols(na_w_qkv[0], 0, KD, it * (2 * P) + (j % 3) * D + (j // 3) * P), ring=3)
    add_square("o", LAT, na_w_o[0])
    add_up("up1", LAT, 1)
    add_down("down1", LAT, 1)

    INIT_EVACS = VT + 2 * KD
    order = list(phases.values())
    lay_out_counts(order, INIT_EVACS)
    following = {a.name: b for a, b in zip(order, order[1:])}

    stack = ExitStack()
    with stack:
        def sb(name, cols, dt=F32, on=stack):
            return on.enter_context(nc.sbuf_tensor(name, [P, cols], dt))

        def sem(name):
            return stack.enter_context(nc.semaphore(name))

        X = {LAT: sb("x_lat", KD * L), CTX: sb("x_ctx", KD * C)}
        raw = [sb(f"w_raw{i}", KD * P) for i in range(RING)]
        whi = [sb(f"w_hi{i}", KD * P, F32R) for i in range(RING)]
        wlo = [sb(f"w_lo{i}", KD * P, F32R) for i in range(RING)]
        vec = sb("vectors", VT * P)
        mod = sb("modulation", 2 * 2 * MOD)
        drv = sb("derived", 2 * 2 * 4 * KD)
        ident = sb("ident", P)
        ones = sb("ones", P)
        cond = sb("cond", 2 * KD)
        acc = {LAT: sb("feature_sum_lat", L), CTX: sb("feature_sum_ctx", C)}
        rowmax = [sb(f"row_max{i}", 1) for i in range(2)]
        negmax = [sb(f"neg_max{i}", 1) for i in range(2)]
        rowsum = [sb(f"row_sum{i}", 1) for i in range(2)]
        spacer = sb("spacer", 1)
        pool_spacer, act_spacer = sb("pool_spacer", 1), sb("act_spacer", 1)
        rowinv = [sb(f"row_inv{i}", 1) for i in range(2)]

        with ExitStack() as g:
            gate_in, gate = sb("gate_in", L + 2, on=g), sb("gate", L, on=g)
        with ExitStack() as g:
            sq = [sb(f"sq{i}", L, on=g) for i in range(2)]
        with ExitStack() as g:
            probs1, probsT1 = sb("probs1", 512, on=g), sb("probs_t1", 512, on=g)
        ada_row = [sb(f"ada_row{i}", P) for i in range(2)]
        root_t, inv_t = ada_row
        sb("scratch_room", 2 * L + 8)

        Hhi, Hlo, Yh, SQ = {}, {}, {}, {}
        for side in (LAT, CTX):
            with ExitStack() as g:
                Hhi[side] = sb(f"h_hi_{side}", KD * N[side], F32R, on=g)
                Hlo[side] = sb(f"h_lo_{side}", KD * N[side], F32R, on=g)
            with ExitStack() as g:
                Yh[side] = sb(f"y_{side}", KD * N[side], on=g)
                SQ[side] = sb(f"squares_{side}", KD * N[side], on=g)
            sb(f"h_room_{side}", 2 * KD * N[side])

        with ExitStack() as g:
            tok = sb("x_by_token", (L + C) // P * D, on=g)
            vec_rows = sb("vector_rows", VT * P, on=g)
            rpb_rows = sb("rpb_rows", RPB_HEAD, on=g)
            rpb_back = sb("rpb_backwards", RPB_HEAD, on=g)
        UW = {s: N[s] + 2 * PADC for s in N}
        with ExitStack() as g:
            U, V, Yb, Ghi, Glo = {}, {}, {}, {}, {}
            with ExitStack() as h:
                U[LAT] = sb("u_lat", KD * UW[LAT], on=h)
            with ExitStack() as h:
                Yb[LAT] = sb("yb_lat", KD * L, on=h)
            sb("u_room", KD * UW[LAT], on=g)
            V[LAT] = sb("v_lat", KD * L, on=g)
            with ExitStack() as h:
                U[CTX] = sb("u_ctx", KD * UW[CTX], on=h)
                V[CTX] = sb("v_ctx", KD * C, on=h)
                glu_a = [sb(f"glu_a{i}", L, on=h) for i in range(2)]
                glu_s = [sb(f"glu_s{i}", L, on=h) for i in range(2)]
                Yb[CTX] = sb("yb_ctx", KD * C, on=h)
            Ghi[CTX] = sb("g_hi_ctx", KF * C, F32R, on=g)
            Glo[CTX] = sb("g_lo_ctx", KF * C, F32R, on=g)
        with ExitStack() as g:
            Ghi[LAT] = sb("g_hi", KF * L, F32R, on=g)
            Glo[LAT] = sb("g_lo", KF * L, F32R, on=g)
        with ExitStack() as g:
            Ohi = sb("o_hi", KD * L, F32R, on=g)
            Olo = sb("o_lo", KD * L, F32R, on=g)
            qT = [sb(f"q{i}", L, on=g) for i in range(2)]
            kT = [sb(f"k{i}", L + C, on=g) for i in range(2)]
            vT = [sb(f"v{i}", NB * NA_KH * KB_W + C, on=g) for i in range(2)]
            vtok = [sb(f"v_by_token{i}", (2 * NB + 2) * P, on=g) for i in range(2)]
            bias = [sb(f"bias{i}", NB * 512, on=g) for i in range(2)]
            table = sb("bias_table", 2 * RUN, on=g)
            mask = sb("mask", NB * KB_W, on=g)
            scores = [sb(f"scores{i}", 512, on=g) for i in range(2)]
            probs = [sb("probs0", 512, on=g)]
            probsT = [sb("probs_t0", 512, on=g)]
        probs.append(probs1)
        probsT.append(probsT1)
        with ExitStack() as g:
            final = sb("final_by_token", L // P * D, on=g)
        sb("large_room", 2 * KF * L + 160)

        bank = [stack.enter_context(nc.psum_tensor(f"bank{i}", [P, 512], F32)) for i in range(8)]
        STAT, RINV = bank[4], bank[6]
        FIRST = [bank[i] for i in (2, 3, 4, 6)]
        SCORES = [[bank[5], bank[6]], [bank[0], bank[1]]]
        TURNED = [bank[7], bank[2]]
        V_TURNED = bank[3]
        ADA_T = [bank[5], bank[7]]

        table_dram = nc.dram_tensor("padded_rpb", (NA_KW + na_rpb.shape[1] * RPB_HEAD + NA_KW,), F32,
                                    kind="Internal").ap()

        w_in = [sem(f"w_in{i}") for i in range(RING)]
        w_hi = sem("w_hi")
        w_lo = sem("w_lo")
        blk = sem("blk")
        evac = sem("evac")
        x_in, c_in, v_in, cst_in = sem("x_in"), sem("c_in"), sem("v_in"), sem("cst_in")
        rpb_in, pad_in, tab_in, mask_in_s = sem("rpb_in"), sem("pad_in"), sem("tab_in"), sem("mask_in")
        rpb_rev, rpb_out = sem("rpb_rev"), sem("rpb_out")
        zeros_s = sem("zeros")
        turned = sem("turned")
        ones_s = sem("ones_s")
        cond_s = sem("cond_s")
        row_out = sem("row_out")
        row_z = sem("row_z")
        ada_tr = sem("ada_tr")
        ada_ev = sem("ada_ev")
        mods = sem("mods")
        stat = sem("stat")
        rms = sem("rms")
        spread = sem("spread")
        rcp = sem("rcp")
        x_sq = sem("x_sq")
        sq_pair = sem("sq_pair")
        x_up = sem("x_up")
        y_sc = sem("y_sc")
        t_rdy = sem("t_rdy")
        h_hi = sem("h_hi")
        h_val = sem("h_val")
        h_lo = sem("h_lo")
        glu = sem("glu")
        tap = sem("tap")
        conv = sem("conv")
        pool_conv = sem("pool_conv")
        pool_tap = sem("pool_tap")
        centred = sem("centred")
        summed = sem("summed")
        pads = sem("pads")
        gate_t0 = sem("gate_t0")
        gate_cv = sem("gate_cv")
        gelu = sem("gelu")
        prod = sem("prod")
        g_hi = sem("g_hi")
        g_rdy = sem("g_rdy")
        kv_ev = sem("kv_ev")
        vt_tr, vt_ev = sem("vt_tr"), sem("vt_ev")
        bias_rdy = sem("bias_rdy")
        bias_z = sem("bias_z")
        s_rdy = sem("s_rdy")
        s_max, s_neg = sem("s_max"), sem("s_neg")
        p_exp = sem("p_exp")
        p_inv, p_nrm = sem("p_inv"), sem("p_nrm")
        pt_tr, pt_ev = sem("pt_tr"), sem("pt_ev")
        pv = sem("pv")
        o_hi, o_lo = sem("o_hi"), sem("o_lo")
        out_tr, out_ev = sem("out_tr"), sem("out_ev")
        stored = sem("stored")

        def vcol(name, i):
            return vec[:, ds(at[name] + i, 1)]

        def window(ap, n, r0, r1):
            return ap.rearrange("p (r c) -> p r c", c=GRID_W)[:, r0:r1, STARTS[n]:STARTS[n] + KB_W]

        def mod_cols(side, layer, part):
            return ((0 if side == LAT else 1) * 2 + layer) * MOD + part * KD

        def drv_col0(side, layer, kind):
            return ((layer * 2 + (0 if side == LAT else 1)) * 4 + kind) * KD

        class Chain:
            def __init__(self, side, Y=None, gain=None, pre=None):
                self.side, self.Y, self.gain, self.pre, self.n = side, Y, gain, pre, N[side]
                self.pair0, self.compact = None, False

        def pre_of(side, layer, ffn):
            return (drv_col0(side, layer, 2 if ffn else 0), mod_cols(side, layer, 3 if ffn else 0))

        chains = {
            "in_c": Chain(CTX, pre=pre_of(CTX, 0, False)),
            "in_l": Chain(LAT, pre=pre_of(LAT, 0, False)),
            "ln_c": Chain(CTX),
            "mix_c": Chain(CTX, Yb[CTX], drv_col0(CTX, 0, 1), pre_of(CTX, 0, True)),
            "ln_l": Chain(LAT),
            "mix_l": Chain(LAT, Yb[LAT], drv_col0(LAT, 0, 1), pre_of(LAT, 0, True)),
            "ffn_c": Chain(CTX, Yh[CTX], drv_col0(CTX, 0, 3), pre_of(CTX, 1, False)),
            "ffn_l": Chain(LAT, Yh[LAT], drv_col0(LAT, 0, 3), pre_of(LAT, 1, False)),
            "att_l": Chain(LAT, Yh[LAT], drv_col0(LAT, 1, 1), pre_of(LAT, 1, True)),
            "out_l": Chain(LAT, Yh[LAT], drv_col0(LAT, 1, 3)),
        }
        for name in COMPACT:
            chains[name].compact = True
        spread0 = {name: 2 * i for i, name in enumerate(COMPACT)}
        paired = ["in_l", "ln_l", "mix_l", "ffn_c"]
        for i, name in enumerate(paired):
            chains[name].pair0 = i * (KD // 2)
        for name in COMPACT:
            chains[name].spread0 = spread0[name]
        n_stat = n_rms = n_sq = n_up = n_h = 0
        for name, ch in chains.items():
            ln = name.startswith("ln")
            ch.stat0, ch.rms0, ch.sq0, ch.up0, ch.h0 = n_stat, n_rms, n_sq, n_up, n_h
            n_stat += (ch.Y is not None) + (ch.pre is not None) + 2 * ln
            n_rms += (ch.Y is not None) + (ch.pre is not None) + ln
            n_up += KD * (ch.Y is not None)
            n_sq += KD * (ch.pre is not None or ln)
            n_h += KD * (ch.pre is not None or ln)
        sums = ["conv_c", "pw2c", "conv_l", "pw2l", "down0c", "down0l", "o", "down1"]
        sum0 = {name: i * (KD + 1) for i, name in enumerate(sums)}
        y_of = {"pw2c": Yb[CTX], "pw2l": Yb[LAT], "down0c": Yh[CTX], "down0l": Yh[LAT], "o": Yh[LAT],
                "down1": Yh[LAT]}
        ups = ["up0c", "up0l", "up1"]
        up_pairs0 = {name: i * KF for i, name in enumerate(ups)}

        def bank0(name):
            return 3 if name == "o" else 0

        def loop(eng, ph, body, cuts=(), hooks=None, inside=None):
            hooks, inside = hooks or {}, inside or {}
            edges = sorted({0, *cuts, ph.iters - 1, ph.iters})
            for a, b in zip(edges, edges[1:]):
                if a in hooks:
                    hooks[a]()
                if b - a == 1:
                    body(a, b == ph.iters)
                    if a in inside:
                        inside[a](a)
                else:
                    with eng.Fori(a, b) as it:
                        body(it, False)
                        if a in inside:
                            inside[a](it)
            if ph.iters in hooks:
                hooks[ph.iters]()

        FFN_CUTS = (1, 5, 6, 10)

        block = stack.enter_context(nc.Block())

        @block.sync
        def _(sp):
            def load(ph, it, j, first):
                s = ph.slot(j)
                if first and j < ph.ring:
                    if ph.user0[s]:
                        who, n = ph.user0[s]
                        sp.wait_ge(w_lo if who == "lo" else blk, n)
                elif ph.split:
                    sp.wait_ge(w_lo, it * ph.per + (ph.spl0 + j - ph.ring + 1))
                else:
                    sp.wait_ge(blk, it * ph.per + (ph.blk0 + j - ph.ring + 1))
                kt = ph.kts[j]
                sp.dma_start(raw[s][:, 0:kt * ph.width].rearrange("p (k n) -> p k n", n=ph.width),
                             ph.src(it, j)).then_inc(w_in[s], 16)

            def tables(it, j, first):
                if not (first and j == 0):
                    sp.wait_ge(bias_rdy, it * 4 + 2 * j)
                else:
                    sp.wait_ge(rpb_out, 16)
                    sp.wait_ge(pad_in, 32)
                    sp.wait_ge(g_rdy, 1 + 2 * KF)
                    sp.wait_ge(blk, phases["qkv"].blk0)
                for hp in range(2):
                    src = bass.AP(tensor=table_dram.tensor, offset=it * (4 * RPB_HEAD) + (2 * j + hp) * RPB_HEAD,
                                  ap=[[RPB_COLS, P // NA_KW], [1, NA_KW], [1, RUN]])
                    sp.dma_start(table[:, hp * RUN:(hp + 1) * RUN], src).then_inc(tab_in, 16)

            for ph in order:
                def body(it, first):
                    for j in range(ph.per):
                        load(ph, it, j, first)
                        if ph.kind == "qkv" and j % 3 == 2:
                            tables(it, j // 3, first)

                body(0, True)
                if ph.iters > 2:
                    with sp.Fori(1, ph.iters) as it:
                        body(it, False)
                elif ph.iters == 2:
                    body(1, False)

            for j in range(L // P):
                for h in range(2):
                    sp.wait_ge(out_ev, h * 4 + j + 1)
                    sp.dma_start(out[j * P:(j + 1) * P, h * 512:(h + 1) * 512],
                                 final[:, j * D + h * 512:j * D + (h + 1) * 512]).then_inc(stored, 16)
            sp.wait_ge(stored, 16 * 2 * (L // P))

        @block.gpsimd
        def _(pool):
            pool.memset(ones[:, :], 1.0).then_inc(ones_s, 1)
            for t in ada_row:
                pool.memset(t[:, :], 0.0).then_inc(row_z, 1)
            pool.memset(acc[CTX][:, 0:NA_KW], 0.0).then_inc(zeros_s, 1)

            def lo_of(ph, it, j):
                s, kt = ph.slot(j), ph.kts[j]
                pool.wait_ge(w_hi, it * ph.per + (ph.spl0 + j + 1))
                pool.tensor_tensor(wlo[s][:, 0:kt * P], raw[s][:, 0:kt * P],
                                   whi[s][:, 0:kt * P].bitcast(F32), ALU.subtract).then_inc(w_lo, 1)

            def lo_ahead(ph, it, j, last):
                nj, nit, nph = j + ph.ring, it, ph
                if nj >= ph.per:
                    nj -= ph.per
                    if last:
                        nph, nit = following.get(ph.name), 0
                        if nph is None or not nph.split or nj >= nph.ring:
                            return
                    else:
                        nit = it + 1
                lo_of(nph, nit, nj)

            def lo_first(ph, prev):
                n = min(prev.ring, ph.ring) if prev.split else 0
                if ph.name == "up0c":
                    n = DVE_LO
                    pool.wait_ge(w_lo, ph.spl0 + n)
                for j in range(n, ph.ring):
                    lo_of(ph, 0, j)

            def add_up(side, base, tile, src, waits):
                waits()
                pool.wait_ge(summed, tile + (base + 1))
                pool.tensor_tensor(acc[side][:, :], acc[side][:, :], src, ALU.add).then_inc(summed, 1)

            pool.wait_ge(evac, INIT_EVACS)
            pool.wait_ge(rpb_out, 16)
            for s in (LAT, CTX):
                u, w = U[s], UW[s]
                pool.memset(u[:, 0:PADC], 0.0)
                between = u[:, w - PADC:KD * w - PADC].rearrange("p (m c) -> p m c", c=w, m=KD - 1)
                pool.memset(between[:, :, 0:2 * PADC], 0.0)
                pool.memset(u[:, KD * w - PADC:KD * w], 0.0).then_inc(glu, 1)
            pool.wait_ge(glu, 2)

            for name, prev in (("pw1c", "ada0a"), ("pw1l", "pw1c")):
                ph = phases[name]
                n, w = N[ph.side], UW[ph.side]
                g0 = 2 + (KD if name == "pw1l" else 0)
                lo_first(ph, phases[prev])

                def body(it, last):
                    for j in range(4):
                        if j % 2 == 1:
                            p = j // 2
                            pool.wait_ge(evac, it * 4 + (ph.evac0 + j + 1))
                            pool.tensor_tensor(U[ph.side][:, ds(it * (2 * w) + p * w + PADC, n)],
                                               glu_a[p][:, 0:n], glu_s[p][:, 0:n], ALU.mult).then_inc(glu, 1)
                        lo_ahead(ph, it, j, last)

                loop(pool, ph, body)

            taps_done = 0

            def convolve(m, s0, s1):
                nonlocal taps_done
                w = UW[LAT]
                v = V[LAT][:, m * L:(m + 1) * L]
                for s in range(s0, s1):
                    u = U[LAT][:, m * w + s:m * w + s + L]
                    if s == 0:
                        pool.tensor_scalar(v, u, vcol("cv_w_dw", m), vcol("cv_b_dw", m), ALU.mult,
                                           ALU.add).then_inc(pool_tap, 1)
                        taps_done += 1
                        continue
                    scaled = glu_a[s % 2][:, 0:L]
                    pool.tensor_scalar(scaled, u, vcol("cv_w_dw", s * KD + m), 1.0, ALU.mult,
                                       ALU.mult).then_inc(pool_tap, 1)
                    pool.wait_ge(pool_tap, taps_done + 1)
                    ins = pool.tensor_tensor(v, v, scaled, ALU.add)
                    ins.then_inc(pool_tap, 1)
                    taps_done += 2
                if s1 < TAPS:
                    return
                pool.wait_ge(pool_tap, taps_done)
                pool.memset(pool_spacer[:, :], 0.0).then_inc(pool_conv, 1)

            def conv_sums(side, name, c0):
                base = sum0[name]
                pool.memset(acc[side][:, :], 0.0).then_inc(summed, 1)
                by_dve = KD if side == CTX else KD - POOL_CONV
                with pool.Fori(0, by_dve) as m:
                    add_up(side, base, m, V[side][:, ds(m * N[side], N[side])],
                           lambda: pool.wait_ge(conv, m + (c0 + 1)))
                for m in range(by_dve, KD):
                    add_up(side, base, m, V[side][:, m * N[side]:(m + 1) * N[side]],
                           lambda: pool.wait_ge(pool_conv, m - by_dve + 1))

            def y_phase(name, prev, stat_read):
                ph = phases[name]
                side, n, base = ph.side, N[ph.side], sum0[name]
                pool.wait_ge(stat, stat_read)
                pool.memset(acc[side][:, :], 0.0).then_inc(summed, 1)
                lo_first(ph, phases[prev])

                def body(it, last):
                    tiles = 0
                    for j in range(ph.per):
                        if ph.kind == "y" or j % 3 == 2:
                            t = tiles
                            add_up(side, base, it * 4 + t, sq[t % 2][:, 0:n],
                                   lambda: pool.wait_ge(evac, it * 4 + (ph.evac0 + t + 1)))
                            tiles += 1
                        lo_ahead(ph, it, j, last)

                loop(pool, ph, body)

            def up_phase(name, prev):
                ph = phases[name]
                lo_first(ph, phases[prev])

                def body(it, last):
                    for j in range(ph.per):
                        lo_ahead(ph, it, j, last)

                loop(pool, ph, body)

            pool.wait_ge(pad_in, 32)
            conv_sums(CTX, "conv_c", 0)
            convolve(KD - 2, 0, TAPS)
            convolve(KD - 1, 0, SOME_TAPS)
            y_phase("pw2c", "ada1a", chains["ln_c"].stat0 + 1)
            convolve(KD - 1, SOME_TAPS, TAPS)
            conv_sums(LAT, "conv_l", KD)
            up_phase("up0c", "ada1b")
            y_phase("pw2l", "up0c", chains["ln_l"].stat0 + 1)
            y_phase("down0c", "pw2l", chains["mix_c"].stat0 + 1)
            up_phase("up0l", "down0c")
            y_phase("down0l", "up0l", chains["mix_l"].stat0 + 1)

            ph = phases["qkv"]

            def head_bias(m, hp):
                if hp == 0:
                    pool.wait_ge(tab_in, m * 32 + 32)
                for n in range(NB):
                    run = table[:, hp * RUN:(hp + 1) * RUN]
                    rel = bass.AP(tensor=run.tensor, offset=run.offset + RUN - 1 - NA_KW - OFFS[n],
                                  ap=[list(run.ap[0]), [-RPB_COLS, NA_KH], [-1, KB_W]])
                    mk = mask[:, n * KB_W:(n + 1) * KB_W]
                    mk = bass.AP(tensor=mk.tensor, offset=mk.offset, ap=[list(mk.ap[0]), [0, NA_KH], [1, KB_W]])
                    ins = pool.tensor_tensor(
                        bias[hp][:, n * 512:n * 512 + 256].rearrange("p (k j) -> p k j", j=KB_W),
                        rel, mk, ALU.add)
                ins.then_inc(bias_rdy, 1)

            pool.wait_ge(blk, ph.blk0)
            for hp in range(2):
                pool.memset(bias[hp][:, :], 0.0).then_inc(bias_z, 1)
            pool.wait_ge(bias_z, 2)
            pool.wait_ge(mask_in_s, 16)
            lo_first(ph, phases["down0l"])
            head_bias(0, 0)
            head_bias(0, 1)

            def qkv_body(it, last):
                for j in range(ph.per):
                    lo_ahead(ph, it, j, last)
                    mj = j // 3
                    if j % 3 == 2 and not (isinstance(it, int) and it == 0 and mj == 0):
                        for hp in range(2):
                            pool.wait_ge(s_max, it * 16 + (8 * mj - 8 + 7 + hp + 2))
                            head_bias(it * 2 + mj, hp)

            loop(pool, ph, qkv_body, cuts=(1,))

            y_phase("o", "qkv", chains["ffn_l"].stat0 + 1)
            up_phase("up1", "o")
            y_phase("down1", "up1", chains["att_l"].stat0 + 1)

        @block.scalar
        def _(act):
            act.dma_start(ident[:, :], ident_in).then_inc(cst_in, 16)
            loads = 0
            for name, ap in vectors.items():
                r, n = at[name], ap.shape[0]
                done = 0
                while done < n:
                    p = (r + done) % P
                    k = min(n - done, P - p)
                    t = (r + done) // P
                    act.dma_start(vec_rows[p:p + k, t * P:(t + 1) * P], ap[done:done + k, :]).then_inc(v_in, 16)
                    done += k
                    loads += 1
            act.dma_start(tok[:, L // P * D:].rearrange("p (t d) -> p t d", d=D),
                          ctx.rearrange("(t p) d -> p t d", p=P)).then_inc(c_in, 16)
            act.dma_start(tok[:, 0:L // P * D].rearrange("p (t d) -> p t d", d=D),
                          x.rearrange("(t p) d -> p t d", p=P)).then_inc(x_in, 16)

            rpb_size = na_rpb.shape[1] * RPB_HEAD
            act.wait_ge(zeros_s, 1)
            for start in (0, NA_KW + rpb_size):
                act.dma_start(table_dram[start:start + NA_KW].rearrange("(a n) -> a n", a=1),
                              acc[CTX][0:1, 0:NA_KW]).then_inc(pad_in, 16)
            act.dma_start(rpb_rows[0:HEADS, :], na_rpb[0].rearrange("h a b -> h (a b)")).then_inc(rpb_in, 16)

            def hi_of(ph, it, j, first):
                s, kt = ph.slot(j), ph.kts[j]
                act.wait_ge(w_in[s], it * (16 * ph.per // ph.ring) + (ph.landed0[s] + 16 * (j // ph.ring + 1)))
                if first and j < ph.ring:
                    if ph.reader0[s]:
                        act.wait_ge(blk, ph.reader0[s])
                else:
                    act.wait_ge(blk, it * ph.per + (ph.blk0 + j - ph.ring + 1))
                act.activation(whi[s][:, 0:kt * P], raw[s][:, 0:kt * P], ACT.Copy).then_inc(w_hi, 1)

            def hi_ahead(ph, it, j, last):
                nj, nit, nph = j + ph.ring, it, ph
                if nj >= ph.per:
                    nj -= ph.per
                    if last:
                        nph, nit = following.get(ph.name), 0
                        if nph is None or not nph.split or nj >= nph.ring:
                            return
                        hi_of(nph, 0, nj, True)
                        return
                    nit = it + 1
                hi_of(nph, nit, nj, False)

            def hi_first(ph, prev):
                n = min(prev.ring, ph.ring) if prev.split else 0
                for j in range(n, ph.ring):
                    hi_of(ph, 0, j, True)

            def root(ch, stage, eps):
                act.wait_ge(stat, ch.stat0 + stage)
                w = P if ch.compact else ch.n
                act.activation((root_t if ch.compact else RINV)[:, 0:w], STAT[:, 0:w], ACT.Sqrt, bias=eps,
                               scale=1.0 / D).then_inc(rms, 1)

            def square_of(ch, t, j):
                tile = ds(t * (2 * ch.n) + j * ch.n, ch.n)
                act.activation(SQ[ch.side][:, tile], X[ch.side][:, tile], ACT.Square).then_inc(x_sq, 1)

            def square_updated(ch, t, j):
                act.wait_ge(x_up, t * 2 + (ch.up0 + j + 1))
                square_of(ch, t, j)

            def hi_h(ch, t, j):
                act.wait_ge(t_rdy, t * 2 + (ch.h0 + j + 1))
                tile = ds(t * (2 * ch.n) + j * ch.n, ch.n)
                act.activation(Hhi[ch.side][:, tile], SQ[ch.side][:, tile],
                               ACT.Identity, bias=mod[:, ds(t * 2 + (ch.pre[1] + j), 1)]).then_inc(h_hi, 1)

            evs = 0
            for t in range(VT):
                act.wait_ge(turned, evs + 1)
                act.activation(vec[:, t * P:(t + 1) * P], FIRST[evs % 4][:, 0:P], ACT.Copy).then_inc(evac, 1)
                evs += 1
            act.wait_ge(evac, VT)
            act.activation(cond[:, :], vec[:, at["c"]:at["c"] + 2 * KD], ACT.Silu).then_inc(cond_s, 1)

            def read_inputs():
                nonlocal evs
                for side in (CTX, LAT):
                    for k in range(KD):
                        act.wait_ge(turned, evs + 1)
                        act.activation(X[side][:, k * N[side]:(k + 1) * N[side]], FIRST[evs % 4][:, 0:N[side]],
                                       ACT.Copy).then_inc(evac, 1)
                        evs += 1
                act.wait_ge(evac, INIT_EVACS)
                in_fori(square_of, chains["in_c"])
                root(chains["in_c"], 1, RMS_EPS)
                in_fori(square_of, chains["in_l"])

            def table_out():
                act.wait_ge(rpb_rev, 1)
                act.dma_start(table_dram[NA_KW:NA_KW + rpb_size].rearrange("(h n) -> h n", n=RPB_HEAD),
                              rpb_back[0:HEADS, :]).then_inc(rpb_out, 16)

            def glu_phase(name, prev, cuts=(), step=None):
                ph = phases[name]
                n = N[ph.side]
                g0 = 2 + (KD if name == "pw1l" else 0)
                if prev:
                    hi_first(ph, phases[prev])

                def body(it, last):
                    for j in range(4):
                        p = j // 2
                        act.wait_ge(blk, it * 4 + (ph.blk0 + j + 1))
                        if j % 2 == 0:
                            act.wait_ge(glu, it * 2 + (g0 + p - 1))
                            act.activation(glu_a[p][:, 0:n], bank[j][:, 0:n], ACT.Identity,
                                           bias=vcol("cv_b_pw1", it * 2 + p)).then_inc(evac, 1)
                        else:
                            act.activation(glu_s[p][:, 0:n], bank[j][:, 0:n], ACT.Sigmoid,
                                           bias=vcol("cv_b_pw1", it * 2 + (KD + p))).then_inc(evac, 1)
                        hi_ahead(ph, it, j, last)
                        if step and isinstance(it, int) and it == 0:
                            step(j)

                loop(act, ph, body, cuts)

            def ada_phase(name, layer, m0, cuts=(), hooks=None):
                ph = phases[name]
                c0 = (layer * MOD + m0) // 4
                act.wait_ge(row_z, 2)

                def body(it, last):
                    for u in range(2):
                        act.wait_ge(blk, it * 8 + (ph.blk0 + 4 * u + 4))
                        for g in range(4):
                            r = slice(32 * g, 32 * g + 2)
                            ins = act.activation(ada_row[u][r, :], bank[u][r, 0:P], ACT.Copy)
                        ins.then_inc(row_out, 1)
                    for u in range(2):
                        act.wait_ge(ada_tr, it * 2 + (c0 + u + 1))
                        for i in range(4):
                            m = layer * MOD + m0 + 4 * u + i
                            cols = mod[:, ds(it * 8 + m, 2, step=2 * MOD)]
                            ins = act.activation(cols, ADA_T[u][:, 32 * i:32 * i + 2], ACT.Identity,
                                                 bias=vcol("mod_b", it * 8 + m))
                        ins.then_inc(ada_ev, 1)

                loop(act, ph, body, cuts, hooks)

            def ln_square(ch, t, j):
                i = 0 if ch.side == CTX else 1
                act.wait_ge(centred, t * 2 + (i * KD + j + 1))
                tile = ds(t * (2 * ch.n) + j * ch.n, ch.n)
                act.activation(SQ[ch.side][:, tile], V[ch.side][:, tile], ACT.Square).then_inc(x_sq, 1)

            def ln_silu(ch, t, j):
                act.wait_ge(t_rdy, t * 2 + (ch.h0 + j + 1))
                bcol = vcol("cv_ln_b", t * 2 + j)
                tile = ds(t * (2 * ch.n) + j * ch.n, ch.n)
                act.activation(V[ch.side][:, tile], V[ch.side][:, tile], ACT.Silu, bias=bcol).then_inc(h_val, 1)

            def pairs_of(f, ch, a=0):
                def step(it):
                    for j in range(2):
                        f(ch, it - a, j)
                return step

            def in_fori(f, ch):
                with act.Fori(0, KD // 2) as t:
                    pairs_of(f, ch)(t)

            def y_phase(name, prev, steps=None):
                ph = phases[name]
                n, Y, q0 = N[ph.side], y_of[name], sum0[name]
                hi_first(ph, phases[prev])
                act.activation(act_spacer[:, :], ident[:, 0:1], ACT.Sqrt)
                if ph.kind == "y" and prev.startswith("up"):
                    act.wait_ge(g_rdy, 1 + up_pairs0[prev] + KF)

                def body(it, last):
                    tiles = 0
                    for j in range(ph.per):
                        if ph.kind == "y" or j % 3 == 2:
                            t = tiles
                            tiles += 1
                            act.wait_ge(blk, it * ph.per + (ph.blk0 + j + 1))
                            act.wait_ge(summed, it * 4 + (q0 + t))
                            kw = {"bias": vcol("cv_b_pw2", it * 4 + t)} if name.startswith("pw2") else {}
                            f = ACT.Identity if kw else ACT.Copy
                            b = bank[(t + bank0(name)) % 4]
                            act.activation(Y[:, ds(it * (4 * n) + t * n, n)], b[:, 0:n], f, **kw)
                            act.activation(sq[t % 2][:, 0:n], b[:, 0:n], ACT.Square, **kw).then_inc(evac, 1)
                        hi_ahead(ph, it, j, last)
                        for step in (steps or {}).get((it, j), ()):
                            step()

                loop(act, ph, body)

            def up_phase(name, prev, layer, cuts=(), hooks=None, inside=None):
                ph = phases[name]
                n, p0 = N[ph.side], up_pairs0[name]
                hi_first(ph, phases[prev])
                act.wait_ge(pads, 2 * (ups.index(name) + 1))

                def body(it, last):
                    for j in range(4):
                        p = j // 2
                        act.wait_ge(blk, it * 4 + (ph.blk0 + j + 1))
                        if j % 2 == 0:
                            act.wait_ge(gate_cv, it * 2 + (p0 + p + 1))
                            act.activation(gate_in[:, 1:n + 1], bank[j][:, 0:n], ACT.Copy).then_inc(gate_t0, 1)
                            act.wait_ge(g_rdy, it * 2 + (p0 + p + 1))
                            act.activation(gate[:, 0:n], bank[j][:, 0:n], ACT.Identity,
                                           bias=vcol("ffn_b_dw", it * 2 + (layer * KF + p)),
                                           scale=vcol("ffn_w_dw", it * 2 + ((layer * 3 + 1) * KF + p))
                                           ).then_inc(evac, 1)
                        else:
                            act.wait_ge(gate_cv, it * 2 + (p0 + p + 2))
                            act.activation(gate[:, 0:n], gate[:, 0:n],
                                           ACT.Gelu_apprx_tanh).then_inc(gelu, 1)
                        hi_ahead(ph, it, j, last)

                loop(act, ph, body, cuts, hooks, inside)

            def post_now(ch):
                root(ch, 1, RMS_EPS)
                if ch.pre:
                    in_fori(square_updated, ch)

            def pre_now(ch):
                root(ch, 2, RMS_EPS)
                in_fori(hi_h, ch)

            mc, ll, ml, fc, fl, al = (chains[k] for k in ("mix_c", "ln_l", "mix_l", "ffn_c", "ffn_l", "att_l"))
            ada_phase("ada0a", 0, 0, hooks={1: read_inputs})
            table_out()
            hi_first(phases["pw1c"], phases["ada0a"])
            in_fori(hi_h, chains["in_c"])
            root(chains["in_l"], 1, RMS_EPS)
            glu_phase("pw1c", None, (1,), pairs_of(hi_h, chains["in_l"]))
            glu_phase("pw1l", "pw1c")
            lc = chains["ln_c"]
            ada_phase("ada0b", 0, 2 * KD)
            ada_phase("ada1a", 1, 0, hooks={2: lambda: (in_fori(ln_square, lc), root(lc, 2, LN_EPS),
                                                        in_fori(ln_silu, lc))})
            y_phase("pw2c", "ada1a")
            ada_phase("ada1b", 1, 3 * KD, (1,), {0: lambda: root(mc, 1, RMS_EPS),
                                                 1: lambda: in_fori(square_updated, mc),
                                                 2: lambda: (root(mc, 2, RMS_EPS), in_fori(hi_h, mc))})
            up_phase("up0c", "ada1b", 0, FFN_CUTS, {6: lambda: root(ll, 2, LN_EPS)},
                     {1: pairs_of(ln_square, ll, 1), 6: pairs_of(ln_silu, ll, 6)})
            y_phase("pw2l", "up0c")

            ml_steps = {(0, 2): [lambda: root(ml, 1, RMS_EPS)], (0, 11): [lambda: root(ml, 2, RMS_EPS)]}
            for k in range(KD // 2):
                ml_steps[0, 5 + k] = [lambda k=k: pairs_of(square_updated, ml)(k)]
                ml_steps[1, 3 + k] = [lambda k=k: pairs_of(hi_h, ml)(k)]
            y_phase("down0c", "pw2l", steps=ml_steps)
            up_phase("up0l", "down0c", 0, FFN_CUTS,
                     {1: lambda: root(fc, 1, RMS_EPS), 6: lambda: root(fc, 2, RMS_EPS)},
                     {1: pairs_of(square_updated, fc, 1), 6: pairs_of(hi_h, fc, 6)})
            y_phase("down0l", "up0l")
            act.wait_ge(blk, phases["qkv"].blk0)
            act.dma_start(mask[:, :], mask_in).then_inc(mask_in_s, 16)
            post_now(fl)
            pre_now(fl)

            ph = phases["qkv"]
            hi_first(ph, phases["down0l"])

            def qkv_evac(q, b):
                act.wait_ge(blk, b(1))
                act.activation(qT[q][:, :].rearrange("p (n r c) -> p r n c", n=NB, c=NA_KW),
                               bank[0][:, 0:L].rearrange("p (r n c) -> p r n c", n=NB, c=NA_KW),
                               ACT.Copy, scale=SCALE).then_inc(kv_ev, 1)
                yield 0
                act.wait_ge(blk, b(2))
                act.activation(kT[q][:, L:L + C], bank[2][:, 0:C], ACT.Copy).then_inc(kv_ev, 1)
                act.activation(kT[q][:, 0:L], bank[1][:, 0:L], ACT.Copy).then_inc(kv_ev, 1)
                yield 1
                act.wait_ge(blk, b(3))
                for n in range(NB):
                    act.activation(vT[q][:, n * WIN:(n + 1) * WIN].rearrange("p (r c) -> p r c", c=KB_W),
                                   window(bank[3][:, 0:L], n, 0, NA_KH), ACT.Copy)
                act.activation(vT[q][:, NB * WIN:NB * WIN + C], bank[2][:, C:2 * C], ACT.Copy).then_inc(kv_ev, 2)
                yield 2

            def take_pair(it, mj, last):
                def b(k):
                    return it * 6 + (ph.blk0 + 3 * mj + k)
                for j in qkv_evac(mj, b):
                    hi_ahead(ph, it, 3 * mj + j, last)

            def exp_tile(m, t):
                h = t % 2
                act.wait_ge(s_neg, m * 8 + (t + 1))
                act.activation(probs[h][:, :], scores[h][:, :], ACT.Exp, bias=negmax[h][:, :],
                               accum_out=rowsum[h][:, :]).then_inc(p_exp, 1)

            def pt_copy(m, t):
                act.wait_ge(pt_tr, m * 8 + (t + 2))
                if t >= 2:
                    act.wait_ge(pv, m * 8 + t)
                act.activation(probsT[t % 2][:, :], TURNED[t % 2][:, :], ACT.Copy).then_inc(pt_ev, 1)

            def by_rows(ap):
                return ap.rearrange("p (n r c) -> p r n c", n=NB, c=NA_KW)

            def o_tile(t, m):
                return t[:, ds(m * L, L)].rearrange("p (r n c) -> p r n c", n=NB, c=NA_KW)

            def attend(m, ahead):
                exp_tile(m, 0)
                exp_tile(m, 1)
                ahead()
                for t in range(8):
                    pt_copy(m, t)
                    if t + 2 < 8:
                        exp_tile(m, t + 2)
                act.wait_ge(pv, m * 8 + 9)
                act.activation(o_tile(Ohi, m), by_rows(bank[4][:, :]), ACT.Copy).then_inc(o_hi, 1)

            act.activation(act_spacer[:, :], ident[:, 0:1], ACT.Copy).then_inc(pt_ev, 1)
            take_pair(0, 0, False)
            with act.Fori(0, ph.iters - 2) as it:
                attend(it * 2, lambda: take_pair(it, 1, False))
                attend(it * 2 + 1, lambda: take_pair(it + 1, 0, False))
            for it in (ph.iters - 2, ph.iters - 1):
                last = it == ph.iters - 1
                attend(it * 2, lambda: take_pair(it, 1, last))
                attend(it * 2 + 1, lambda: None if last else take_pair(it + 1, 0, True))

            y_phase("o", "qkv")
            post_now(al)
            pre_now(al)
            up_phase("up1", "o", 1)
            y_phase("down1", "up1")
            root(chains["out_l"], 1, RMS_EPS)
            for i in range(8):
                h, j = i // 4, i % 4
                act.wait_ge(out_tr, i + 1)
                act.activation(final[:, j * D + h * 512:j * D + (h + 1) * 512], bank[i % 4][:, :],
                               ACT.Copy).then_inc(out_ev, 1)

        @block.vector
        def _(dve):
            dve.memset(negmax[0][:, :], 0.0).then_inc(gate_cv, 1)
            dve.memset(negmax[1][:, :], 0.0).then_inc(g_rdy, 1)
            dve.memset(rowmax[0][:, :], 0.0).then_inc(prod, 1)
            dve.memset(rowmax[1][:, :], 0.0).then_inc(prod, 1)
            dve.memset(rowinv[0][:, :], 0.0).then_inc(s_max, 1)
            dve.memset(spacer[:, :], 0.0).then_inc(s_max, 1)
            dve.memset(rowinv[1][:, :], 0.0).then_inc(o_lo, 1)

            def gains(side, layer, kinds):
                for kind in kinds:
                    part = {0: 1, 1: 2, 2: 4, 3: 5}[kind]
                    g = {0: "mix_pre_g", 1: "mix_post_g", 2: "ffn_pre_g", 3: "ffn_post_g"}[kind]
                    c0 = mod_cols(side, layer, part)
                    d0 = drv_col0(side, layer, kind)
                    v0 = at[g] + layer * KD
                    dve.scalar_tensor_tensor(drv[:, d0:d0 + KD], mod[:, c0:c0 + KD],
                                             1.0 if kind in (0, 2) else 0.0, vec[:, v0:v0 + KD],
                                             ALU.add, ALU.mult).then_inc(mods, 1)

            dve.wait_ge(rpb_in, 16)
            dve.tensor_copy(rpb_back[0:HEADS, :], rpb_rows[0:HEADS, ::-1]).then_inc(rpb_rev, 1)
            dve.wait_ge(evac, VT)

            def recip(ch, stage):
                dve.wait_ge(rms, ch.rms0 + stage)
                if ch.compact:
                    dve.reciprocal(inv_t[:, :], root_t[:, :]).then_inc(rcp, 1)
                    dve.wait_ge(spread, ch.spread0 + stage)
                else:
                    dve.reciprocal(RINV[:, 0:ch.n], RINV[:, 0:ch.n]).then_inc(rcp, 1)
                    dve.wait_ge(rcp, ch.rms0 + stage)

            def update_pair(ch, t):
                n, s = ch.n, ch.side
                for j in range(2):
                    y = ch.Y[:, ds(t * (2 * n) + j * n, n)]
                    dve.scalar_tensor_tensor(y, y, drv[:, ds(t * 2 + (ch.gain + j), 1)], RINV[:, 0:n],
                                             ALU.mult, ALU.mult).then_inc(y_sc, 1)
                for j in range(2):
                    xk = X[s][:, ds(t * (2 * n) + j * n, n)]
                    dve.wait_ge(y_sc, t * 2 + (ch.up0 + j + 1))
                    dve.tensor_tensor(xk, xk, ch.Y[:, ds(t * (2 * n) + j * n, n)], ALU.add).then_inc(x_up, 1)

            def add_squares_pair(ch, t):
                n, sq_ = ch.n, SQ[ch.side]
                dve.wait_ge(x_sq, t * 2 + (ch.sq0 + 2))
                even = sq_[:, ds(t * (2 * n), n)]
                dve.tensor_tensor(even, even, sq_[:, ds(t * (2 * n) + n, n)], ALU.add).then_inc(sq_pair, 1)

            def scale_pair(ch, t):
                n, s = ch.n, ch.side
                for j in range(2):
                    tile = ds(t * (2 * n) + j * n, n)
                    dve.scalar_tensor_tensor(SQ[s][:, tile], X[s][:, tile],
                                             drv[:, ds(t * 2 + (ch.pre[0] + j), 1)], RINV[:, 0:n],
                                             ALU.mult, ALU.mult).then_inc(t_rdy, 1)

            def lo_pair(ch, t):
                n, s = ch.n, ch.side
                for j in range(2):
                    tile = ds(t * (2 * n) + j * n, n)
                    dve.wait_ge(h_hi, t * 2 + (ch.h0 + j + 1))
                    dve.scalar_tensor_tensor(Hlo[s][:, tile], SQ[s][:, tile],
                                             mod[:, ds(t * 2 + (ch.pre[1] + j), 1)],
                                             Hhi[s][:, tile].bitcast(F32),
                                             ALU.add, ALU.subtract).then_inc(h_lo, 1)

            def ln_centre_pair(ch, t):
                n, s = ch.n, ch.side
                for j in range(2):
                    v = V[s][:, ds(t * (2 * n) + j * n, n)]
                    dve.scalar_tensor_tensor(v, STAT[:, 0:n], -1.0 / D, v, ALU.mult, ALU.add).then_inc(centred, 1)

            def ln_scale_pair(ch, t):
                n, s = ch.n, ch.side
                for j in range(2):
                    v = V[s][:, ds(t * (2 * n) + j * n, n)]
                    dve.scalar_tensor_tensor(v, v, vcol("cv_ln_g", t * 2 + j), RINV[:, 0:n],
                                             ALU.mult, ALU.mult).then_inc(t_rdy, 1)

            def ln_lo_pair(ch, t):
                n, s = ch.n, ch.side
                i = 0 if s == CTX else 1
                for j in range(2):
                    tile = ds(t * (2 * n) + j * n, n)
                    dve.wait_ge(h_val, t * 2 + (i * KD + j + 1))
                    dve.tensor_copy(Hhi[s][:, tile], V[s][:, tile]).then_inc(h_hi, 1)
                for j in range(2):
                    tile = ds(t * (2 * n) + j * n, n)
                    dve.wait_ge(h_hi, t * 2 + (ch.h0 + j + 1))
                    dve.tensor_tensor(Hlo[s][:, tile], V[s][:, tile], Hhi[s][:, tile].bitcast(F32),
                                      ALU.subtract).then_inc(h_lo, 1)

            def in_fori(*steps):
                for f, ch in steps:
                    with dve.Fori(0, KD // 2) as t:
                        f(ch, t)

            def post_now(ch):
                recip(ch, 1)
                with dve.Fori(0, KD // 2) as t:
                    update_pair(ch, t)

            def pre_now(ch, stage=2):
                recip(ch, stage)
                in_fori((scale_pair, ch), (lo_pair, ch))

            recip(chains["in_c"], 1)
            in_fori((add_squares_pair, chains["in_l"]))
            dve.wait_ge(ada_ev, 2 * KD // 4)
            gains(CTX, 0, (0,))
            gains(LAT, 0, (0,))
            dve.wait_ge(mods, 2)
            in_fori((scale_pair, chains["in_c"]), (lo_pair, chains["in_c"]))
            pre_now(chains["in_l"], 1)

            def convolve(side, a, b):
                n, w = N[side], UW[side]
                g0, t0 = (2, 0) if side == CTX else (2 + KD, KD * (TAPS - 1))
                with dve.Fori(a, b) as t:
                    dve.wait_ge(glu, t * 2 + (g0 + 2))
                    for s in range(TAPS):
                        for j in range(2):
                            v = V[side][:, ds(t * (2 * n) + j * n, n)]
                            u = U[side][:, ds(t * (2 * w) + j * w + s, n)]
                            w_col = vcol("cv_w_dw", t * 2 + (s * KD + j))
                            if s == 0:
                                ins = dve.tensor_scalar(v, u, w_col, vcol("cv_b_dw", t * 2 + j), ALU.mult, ALU.add)
                            else:
                                dve.wait_ge(tap, t * (2 * (TAPS - 1)) + (t0 + 2 * s - 1 + j))
                                ins = dve.scalar_tensor_tensor(v, u, w_col, v, ALU.mult, ALU.add)
                            ins.then_inc(conv if s == TAPS - 1 else tap, 1)

            def ln_first(ch, convolved):
                dve.wait_ge(stat, ch.stat0 + 1)
                dve.wait_ge(conv, convolved)

            convolve(CTX, 0, KD // 2)
            lc, ll = chains["ln_c"], chains["ln_l"]
            convolve(LAT, 0, 2)
            ln_first(lc, KD + 4)
            in_fori((ln_centre_pair, lc))
            recip(lc, 1)
            in_fori((ln_scale_pair, lc), (ln_lo_pair, lc))
            dve.wait_ge(ada_ev, MOD // 4)
            for side in (CTX, LAT):
                for kind in (1, 2, 3):
                    gains(side, 0, (kind,))
            dve.wait_ge(mods, 8)
            mc, ml, fc, fl, al = (chains[k] for k in ("mix_c", "mix_l", "ffn_c", "ffn_l", "att_l"))
            convolve(LAT, 2, 3)
            post_now(mc)
            pre_now(mc)
            dve.wait_ge(pool_conv, POOL_CONV)
            dve.wait_ge(ada_ev, 2 * MOD // 4)
            for side in (CTX, LAT):
                for kind in (0, 1, 2, 3):
                    gains(side, 1, (kind,))
            dve.wait_ge(mods, 16)
            for s in range(DVE_LO):
                dve.wait_ge(w_hi, phases["up0c"].spl0 + s + 1)
                dve.tensor_tensor(wlo[s][:, :], raw[s][:, :], whi[s][:, :].bitcast(F32),
                                  ALU.subtract).then_inc(w_lo, 1)

            def up_phase(name, layer, summed_before, cuts=(), hooks=None, inside=None):
                ph = phases[name]
                side, n, p0 = ph.side, N[ph.side], up_pairs0[name]
                dve.wait_ge(summed, summed_before)
                dve.memset(gate_in[:, 0:1], 0.0).then_inc(pads, 1)
                dve.memset(gate_in[:, n + 1:n + 2], 0.0).then_inc(pads, 1)
                dve.wait_ge(pads, 2 * (ups.index(name) + 1))

                def body(it, last):
                    for p in range(2):
                        gt = gate[:, 0:n]
                        m = it * 2 + p
                        dve.wait_ge(evac, it * 2 + (ph.evac0 + p + 1))
                        dve.scalar_tensor_tensor(gt, gate_in[:, 0:n], vcol("ffn_w_dw", m + layer * 3 * KF),
                                                 gt, ALU.mult, ALU.add).then_inc(tap, 1)
                        dve.wait_ge(tap, it * 2 + ((2 * KD - POOL_CONV) * (TAPS - 1) + p0 + p + 1))
                        dve.scalar_tensor_tensor(gt, gate_in[:, 2:n + 2],
                                                 vcol("ffn_w_dw", m + (layer * 3 + 2) * KF),
                                                 gt, ALU.mult, ALU.add).then_inc(gate_cv, 1)
                        dve.wait_ge(gelu, it * 2 + (p0 + p + 1))
                        dve.wait_ge(blk, it * 4 + (ph.blk0 + 2 * p + 2))
                        dve.tensor_tensor(gt, gt, bank[2 * p + 1][:, 0:n], ALU.mult).then_inc(prod, 1)
                        dve.wait_ge(prod, it * 2 + (2 + p0 + p + 1))
                        hi = Ghi[side][:, ds(it * (2 * n) + p * n, n)]
                        dve.tensor_copy(hi, gt).then_inc(g_hi, 1)
                        dve.wait_ge(g_hi, it * 2 + (p0 + p + 1))
                        dve.tensor_tensor(Glo[side][:, ds(it * (2 * n) + p * n, n)], gt, hi.bitcast(F32),
                                          ALU.subtract).then_inc(g_rdy, 1)

                loop(dve, ph, body, cuts, hooks, inside)

            up_phase("up0c", 0, sum0["conv_l"], FFN_CUTS,
                     {1: lambda: ln_first(ll, 2 * KD - POOL_CONV), 6: lambda: recip(ll, 1)},
                     {1: lambda it: (ln_centre_pair(ll, it - 1), add_squares_pair(ll, it - 1)),
                      6: lambda it: (ln_scale_pair(ll, it - 6), ln_lo_pair(ll, it - 6))})
            recip(ml, 1)
            with dve.Fori(0, KD // 2) as t:
                update_pair(ml, t)
                add_squares_pair(ml, t)
            pre_now(ml)
            up_phase("up0l", 0, sum0["down0l"], FFN_CUTS,
                     {1: lambda: recip(fc, 1), 6: lambda: recip(fc, 2)},
                     {1: lambda it: (update_pair(fc, it - 1), add_squares_pair(fc, it - 1)),
                      6: lambda it: (scale_pair(fc, it - 6), lo_pair(fc, it - 6))})
            post_now(fl)
            pre_now(fl)

            def v_by_token(m, q, b):
                w = 512 if b < 2 else 256
                dve.wait_ge(vt_tr, m * 3 + (b + 1))
                dve.tensor_copy(vtok[q][:, b * 512:b * 512 + w], V_TURNED[:, 0:w]).then_inc(vt_ev, 1)

            def take_max(m, t):
                par, hp, n = t % 2, t % 2, t // 2
                if t < 2:
                    dve.wait_ge(bias_rdy, m * 2 + (hp + 1))
                dve.wait_ge(s_rdy, m * 8 + (t + 1))
                dve.memset(spacer[:, :], 0.0)
                dve.tensor_tensor_reduce(out=scores[par][:, :], in0=SCORES[n % 2][hp][:, :],
                                         in1=bias[hp][:, n * 512:(n + 1) * 512], scale=1.0, scalar=-3e38,
                                         op0=ALU.add, op1=ALU.max,
                                         accum_out=rowmax[par][:, :]).then_inc(s_max, 1)
                dve.wait_ge(s_max, m * 8 + (t + 3))
                dve.tensor_scalar(negmax[par][:, :], rowmax[par][:, :], -1.0, None, ALU.mult).then_inc(s_neg, 1)

            def normalise(m, t):
                par = t % 2
                dve.wait_ge(p_exp, m * 8 + (t + 1))
                dve.reciprocal(rowinv[par][:, :], rowsum[par][:, :]).then_inc(p_inv, 1)
                dve.wait_ge(p_inv, m * 8 + (t + 1))
                dve.tensor_scalar(probs[par][:, :], probs[par][:, :], rowinv[par][:, :], None,
                                  ALU.mult).then_inc(p_nrm, 1)

            def attend(m, q, more=True):
                take_max(m, 0)
                take_max(m, 1)
                for t in range(8):
                    normalise(m, t)
                    if t + 2 < 8:
                        take_max(m, t + 2)
                    if more and t in (5, 7):
                        v_by_token(m + 1, 1 - q, 0 if t == 5 else 1)
                dve.wait_ge(o_hi, m + 1)
                o = [t[:, ds(m * L, L)].rearrange("p (r n c) -> p r n c", n=NB, c=NA_KW) for t in (Olo, Ohi)]
                b4 = bank[4][:, :].rearrange("p (n r c) -> p r n c", n=NB, c=NA_KW)
                dve.tensor_tensor(o[0], b4, o[1].bitcast(F32), ALU.subtract).then_inc(o_lo, 1)
                if more:
                    v_by_token(m + 1, 1 - q, 2)

            for b in range(3):
                v_by_token(0, 0, b)
            with dve.Fori(0, KD // 2 - 1) as it:
                attend(it * 2, 0)
                attend(it * 2 + 1, 1)
            attend(KD - 2, 0)
            attend(KD - 1, 1, more=False)

            post_now(al)
            pre_now(al)
            up_phase("up1", 1, sum0["down1"])
            post_now(chains["out_l"])

        @block.tensor
        def _(pe):
            pe.wait_ge(cst_in, 16)
            n_loads = sum(-(-((at[name] % P) + ap.shape[0]) // P) for name, ap in vectors.items())
            pe.wait_ge(v_in, 16 * n_loads)
            evs = 0

            def own_bank():
                if evs >= 4:
                    pe.wait_ge(evac, evs - 3)
                return FIRST[evs % 4]

            for t in range(VT):
                b = own_bank()
                r = min(P, rows - t * P)
                pe.transpose(b[:, 0:r], vec_rows[0:r, t * P:(t + 1) * P], ident[0:r, 0:r]).then_inc(turned, 1)
                evs += 1

            def turn_inputs():
                nonlocal evs
                for side, s, t0 in ((CTX, c_in, L // P), (LAT, x_in, 0)):
                    pe.wait_ge(s, 16)
                    for k in range(KD):
                        b = own_bank()
                        for t in range(N[side] // P):
                            ins = pe.transpose(b[:, t * P:(t + 1) * P],
                                               tok[:, (t0 + t) * D + k * P:(t0 + t) * D + (k + 1) * P],
                                               ident[:, :])
                        ins.then_inc(turned, 1)
                        evs += 1
                pe.wait_ge(evac, INIT_EVACS)
                stat_squares(chains["in_c"])

            def ada_phase(name, layer, m0, cuts=(), hooks=None):
                ph = phases[name]
                c0 = (layer * MOD + m0) // 4
                if name != "ada0a":
                    pe.wait_ge(evac, ph.evac0)

                def body(it, last):
                    for u in range(2):
                        for b in range(4):
                            j = 4 * u + b
                            s = ph.slot(j)
                            pe.wait_ge(w_in[s], it * 32 + (ph.landed0[s] + 16 * (j // ph.ring + 1)))
                            for i in range(2):
                                k = 2 * b + i
                                for g in range(4):
                                    c = i * CHUNK + g * P
                                    ins = pe.matmul(bank[u][32 * g:32 * g + 2, 0:P], cond[:, k:2 * KD:KD],
                                                    raw[s][:, c:c + P], start=(k == 0), stop=(k == KD - 1))
                            ins.then_inc(blk, 1)
                    for u in range(2):
                        pe.wait_ge(row_out, it * 2 + (c0 + u + 1))
                        pe.transpose(ADA_T[u][:, 0:P], ada_row[u][:, :], ident[:, :]).then_inc(ada_tr, 1)

                loop(pe, ph, body, cuts, hooks)

            def products(b, n, s, kts, hi, lo, k0, first, last, ready=None):
                for k in range(kts):
                    if ready:
                        pe.wait_ge(ready[0], ready[1] + k0 + k + 1)
                    w = slice(k * P, (k + 1) * P)
                    a = slice((k0 + k) * n, (k0 + k + 1) * n)
                    pe.matmul(b, whi[s][:, w], hi[:, a], start=(first and k == 0), stop=False)
                    pe.matmul(b, whi[s][:, w], lo[:, a], start=False, stop=False)
                    ins = pe.matmul(b, wlo[s][:, w], hi[:, a], start=False, stop=(last and k == kts - 1))
                return ins

            def products_as_made(slots, h0):
                hi, lo = Hhi[LAT], Hlo[LAT]
                for i, s in enumerate(slots):
                    for k in range(KD):
                        if i == 0:
                            pe.wait_ge(h_hi, h0 + k + 1)
                        a = slice(k * L, (k + 1) * L)
                        for part in (whi[s], wlo[s]):
                            pe.matmul(bank[i][:, 0:L], part[:, k * P:(k + 1) * P], hi[:, a],
                                      start=(part is whi[s] and k == 0), stop=False)
                for i, s in enumerate(slots):
                    for k in range(KD):
                        if i == 0:
                            pe.wait_ge(h_lo, h0 + k + 1)
                        ins = pe.matmul(bank[i][:, 0:L], whi[s][:, k * P:(k + 1) * P],
                                        lo[:, k * L:(k + 1) * L], start=False, stop=(k == KD - 1))
                    ins.then_inc(blk, 1)

            def split_wait(ph, it, j):
                pe.wait_ge(w_lo, it * ph.per + (ph.spl0 + j + 1))

            def o_begun(b, k0, k1):
                for k in range(k0, k1):
                    w = slice(k * P, (k + 1) * P)
                    a = slice(k * L, (k + 1) * L)
                    pe.matmul(b, whi[0][:, w], Ohi[:, a], start=(k == 0), stop=False)
                    pe.matmul(b, whi[0][:, w], Olo[:, a], start=False, stop=False)
                    ins = pe.matmul(b, wlo[0][:, w], Ohi[:, a], start=False, stop=(k == KD - 1))
                return ins

            def linear(name, ready, cuts=(), hooks=None):
                ph = phases[name]
                n = N[ph.side]
                hi, lo = (Ohi, Olo) if name == "o" else (Hhi[ph.side], Hlo[ph.side])

                def body(it, last):
                    for j in range(4):
                        if name == "up1" and isinstance(it, int) and it == 0 and j < 2:
                            if j == 0:
                                split_wait(ph, 0, 1)
                                pe.wait_ge(evac, ph.evac0)
                                products_as_made((ph.slot(0), ph.slot(1)), ready[1])
                            continue
                        split_wait(ph, it, j)
                        if ph.kind == "up" and j % 2 == 0:
                            pe.wait_ge(evac, it * 2 + (ph.evac0 + j // 2 - 1))
                        elif ph.kind == "up":
                            pe.wait_ge(prod, it * 2 + (2 + up_pairs0[name] + j // 2 - 1))
                        else:
                            pe.wait_ge(evac, it * 4 + (ph.evac0 + j - 3))
                            if name == "pw2l" and j % 2 == 1:
                                pe.wait_ge(prod, 2 + KF - 1 + j // 2)
                        at_first = isinstance(it, int) and (it, j) == (0, 0)
                        b = bank[(j + bank0(name)) % 4][:, 0:n]
                        if at_first and name == "o":
                            pe.wait_ge(ready[0], ready[1] + KD)
                            o_begun(b, KD - 1, KD).then_inc(blk, 1)
                            continue
                        products(b, n, ph.slot(j), KD, hi, lo, 0, True, True,
                                 ready if at_first else None).then_inc(blk, 1)

                loop(pe, ph, body, (1, *cuts), hooks)

            def down(name, pairs0, steps=None):
                ph = phases[name]
                n = N[ph.side]
                pe.wait_ge(evac, ph.evac0)

                def body(it, last):
                    for j in range(ph.per):
                        t, part = j // 3, j % 3
                        split_wait(ph, it, j)
                        if part == 0:
                            pe.wait_ge(evac, it * 4 + (ph.evac0 + t - 3))
                        products(bank[t][:, 0:n], n, ph.slot(j), DOWN_K[part], Ghi[ph.side], Glo[ph.side],
                                 DOWN_R[part], part == 0, part == 2,
                                 (g_rdy, 1 + pairs0) if (it, t) == (0, 0) else None).then_inc(blk, 1)
                        for step in (steps or {}).get((it, j), ()):
                            step()

                loop(pe, ph, body)

            def by_quarter(src, col0, first, last):
                for g in range(4):
                    ins = pe.matmul(STAT[32 * g:32 * (g + 1), 0:P], ones[:, 0:32],
                                    src[:, col0 + g * P:col0 + (g + 1) * P], start=first, stop=last)
                return ins

            def spread_inverse(ch, stage):
                pe.wait_ge(rcp, ch.rms0 + stage)
                for g in range(4):
                    pick = ident[:, 32 * g:32 * g + 1]
                    pick = bass.AP(tensor=pick.tensor, offset=pick.offset, ap=[list(pick.ap[0]), [0, P]])
                    ins = pe.matmul(RINV[:, g * P:(g + 1) * P], pick, inv_t[:, :], start=True, stop=True)
                ins.then_inc(spread, 1)

            def stat_sum(ch, name):
                pe.wait_ge(summed, sum0[name] + KD + 1)
                if ch.compact:
                    by_quarter(acc[ch.side], 0, True, True).then_inc(stat, 1)
                    spread_inverse(ch, 1)
                    return
                pe.matmul(STAT[:, 0:ch.n], ones[:, :], acc[ch.side][:, :], start=True, stop=True).then_inc(stat, 1)

            def stat_squares(ch):
                step = 1 if ch.pair0 is None else 2
                for k in range(0, KD, step):
                    if step == 1:
                        pe.wait_ge(x_sq, ch.sq0 + k + 1)
                    else:
                        pe.wait_ge(sq_pair, ch.pair0 + k // 2 + 1)
                    if ch.compact:
                        ins = by_quarter(SQ[ch.side], k * ch.n, k == 0, k == KD - 1)
                        continue
                    ins = pe.matmul(STAT[:, 0:ch.n], ones[:, :], SQ[ch.side][:, k * ch.n:(k + 1) * ch.n],
                                    start=(k == 0), stop=(k == KD - step))
                ins.then_inc(stat, 1)
                if ch.compact:
                    spread_inverse(ch, 2)

            def normed(name):
                return h_lo, chains[name].h0

            mc, ll, ml, fc, fl, al = (chains[k] for k in ("mix_c", "ln_l", "mix_l", "ffn_c", "ffn_l", "att_l"))
            pe.wait_ge(ones_s, 1)
            pe.wait_ge(cond_s, 1)
            ada_phase("ada0a", 0, 0, hooks={1: turn_inputs})
            pe.wait_ge(rms, 1)
            stat_squares(chains["in_l"])
            linear("pw1c", normed("in_c"))
            linear("pw1l", normed("in_l"))
            lc = chains["ln_c"]

            def ln_c_stats():
                stat_sum(lc, "conv_c")
                pe.wait_ge(centred, KD)
                stat_squares(lc)

            ada_phase("ada0b", 0, 2 * KD)
            ada_phase("ada1a", 1, 0, hooks={2: ln_c_stats})
            linear("pw2c", normed("ln_c"))
            stat_sum(mc, "pw2c")
            ada_phase("ada1b", 1, 3 * KD, hooks={2: lambda: stat_squares(mc)})

            def ln_l_squares():
                pe.wait_ge(centred, 2 * KD)
                stat_squares(ll)

            linear("up0c", normed("mix_c"), FFN_CUTS, {1: lambda: stat_sum(ll, "conv_l"), 6: ln_l_squares})
            linear("pw2l", normed("ln_l"))
            down("down0c", 0, {(0, 1): [lambda: stat_sum(ml, "pw2l")], (0, 10): [lambda: stat_squares(ml)]})
            linear("up0l", normed("mix_l"), FFN_CUTS,
                   {1: lambda: stat_sum(fc, "down0c"), 6: lambda: stat_squares(fc)})
            down("down0l", KF)
            stat_sum(fl, "down0l")
            ph = phases["qkv"]
            pe.wait_ge(evac, ph.evac0)
            def context_first(j):
                split_wait(ph, 0, j)
                products(bank[2][:, (j - 1) * C:j * C], C, ph.slot(j), KD, Hhi[CTX], Hlo[CTX], 0, True, True)

            context_first(1)
            stat_squares(fl)
            context_first(2)


            def qkv_products(it, mj, first=False):
                def ev(k):
                    if not first:
                        pe.wait_ge(kv_ev, it * 10 + (5 * mj - 5 + k))
                b0, n1, n2 = bank, L, C
                s = [ph.slot(3 * mj + j) for j in range(3)]
                if first:
                    split_wait(ph, it, 1)
                    products_as_made(s[0:2], chains["ffn_l"].h0)
                else:
                    split_wait(ph, it, 3 * mj)
                    ev(1)
                    products(b0[0][:, 0:n1], n1, s[0], KD, Hhi[LAT], Hlo[LAT], 0, True, True).then_inc(blk, 1)
                    split_wait(ph, it, 3 * mj + 1)
                    ev(5)
                    products(b0[1][:, 0:n1], n1, s[1], KD, Hhi[LAT], Hlo[LAT], 0, True, True)
                    products(b0[2][:, 0:n2], n2, s[1], KD, Hhi[CTX], Hlo[CTX], 0, True, True).then_inc(blk, 1)
                split_wait(ph, it, 3 * mj + 2)
                if not first:
                    pe.wait_ge(vt_ev, it * 6 + 3 * mj)
                ins = products(b0[3][:, 0:n1], n1, s[2], KD, Hhi[LAT], Hlo[LAT], 0, True, True)
                if not first:
                    pe.wait_ge(kv_ev, it * 10 + (5 * mj + 2))
                    ins = products(b0[2][:, n2:2 * n2], n2, s[2], KD, Hhi[CTX], Hlo[CTX], 0, True, True)
                ins.then_inc(blk, 1)

            def turn_v(m, q, b):
                if b == 0:
                    pe.wait_ge(kv_ev, m * 5 + 5)
                else:
                    pe.wait_ge(vt_ev, m * 3 + b)
                for i in range(4 if b < 2 else 2):
                    ins = pe.transpose(V_TURNED[:, i * P:(i + 1) * P],
                                       vT[q][:, (4 * b + i) * P:(4 * b + i + 1) * P], ident[:, :])
                ins.then_inc(vt_tr, 1)

            def score(m, q, n, products_ahead=True):
                if n < 2:
                    pe.wait_ge(s_max, m * 8 + 2)
                if n == 1 and products_ahead:
                    pe.wait_ge(kv_ev, m * 5 + 8)
                for part in range(2):
                    for h in range(2):
                        rows_ = slice(h * HEAD_D, (h + 1) * HEAD_D)
                        keys = kT[q][rows_, L:L + C] if part else window(kT[q][rows_, 0:L], n, 0, NA_KH)
                        if n >= 2 and part == 0:
                            pe.wait_ge(s_max, m * 8 + (2 * n + h - 1))
                        ins = pe.matmul(SCORES[n % 2][h][:, part * C:(part + 1) * C],
                                        qT[q][rows_, n * P:(n + 1) * P], keys, start=True, stop=True)
                        if part:
                            ins.then_inc(s_rdy, 1)

            def turn_p(m, t, products_ahead):
                if t >= 2:
                    pe.wait_ge(pt_ev, m * 8 + t)
                elif t == 1 and products_ahead:
                    pe.wait_ge(kv_ev, m * 5 + 10)
                pe.wait_ge(p_nrm, m * 8 + (t + 1))
                for i in range(4):
                    ins = pe.transpose(TURNED[t % 2][:, i * P:(i + 1) * P], probs[t % 2][:, i * P:(i + 1) * P],
                                       ident[:, :])
                ins.then_inc(pt_tr, 1)

            def weighted(m, q, n):
                if n == 0:
                    pe.wait_ge(o_lo, m + 1)
                pe.wait_ge(pt_ev, m * 8 + (2 * n + 3))
                for i in range(4):
                    c = 2 * n + i if i < 2 else 2 * NB + i - 2
                    for h in range(2):
                        ins = pe.matmul(bank[4][h * HEAD_D:(h + 1) * HEAD_D, n * P:(n + 1) * P],
                                        vtok[q][:, c * P + h * HEAD_D:c * P + (h + 1) * HEAD_D],
                                        probsT[h][:, i * P:(i + 1) * P], start=(i == 0), stop=(i == 3))
                        if i == 3:
                            ins.then_inc(pv, 1)

            def attend(m, q, ahead=None):
                score(m, q, 0)
                if ahead:
                    ahead()
                score(m, q, 1, bool(ahead))
                pe.wait_ge(vt_ev, m * 3 + 3)
                for n in range(NB):
                    turn_p(m, 2 * n, bool(ahead))
                    turn_p(m, 2 * n + 1, bool(ahead))
                    if n + 2 < NB:
                        score(m, q, n + 2)
                    elif ahead:
                        turn_v(m + 1, 1 - q, n + 2 - NB)
                    if not ahead:
                        if n == 0:
                            split_wait(phases["o"], 0, 0)
                            pe.wait_ge(o_lo, m + 1)
                        o_begun(bank[3][:, :], 2 * n, min(2 * n + 2, KD - 1))
                    weighted(m, q, n)
                if ahead:
                    turn_v(m + 1, 1 - q, 2)

            qkv_products(0, 0, first=True)
            pe.transpose(bank[7][:, 0:P], ident[:, :], ident[:, :]).then_inc(pt_tr, 1)
            pe.matmul(bank[4][0:HEAD_D, 0:2], ident[:, 0:HEAD_D], ident[:, 0:2], start=True, stop=True).then_inc(pv, 1)
            for b in range(3):
                turn_v(0, 0, b)
            with pe.Fori(0, ph.iters - 1) as it:
                attend(it * 2, 0, lambda: qkv_products(it, 1))
                attend(it * 2 + 1, 1, lambda: qkv_products(it + 1, 0))
            last = ph.iters - 1
            attend(2 * last, 0, lambda: qkv_products(last, 1))
            attend(2 * last + 1, 1)

            linear("o", (o_lo, 1))
            stat_sum(al, "o")
            stat_squares(al)
            linear("up1", normed("att_l"), (1,))
            down("down1", 2 * KF)
            fin = chains["out_l"]
            stat_sum(fin, "down1")
            for i in range(8):
                h, j = i // 4, i % 4
                pe.wait_ge(x_up, fin.up0 + 4 * (h + 1))
                pe.wait_ge(evac, phases["down1"].evac0 + KD)
                if i >= 4:
                    pe.wait_ge(out_ev, i - 3)
                for k in range(4):
                    kk = 4 * h + k
                    ins = pe.transpose(bank[i % 4][:, k * P:(k + 1) * P],
                                       X[LAT][:, kk * L + j * P:kk * L + (j + 1) * P], ident[:, :])
                ins.then_inc(out_tr, 1)


VECTORS = ["mod_b", "mix_pre_g", "mix_post_g", "ffn_pre_g", "ffn_post_g", "cv_b_pw1", "cv_b_dw", "cv_ln_g",
           "cv_ln_b", "cv_b_pw2", "cv_w_dw", "ffn_b_dw", "ffn_w_dw", "c", "c_ctx"]
MATRICES = ["mod_w", "cv_w_pw1", "cv_w_pw2", "na_w_qkv", "na_w_o", "ffn_w_up", "ffn_w_down", "na_rpb"]


def kernel(**inputs):
    import numpy as np
    import concourse.bacc as bacc
    from concourse.bass_utils import run_bass_kernel_spmd

    nc = bacc.Bacc("TRN2", target_bir_lowering=False, num_devices=1, dynamic_dma_scratch_size=1024)
    arrays = {}

    def give(name, a):
        arrays[f"in_{name}"] = a
        return nc.dram_tensor(f"in_{name}", a.shape, F32, kind="ExternalInput").ap()

    x = give("x", np.ascontiguousarray(inputs["x"])[0])
    ctx = give("ctx", np.ascontiguousarray(inputs["ctx"])[0])
    mats = {n: give(n, np.ascontiguousarray(inputs[n])) for n in MATRICES}
    vecs = {n: give(n, np.ascontiguousarray(inputs[n]).reshape(-1, P)) for n in VECTORS}

    ident = np.eye(P, dtype=np.float32)
    starts = col_starts()
    mask = np.zeros((P, len(starts), KB_W), np.float32)
    for p in range(P):
        for n, k0 in enumerate(starts):
            q = n * NA_KW + p % NA_KW
            c0 = min(max(q - NA_KW // 2, 0), GRID_W - NA_KW)
            for j in range(KB_W):
                if not c0 <= k0 + j < c0 + NA_KW:
                    mask[p, n, j] = NEG_INF
    ident_in = give("ident", ident)
    mask_in = give("mask", mask.reshape(P, -1))
    out = nc.dram_tensor("out", tuple(x.shape), F32, kind="ExternalOutput").ap()
    build(nc, x, ctx, **mats, vectors=vecs, ident_in=ident_in, mask_in=mask_in, out=out)
    r = run_bass_kernel_spmd(nc, [arrays], core_ids=[0])
    return r.results[0]["out"][None]
```
